# Optimizing a Trainium2 kernel written in Bass

```python
import jax, jax.numpy as jnp
from jax import lax
import numpy as np
import math

D_MODEL = 1024
BATCH = 1
SEQ = 256
DEPTH = 2

N_MIXERS = 2
N_CONV_LAYERS = (DEPTH + 1) // 2
N_MLA_LAYERS = DEPTH // 2
N_DENSE_LAYERS = (DEPTH + 1) // 2
N_MOE_LAYERS = DEPTH // 2
CONV_WIDTH = 3
N_HEADS = 8
QK_NOPE_DIM = 128
QK_ROPE_DIM = 64
QK_HEAD_DIM = QK_NOPE_DIM + QK_ROPE_DIM
V_HEAD_DIM = 128
Q_LORA_RANK = 384
KV_LORA_RANK = 256
ROPE_THETA = 10000.0
Q_BLOCK = 128
D_FF_DENSE = 2816
N_EXPERTS = 8
TOP_K = 2
D_FF_EXPERT = 2048
EPS = 1e-6


def rmsnorm(x, g):
    xf = x.astype(jnp.float32)
    y = xf * lax.rsqrt(jnp.mean(xf * xf, axis=-1, keepdims=True) + EPS)
    return (y * g.astype(jnp.float32)).astype(x.dtype)

def rope_tables(positions):
    inv_freq = ROPE_THETA ** (-jnp.arange(0, QK_ROPE_DIM, 2, dtype=jnp.float32) / QK_ROPE_DIM)
    ang = positions.astype(jnp.float32)[..., None] * inv_freq
    return jnp.cos(ang)[:, :, None, :], jnp.sin(ang)[:, :, None, :]

def apply_rope(x, cos, sin):
    x1, x2 = jnp.split(x, 2, axis=-1)
    cos = cos.astype(x.dtype)
    sin = sin.astype(x.dtype)
    return jnp.concatenate([x1 * cos - x2 * sin, x2 * cos + x1 * sin], axis=-1)

def short_conv_mixer(h, w_in, w_conv, w_out):
    seq = h.shape[1]
    b_gate, c_gate, u = jnp.split(h @ w_in, 3, axis=-1)
    v = c_gate * u
    vp = jnp.pad(v, ((0, 0), (CONV_WIDTH - 1, 0), (0, 0)))
    conv = vp[:, 0:seq] * w_conv[0]
    for k in range(1, CONV_WIDTH):
        conv = conv + vp[:, k:k + seq] * w_conv[k]
    return (b_gate * conv) @ w_out

def mla_mixer(h, cos, sin, w_down, q_a_norm, kv_a_norm, w_uq, w_ukv, q_norm, k_norm, w_o):
    bsz, seq, _ = h.shape
    down = h @ w_down
    c_q = rmsnorm(down[..., :Q_LORA_RANK], q_a_norm)
    c_kv = rmsnorm(down[..., Q_LORA_RANK:Q_LORA_RANK + KV_LORA_RANK], kv_a_norm)
    k_rope = down[..., Q_LORA_RANK + KV_LORA_RANK:]
    q = (c_q @ w_uq).reshape(bsz, seq, N_HEADS, QK_HEAD_DIM)
    kv = (c_kv @ w_ukv).reshape(bsz, seq, N_HEADS, QK_NOPE_DIM + V_HEAD_DIM)
    k_nope, v = kv[..., :QK_NOPE_DIM], kv[..., QK_NOPE_DIM:]
    k_rope_h = jnp.broadcast_to(k_rope[:, :, None, :], (bsz, seq, N_HEADS, QK_ROPE_DIM))
    k = jnp.concatenate([k_nope, k_rope_h], axis=-1)
    q = rmsnorm(q, q_norm)
    k = rmsnorm(k, k_norm)
    q = jnp.concatenate([q[..., :QK_NOPE_DIM], apply_rope(q[..., QK_NOPE_DIM:], cos, sin)], axis=-1)
    k = jnp.concatenate([k[..., :QK_NOPE_DIM], apply_rope(k[..., QK_NOPE_DIM:], cos, sin)], axis=-1)
    scale = QK_HEAD_DIM ** -0.5
    neg = jnp.finfo(jnp.float32).min
    outs = []
    for blk in range(seq // Q_BLOCK):
        s0 = blk * Q_BLOCK
        end = s0 + Q_BLOCK
        scores = jnp.einsum('bqhd,bkhd->bhqk', q[:, s0:end], k[:, :end]).astype(jnp.float32) * scale
        mask = jnp.arange(end)[None, :] <= (s0 + jnp.arange(Q_BLOCK))[:, None]
        p = jax.nn.softmax(jnp.where(mask, scores, neg), axis=-1).astype(v.dtype)
        outs.append(jnp.einsum('bhqk,bkhd->bqhd', p, v[:, :end]))
    o = jnp.concatenate(outs, axis=1).reshape(bsz, seq, N_HEADS * V_HEAD_DIM)
    return o @ w_o

def swiglu(h, w_gate, w_up, w_down):
    return (jax.nn.silu(h @ w_gate) * (h @ w_up)) @ w_down

def moe_swiglu(h, router, w_gate, w_up, w_down):
    bsz, seq, d = h.shape
    ht = h.reshape(bsz * seq, d)
    probs = jax.nn.softmax((ht @ router).astype(jnp.float32), axis=-1)
    vals, idx = lax.top_k(probs, TOP_K)
    wts = vals / jnp.sum(vals, axis=-1, keepdims=True)
    gates = jnp.einsum('tk,tke->te', wts, jax.nn.one_hot(idx, N_EXPERTS, dtype=jnp.float32)).astype(h.dtype)
    out = jnp.zeros_like(ht)
    for e in range(N_EXPERTS):
        out = out + gates[:, e:e + 1] * swiglu(ht, w_gate[e], w_up[e], w_down[e])
    return out.reshape(bsz, seq, d)

def first_inputs(seed: int = 0) -> dict:
    key = jax.random.key(seed)
    ks = jax.random.split(key, 24)
    f32 = jnp.float32
    res_scale = (2 * DEPTH) ** -0.5

    def w(k, shape, fan_in, extra=1.0):
        return jax.random.normal(k, shape, f32) * (fan_in ** -0.5) * extra

    def gain(k, shape):
        return 1.0 + 0.02 * jax.random.normal(k, shape, f32)

    x = jax.random.normal(ks[0], (BATCH, SEQ, D_MODEL), f32)
    start = jax.random.randint(ks[1], (BATCH, 1), 0, 4096, dtype=jnp.int32)
    positions = (start + jnp.arange(SEQ, dtype=jnp.int32)[None, :]).astype(jnp.int32)
    return {
        "x": x,
        "positions": positions,
        "norm_mix": gain(ks[2], (DEPTH, D_MODEL)),
        "norm_ffn": gain(ks[3], (DEPTH, D_MODEL)),
        "conv_w_in": w(ks[4], (N_CONV_LAYERS, D_MODEL, 3 * D_MODEL), D_MODEL),
        "conv_w": w(ks[5], (N_CONV_LAYERS, CONV_WIDTH, D_MODEL), CONV_WIDTH),
        "conv_w_out": w(ks[6], (N_CONV_LAYERS, D_MODEL, D_MODEL), D_MODEL, res_scale),
        "mla_w_down": w(ks[7], (N_MLA_LAYERS, D_MODEL, Q_LORA_RANK + KV_LORA_RANK + QK_ROPE_DIM), D_MODEL),
        "mla_q_a_norm": gain(ks[8], (N_MLA_LAYERS, Q_LORA_RANK)),
        "mla_kv_a_norm": gain(ks[9], (N_MLA_LAYERS, KV_LORA_RANK)),
        "mla_w_uq": w(ks[10], (N_MLA_LAYERS, Q_LORA_RANK, N_HEADS * QK_HEAD_DIM), Q_LORA_RANK),
        "mla_w_ukv": w(ks[11], (N_MLA_LAYERS, KV_LORA_RANK, N_HEADS * (QK_NOPE_DIM + V_HEAD_DIM)), KV_LORA_RANK),
        "mla_q_norm": gain(ks[12], (N_MLA_LAYERS, QK_HEAD_DIM)),
        "mla_k_norm": gain(ks[13], (N_MLA_LAYERS, QK_HEAD_DIM)),
        "mla_w_o": w(ks[14], (N_MLA_LAYERS, N_HEADS * V_HEAD_DIM, D_MODEL), N_HEADS * V_HEAD_DIM, res_scale),
        "ffn_w_gate": w(ks[15], (N_DENSE_LAYERS, D_MODEL, D_FF_DENSE), D_MODEL),
        "ffn_w_up": w(ks[16], (N_DENSE_LAYERS, D_MODEL, D_FF_DENSE), D_MODEL),
        "ffn_w_down": w(ks[17], (N_DENSE_LAYERS, D_FF_DENSE, D_MODEL), D_FF_DENSE, res_scale),
        "moe_router": w(ks[18], (N_MOE_LAYERS, D_MODEL, N_EXPERTS), D_MODEL),
        "moe_w_gate": w(ks[19], (N_MOE_LAYERS, N_EXPERTS, D_MODEL, D_FF_EXPERT), D_MODEL),
        "moe_w_up": w(ks[20], (N_MOE_LAYERS, N_EXPERTS, D_MODEL, D_FF_EXPERT), D_MODEL),
        "moe_w_down": w(ks[21], (N_MOE_LAYERS, N_EXPERTS, D_FF_EXPERT, D_MODEL), D_FF_EXPERT, res_scale),
    }

def first_block(x, positions, norm_mix, norm_ffn, conv_w_in, conv_w, conv_w_out,
              mla_w_down, mla_q_a_norm, mla_kv_a_norm, mla_w_uq, mla_w_ukv,
              mla_q_norm, mla_k_norm, mla_w_o, ffn_w_gate, ffn_w_up, ffn_w_down,
              moe_router, moe_w_gate, moe_w_up, moe_w_down):
    cos, sin = rope_tables(positions)
    for i in range(DEPTH):
        j = i // 2
        h = rmsnorm(x, norm_mix[i])
        if i % N_MIXERS == 0:
            x = x + short_conv_mixer(h, conv_w_in[j], conv_w[j], conv_w_out[j])
        else:
            x = x + mla_mixer(h, cos, sin, mla_w_down[j], mla_q_a_norm[j], mla_kv_a_norm[j],
                              mla_w_uq[j], mla_w_ukv[j], mla_q_norm[j], mla_k_norm[j], mla_w_o[j])
        h = rmsnorm(x, norm_ffn[i])
        if i % 2 == 0:
            x = x + swiglu(h, ffn_w_gate[j], ffn_w_up[j], ffn_w_down[j])
        else:
            x = x + moe_swiglu(h, moe_router[j], moe_w_gate[j], moe_w_up[j], moe_w_down[j])
    return x


N_A_LAYERS = (DEPTH + N_MIXERS - 1) // N_MIXERS
N_B_LAYERS = DEPTH // N_MIXERS

ATTN_HEAD_DIM = 128
ATTN_HEADS = D_MODEL // ATTN_HEAD_DIM
MOBA_BLOCK = 256
MOBA_TOPK = 3
Q_CHUNK = 128

SSM_EXPAND = 2
SSM_D_INNER = SSM_EXPAND * D_MODEL
SSM_HEAD_DIM = 64
SSM_HEADS = SSM_D_INNER // SSM_HEAD_DIM
SSM_GROUPS = 8
SSM_HEADS_PER_GROUP = SSM_HEADS // SSM_GROUPS
SSM_STATE = 128
SSM_CONV = 4
SSM_CHUNK = 128
SSM_CONV_DIM = SSM_D_INNER + 2 * SSM_GROUPS * SSM_STATE
SSM_IN_DIM = SSM_D_INNER + SSM_CONV_DIM + SSM_HEADS

D_FF = 2816


def rms_norm(x, g):
    xf = x.astype(jnp.float32)
    y = xf * lax.rsqrt(jnp.mean(xf * xf, axis=-1, keepdims=True) + EPS)
    return (y * g.astype(jnp.float32)).astype(x.dtype)

def swiglu_2(x, w_gate, w_up, w_down):
    return (jax.nn.silu(x @ w_gate) * (x @ w_up)) @ w_down

def rope(x, positions):
    half = x.shape[-1] // 2
    inv_freq = ROPE_THETA ** (-jnp.arange(half, dtype=jnp.float32) / half)
    ang = positions.astype(jnp.float32)[..., None] * inv_freq
    cos = jnp.cos(ang)[:, :, None, :]
    sin = jnp.sin(ang)[:, :, None, :]
    xf = x.astype(jnp.float32)
    x1, x2 = xf[..., :half], xf[..., half:]
    out = jnp.concatenate([x1 * cos - x2 * sin, x2 * cos + x1 * sin], axis=-1)
    return out.astype(x.dtype)

def moba_mixer(h, positions, w_qkv, q_gain, k_gain, w_o):
    bsz, seq, _ = h.shape
    H, Dh, BS = ATTN_HEADS, ATTN_HEAD_DIM, MOBA_BLOCK
    qkv = (h @ w_qkv).reshape(bsz, seq, 3, H, Dh)
    q = rope(rms_norm(qkv[:, :, 0], q_gain), positions)
    k = rope(rms_norm(qkv[:, :, 1], k_gain), positions)
    v = qkv[:, :, 2]
    q = jnp.swapaxes(q, 1, 2)
    k = jnp.swapaxes(k, 1, 2)
    v = jnp.swapaxes(v, 1, 2)
    n_blk = -(-seq // BS)
    pad = n_blk * BS - seq
    k = jnp.pad(k, ((0, 0), (0, 0), (0, pad), (0, 0)))
    v = jnp.pad(v, ((0, 0), (0, 0), (0, pad), (0, 0)))
    kb = k.reshape(bsz, H, n_blk, BS, Dh)
    vb = v.reshape(bsz, H, n_blk, BS, Dh)
    n_sel = min(MOBA_TOPK, n_blk - 1)
    q_blk = jnp.arange(seq) // BS
    scale = Dh ** -0.5

    if n_sel > 0:
        k_mean = jnp.mean(kb.astype(jnp.float32), axis=3)
        gate = jnp.einsum('bhtd,bhnd->bhtn', q.astype(jnp.float32), k_mean)
        past = jnp.arange(n_blk)[None, :] < q_blk[:, None]
        gate = jnp.where(past, gate, -jnp.inf)
        _, sel_idx = lax.top_k(gate, n_sel)
        sel_valid = sel_idx < q_blk[:, None]

    n_qc = seq // Q_CHUNK
    head_ix = jnp.arange(H)[:, None, None]

    def one_chunk(s):
        b = s // n_qc
        t0 = (s % n_qc) * Q_CHUNK
        qc = lax.dynamic_slice_in_dim(lax.dynamic_index_in_dim(q, b, 0, False), t0, Q_CHUNK, 1)
        kb_b = lax.dynamic_index_in_dim(kb, b, 0, False)
        vb_b = lax.dynamic_index_in_dim(vb, b, 0, False)
        own = t0 // BS
        k_own = lax.dynamic_index_in_dim(kb_b, own, 1, False)
        v_own = lax.dynamic_index_in_dim(vb_b, own, 1, False)
        q_pos = t0 + jnp.arange(Q_CHUNK)
        k_pos = own * BS + jnp.arange(BS)
        s_own = jnp.einsum('hqd,hkd->hqk', qc, k_own).astype(jnp.float32) * scale
        s_own = jnp.where(k_pos[None, :] <= q_pos[:, None], s_own, -jnp.inf)
        if n_sel == 0:
            p = jax.nn.softmax(s_own, axis=-1).astype(v_own.dtype)
            return jnp.einsum('hqk,hkd->hqd', p, v_own)
        idx = lax.dynamic_slice_in_dim(lax.dynamic_index_in_dim(sel_idx, b, 0, False), t0, Q_CHUNK, 1)
        valid = lax.dynamic_slice_in_dim(lax.dynamic_index_in_dim(sel_valid, b, 0, False), t0, Q_CHUNK, 1)
        k_sel = kb_b[head_ix, idx]
        v_sel = vb_b[head_ix, idx]
        s_sel = jnp.einsum('hqd,hqjkd->hqjk', qc, k_sel).astype(jnp.float32) * scale
        s_sel = jnp.where(valid[..., None], s_sel, -jnp.inf).reshape(H, Q_CHUNK, n_sel * BS)
        p = jax.nn.softmax(jnp.concatenate([s_sel, s_own], axis=-1), axis=-1).astype(v_own.dtype)
        p_sel = p[..., :n_sel * BS].reshape(H, Q_CHUNK, n_sel, BS)
        p_own = p[..., n_sel * BS:]
        return (jnp.einsum('hqjk,hqjkd->hqd', p_sel, v_sel)
                + jnp.einsum('hqk,hkd->hqd', p_own, v_own))

    o = lax.map(one_chunk, jnp.arange(bsz * n_qc))
    o = o.reshape(bsz, n_qc, H, Q_CHUNK, Dh).transpose(0, 1, 3, 2, 4).reshape(bsz, seq, H * Dh)
    return o @ w_o

def ssd_chunked(xdt, a_dt, bm, cm):
    bsz, seq = xdt.shape[:2]
    G, R, P, N, CH = SSM_GROUPS, SSM_HEADS_PER_GROUP, SSM_HEAD_DIM, SSM_STATE, SSM_CHUNK
    nc = seq // CH
    x = xdt.reshape(bsz, nc, CH, G, R, P)
    a = a_dt.reshape(bsz, nc, CH, G, R).transpose(0, 3, 4, 1, 2)
    bc = bm.reshape(bsz, nc, CH, G, N)
    cc = cm.reshape(bsz, nc, CH, G, N)
    a_cs = jnp.cumsum(a, axis=-1)
    tril = jnp.tril(jnp.ones((CH, CH), dtype=bool))
    seg = a_cs[..., :, None] - a_cs[..., None, :]
    L = jnp.exp(jnp.where(tril, seg, -jnp.inf))
    cb = jnp.einsum('bclgn,bcsgn->bgcls', cc, bc)
    y_diag = jnp.einsum('bgrcls,bcsgrp->bclgrp', cb[:, :, None] * L, x)
    decay = jnp.exp(a_cs[..., -1:] - a_cs)
    states = jnp.einsum('bclgn,bgrcl,bclgrp->bcgrpn', bc, decay, x)
    chunk_decay = jnp.exp(a_cs[..., -1])

    def step(hs, inp):
        st, dec = inp
        return hs * dec[..., None, None] + st, hs

    h0 = jnp.zeros((bsz, G, R, P, N), dtype=jnp.float32)
    _, prev = lax.scan(step, h0, (jnp.moveaxis(states, 1, 0), jnp.moveaxis(chunk_decay, -1, 0)))
    prev = jnp.moveaxis(prev, 0, 1)
    y_off = jnp.einsum('bclgn,bcgrpn,bgrcl->bclgrp', cc, prev, jnp.exp(a_cs))
    return (y_diag + y_off).reshape(bsz, seq, G * R, P)

def mamba2_mixer(h, w_in, conv_w, conv_b, dt_bias, a_log, d_skip, norm_g, w_out):
    bsz, seq, _ = h.shape
    DI, G, N, H, P = SSM_D_INNER, SSM_GROUPS, SSM_STATE, SSM_HEADS, SSM_HEAD_DIM
    proj = h @ w_in
    z = proj[..., :DI]
    xbc = proj[..., DI:DI + SSM_CONV_DIM]
    dt = proj[..., DI + SSM_CONV_DIM:]
    xbc = lax.conv_general_dilated(xbc, conv_w[:, None, :], window_strides=(1,),
                                   padding=[(SSM_CONV - 1, 0)],
                                   dimension_numbers=('NWC', 'WIO', 'NWC'),
                                   feature_group_count=SSM_CONV_DIM)
    xbc = jax.nn.silu(xbc + conv_b)
    xs = xbc[..., :DI].reshape(bsz, seq, H, P).astype(jnp.float32)
    bm = xbc[..., DI:DI + G * N].reshape(bsz, seq, G, N).astype(jnp.float32)
    cm = xbc[..., DI + G * N:].reshape(bsz, seq, G, N).astype(jnp.float32)
    dt = jax.nn.softplus(dt.astype(jnp.float32) + dt_bias.astype(jnp.float32))
    a = -jnp.exp(a_log.astype(jnp.float32))
    y = ssd_chunked(xs * dt[..., None], dt * a, bm, cm)
    y = y + d_skip.astype(jnp.float32)[:, None] * xs
    y = y.reshape(bsz, seq, DI) * jax.nn.silu(z.astype(jnp.float32))
    yg = y.reshape(bsz, seq, G, DI // G)
    yg = yg * lax.rsqrt(jnp.mean(yg * yg, axis=-1, keepdims=True) + EPS)
    y = yg.reshape(bsz, seq, DI) * norm_g.astype(jnp.float32)
    return y.astype(h.dtype) @ w_out

def second_inputs(seed: int = 0) -> dict:
    key = jax.random.key(seed)
    ks = jax.random.split(key, 26)
    f32 = jnp.float32

    def nrm(k, shape, fan_in):
        return jax.random.normal(k, shape, f32) * (fan_in ** -0.5)

    def gain(k, shape):
        return 1.0 + 0.05 * jax.random.normal(k, shape, f32)

    dt_init = jnp.exp(jax.random.uniform(ks[20], (N_B_LAYERS, SSM_HEADS), f32)
                      * (math.log(0.1) - math.log(0.001)) + math.log(0.001))
    dt_init = jnp.maximum(dt_init, 1e-4)
    return {
        "x": jax.random.normal(ks[0], (BATCH, SEQ, D_MODEL), f32),
        "positions": jnp.broadcast_to(jnp.arange(SEQ, dtype=jnp.int32), (BATCH, SEQ)),
        "ffn1_norm": gain(ks[1], (DEPTH, D_MODEL)),
        "ffn1_w_gate": nrm(ks[2], (DEPTH, D_MODEL, D_FF), D_MODEL),
        "ffn1_w_up": nrm(ks[3], (DEPTH, D_MODEL, D_FF), D_MODEL),
        "ffn1_w_down": nrm(ks[4], (DEPTH, D_FF, D_MODEL), D_FF),
        "mix_norm": gain(ks[5], (DEPTH, D_MODEL)),
        "ffn2_norm": gain(ks[6], (DEPTH, D_MODEL)),
        "ffn2_w_gate": nrm(ks[7], (DEPTH, D_MODEL, D_FF), D_MODEL),
        "ffn2_w_up": nrm(ks[8], (DEPTH, D_MODEL, D_FF), D_MODEL),
        "ffn2_w_down": nrm(ks[9], (DEPTH, D_FF, D_MODEL), D_FF),
        "attn_w_qkv": nrm(ks[10], (N_A_LAYERS, D_MODEL, 3 * D_MODEL), D_MODEL),
        "attn_q_norm": gain(ks[11], (N_A_LAYERS, ATTN_HEAD_DIM)),
        "attn_k_norm": gain(ks[12], (N_A_LAYERS, ATTN_HEAD_DIM)),
        "attn_w_o": nrm(ks[13], (N_A_LAYERS, D_MODEL, D_MODEL), D_MODEL),
        "ssm_w_in": nrm(ks[14], (N_B_LAYERS, D_MODEL, SSM_IN_DIM), D_MODEL),
        "ssm_conv_w": nrm(ks[15], (N_B_LAYERS, SSM_CONV, SSM_CONV_DIM), SSM_CONV),
        "ssm_conv_b": 0.02 * jax.random.normal(ks[16], (N_B_LAYERS, SSM_CONV_DIM), f32),
        "ssm_dt_bias": dt_init + jnp.log(-jnp.expm1(-dt_init)),
        "ssm_a_log": jnp.log(jax.random.uniform(ks[17], (N_B_LAYERS, SSM_HEADS), f32, 1.0, 16.0)),
        "ssm_d": 1.0 + 0.1 * jax.random.normal(ks[18], (N_B_LAYERS, SSM_HEADS), f32),
        "ssm_norm": gain(ks[19], (N_B_LAYERS, SSM_D_INNER)),
        "ssm_w_out": nrm(ks[21], (N_B_LAYERS, SSM_D_INNER, D_MODEL), SSM_D_INNER),
    }

def second_block(x, positions, ffn1_norm, ffn1_w_gate, ffn1_w_up, ffn1_w_down, mix_norm,
              ffn2_norm, ffn2_w_gate, ffn2_w_up, ffn2_w_down,
              attn_w_qkv, attn_q_norm, attn_k_norm, attn_w_o,
              ssm_w_in, ssm_conv_w, ssm_conv_b, ssm_dt_bias, ssm_a_log, ssm_d, ssm_norm, ssm_w_out):
    for i in range(DEPTH):
        x = x + 0.5 * swiglu_2(rms_norm(x, ffn1_norm[i]), ffn1_w_gate[i], ffn1_w_up[i], ffn1_w_down[i])
        h = rms_norm(x, mix_norm[i])
        j = i // N_MIXERS
        if i % N_MIXERS == 0:
            x = x + moba_mixer(h, positions, attn_w_qkv[j], attn_q_norm[j], attn_k_norm[j], attn_w_o[j])
        else:
            x = x + mamba2_mixer(h, ssm_w_in[j], ssm_conv_w[j], ssm_conv_b[j], ssm_dt_bias[j],
                                 ssm_a_log[j], ssm_d[j], ssm_norm[j], ssm_w_out[j])
        x = x + 0.5 * swiglu_2(rms_norm(x, ffn2_norm[i]), ffn2_w_gate[i], ffn2_w_up[i], ffn2_w_down[i])
    return x


def setup_inputs(seed=0):
    out = dict(first_inputs(seed))
    for name, value in second_inputs(seed + 1).items():
        if name != "x":
            out[name + "_2"] = value
    return out


def reference(
    x, positions, norm_mix, norm_ffn, conv_w_in, conv_w, conv_w_out, mla_w_down, mla_q_a_norm,
    mla_kv_a_norm, mla_w_uq, mla_w_ukv, mla_q_norm, mla_k_norm, mla_w_o, ffn_w_gate, ffn_w_up,
    ffn_w_down, moe_router, moe_w_gate, moe_w_up, moe_w_down, positions_2, ffn1_norm_2,
    ffn1_w_gate_2, ffn1_w_up_2, ffn1_w_down_2, mix_norm_2, ffn2_norm_2, ffn2_w_gate_2,
    ffn2_w_up_2, ffn2_w_down_2, attn_w_qkv_2, attn_q_norm_2, attn_k_norm_2, attn_w_o_2,
    ssm_w_in_2, ssm_conv_w_2, ssm_conv_b_2, ssm_dt_bias_2, ssm_a_log_2, ssm_d_2, ssm_norm_2,
    ssm_w_out_2,
):
    x = first_block(
        x, positions, norm_mix, norm_ffn, conv_w_in, conv_w, conv_w_out, mla_w_down,
        mla_q_a_norm, mla_kv_a_norm, mla_w_uq, mla_w_ukv, mla_q_norm, mla_k_norm, mla_w_o,
        ffn_w_gate, ffn_w_up, ffn_w_down, moe_router, moe_w_gate, moe_w_up, moe_w_down,
    )
    return second_block(
        x, positions_2, ffn1_norm_2, ffn1_w_gate_2, ffn1_w_up_2, ffn1_w_down_2, mix_norm_2,
        ffn2_norm_2, ffn2_w_gate_2, ffn2_w_up_2, ffn2_w_down_2, attn_w_qkv_2, attn_q_norm_2,
        attn_k_norm_2, attn_w_o_2, ssm_w_in_2, ssm_conv_w_2, ssm_conv_b_2, ssm_dt_bias_2,
        ssm_a_log_2, ssm_d_2, ssm_norm_2, ssm_w_out_2,
    )


_drawn_inputs = setup_inputs


def setup_inputs(seed=0):
    import zlib

    import numpy as np

    out = dict(_drawn_inputs(seed))
    spreads = {}
    factors = {'mla_q_a_norm': 8.0,
     'mla_kv_a_norm': 5.093,
     'mla_q_norm': 8.0,
     'mla_k_norm': 6.369,
     'attn_q_norm_2': 5.921,
     'attn_k_norm_2': 6.226,
     'ssm_conv_b_2': 3.164,
     'ffn2_norm_2': 5.463,
     'ssm_d_2': 2.784,
     'ssm_norm_2': 10.627}
    for name, (base, spread) in spreads.items():
        noise = np.random.default_rng([zlib.crc32(name.encode()), seed]).standard_normal(out[name].shape)
        drawn = base * np.exp(spread * noise) if base else spread * noise
        out[name] = __import__('jax').numpy.asarray(drawn.astype(out[name].dtype))
    for name, factor in factors.items():
        out[name] = (out[name] * factor).astype(out[name].dtype)
    return out
```

```python
import numpy as np
import concourse.bass as bass
from concourse import mybir
from concourse.alu_op_type import AluOpType as ALU
from contextlib import ExitStack

F32 = mybir.dt.float32
F32R = mybir.dt.float32r
I32 = mybir.dt.int32
ACT = mybir.ActivationFunctionType
AX = mybir.AxisListType

P = 128
SEQ = 256
NT = SEQ // P
D = 1024
KT = D // P
RAW = 6
SPLIT = 3
SLAB = 2048
EPS = 1e-6
F_DENSE = 2816
F_EXPERT = 2048
EXPERTS = 8
FC = 256
HEADS = 8
QK_NOPE, QK_ROPE = 128, 64
Q_RANK, KV_RANK = 384, 256
LATENT = Q_RANK + KV_RANK
DOWN = LATENT + QK_ROPE
HEAD = 128
THETA = 10000.0
D_INNER = 2048
SSM_HEADS = 32
SSM_HEAD = 64
GROUPS = 8
PER_GROUP = SSM_HEADS // GROUPS
TAPS = 4
START, STOP = 0, 99


def program(nc, a, out):
    ctx = ExitStack()
    with ctx:
        def sb(name, shape, dt=F32):
            return ctx.enter_context(nc.sbuf_tensor(name, shape, dt))

        def sem(name):
            return ctx.enter_context(nc.semaphore(name))

        raw = sb("raw", [P, RAW, SLAB])
        whi = sb("whi", [P, SPLIT, SLAB], F32R)
        wlo = sb("wlo", [P, SPLIT, SLAB], F32R)
        raw_full = [sem(f"raw_full{n}") for n in range(RAW)]
        slab_hi = sem("slab_hi")
        slab_split = sem("slab_split")
        slab_used = sem("slab_used")

        x = sb("x", [P, NT, D])
        actA_hi = sb("actA_hi", [P, KT, SEQ], F32R)
        actA_lo = sb("actA_lo", [P, KT, SEQ], F32R)
        actB_hi = sb("actB_hi", [P, KT, SEQ], F32R)
        actB_lo = sb("actB_lo", [P, KT, SEQ], F32R)
        hT_hi = sb("hT_hi", [P, 2 * SEQ], F32R)
        hT_lo = sb("hT_lo", [P, 2 * SEQ], F32R)
        h_tok = sb("h_tok", [P, NT, FC])
        silu_g = sb("silu_g", [P, NT, FC])
        big = sb("big", [P, 12800])
        ident = sb("ident", [P, P])
        zero_r = sb("zero_r", [P, P], F32R)
        vecs = sb("vecs", [P, 3, P])
        n_sum = sb("n_sum", [P, 10, NT])
        n_ms = sb("n_ms", [P, 10, NT])
        n_rstd = sb("n_rstd", [P, 10, NT])
        n_half = sb("n_half", [P, 64])
        aux = sb("aux", [P, 1408])
        gains = aux[:, 0:640]
        rope_cos = aux[:, 640:832].rearrange("p (t n) -> p t n", t=NT)
        rope_sin = aux[:, 832:1024].rearrange("p (t n) -> p t n", t=NT)
        mask = aux[:, 1024:1408]
        aux2 = sb("aux2", [P, 512])
        ident_r = sb("ident_r", [P, P], F32R)
        later_r = sb("later_r", [P, P], F32R)
        router_w = aux2[:, 256:256 + KT * EXPERTS]
        router_hi = sb("router_hi", [P, KT * EXPERTS], F32R)
        router_lo = sb("router_lo", [P, KT * EXPERTS], F32R)
        gates = sb("gates", [P, NT, EXPERTS])
        qk_ss = sb("qk_ss", [P, 2, 16])
        qk_rstd = sb("qk_rstd", [P, 2, 16])
        lat_ss = sb("lat_ss", [P, 2, NT])
        lat_rstd = sb("lat_rstd", [P, 2, NT])
        s_max = sb("s_max", [P, HEADS, NT])
        s_neg = sb("s_neg", [P, HEADS, NT])
        s_sum = sb("s_sum", [P, HEADS, NT])
        s_inv = sb("s_inv", [P, HEADS, NT])

        acc = ctx.enter_context(nc.psum_tensor("acc", [P, 4, 512], F32))
        gu = ctx.enter_context(nc.psum_tensor("gu", [P, 2, 512], F32))
        tp = ctx.enter_context(nc.psum_tensor("tp", [P, 2, 512], F32))
        banks6 = [acc[:, 0], acc[:, 1], acc[:, 2], acc[:, 3], gu[:, 0], gu[:, 1]]

        x_loaded = sem("x_loaded")
        gains_loaded = sem("gains_loaded")
        pos_loaded = sem("pos_loaded")
        mask_ready = sem("mask_ready")
        angles = sem("angles")
        tables_ready = sem("tables_ready")
        lat_full = sem("lat_full")
        lat_sum = sem("lat_sum")
        lat_root = sem("lat_root")
        lat_tok = sem("lat_tok")
        rows_loaded = sem("rows_loaded")
        rows_zero = sem("rows_zero")
        vecs_full = sem("vecs_full")
        vecs_ready = sem("vecs_ready")
        masks_ready = sem("masks_ready")
        x_ready = sem("x_ready")
        norm_sum = sem("norm_sum")
        norm_rstd = sem("norm_rstd")
        norm_tok = sem("norm_tok")
        tp_full = sem("tp_full")
        tp_hi = sem("tp_hi")
        tp_read = sem("tp_read")
        gu_silu = sem("gu_silu")
        gu_read = sem("gu_read")
        out_done = sem("out_done")

        V_MIX, V_FFN, V_CONV, V_QA, V_KVA = (0, 0), (0, 16), (0, 32), (0, 56), (0, 59)
        V_FFN1, V_MIX2, V_FFN2 = (0, 61), (0, 77), (0, 93)
        V_SCONV, V_SBIAS, V_SNORM = (1, 0), (2, 0), (2, 32)

        def col(v, n):
            return vecs[:, v[0], v[1] + n:v[1] + n + 1]

        row_loads = [(V_MIX, 16, a["norm_mix"]), (V_FFN, 16, a["norm_ffn"]), (V_CONV, 24, a["conv_w"]),
                     (V_QA, 3, a["mla_q_a_norm"]), (V_KVA, 2, a["mla_kv_a_norm"]), (V_FFN1, 16, a["ffn1_norm_2"]),
                     (V_MIX2, 16, a["mix_norm_2"]), (V_FFN2, 16, a["ffn2_norm_2"]), (V_SCONV, 128, a["ssm_conv_w_2"]),
                     (V_SBIAS, 32, a["ssm_conv_b_2"]), (V_SNORM, 16, a["ssm_norm_2"])]

        class Stage:

            def __init__(self, kind, kw):
                self.kind = kind
                self.s0, self.u0, self.h0, self.x0, self.c0, self.m = [count[k] for k in (
                    "slab", "tp", "hi", "x", "chunk", "norm")]
                self.gate, self.up, self.down, self.C = kw.get("gate"), kw.get("up"), kw.get("down"), kw.get("C")
                self.scale, self.experts, self.gates = kw.get("scale"), kw.get("experts"), kw.get("gates")
                self.gain, self.w, self.act, self.ready = kw.get("gain"), kw.get("w"), kw.get("act"), kw.get("ready")
                self.n, self.sems, self.mem, self.parts = kw.get("n"), kw.get("sems"), kw.get("mem"), kw.get("parts")
                self.Dh, self.half, self.rope0 = kw.get("Dh"), kw.get("half"), kw.get("rope0")
                self.angle0, self.gain0 = kw.get("angle0"), kw.get("gain0")

        stages = []
        count = dict(slab=0, tp=0, hi=0, x=0, chunk=0, norm=0)
        x_count = 0

        def stage(kind, slabs=0, tp=0, hi=0, x=0, chunk=0, norm=0, **kw):
            f = Stage(kind, kw)
            for k, n in zip(("slab", "tp", "hi", "x", "chunk", "norm"), (slabs, tp, hi, x, chunk, norm)):
                count[k] += n
            stages.append(f)

        def ffn_stage(gate, up, down, scale, experts=1, gates=None):
            C = gate.shape[-1] // FC
            stage("ffn", slabs=3 * C * experts, tp=C * experts, hi=C * experts, x=experts, chunk=C * experts,
                  gate=gate, up=up, down=down, C=C, scale=scale, experts=experts, gates=gates)

        vec_rows = big[:, 6144:6144 + 3 * P].rearrange("p (a b) -> p a b", a=3)

        def norm_stage(gain):
            stage("norm", tp=4, hi=4, norm=1, gain=gain)

        def out_stage(w, act, ready):
            stage("out", slabs=4, x=2, w=w, act=act, ready=ready)

        def attention_sems(n):
            return {k: sem(f"{k}{n}") for k in ("qk_evac", "qk_square", "qk_sum", "qk_root", "qk_done", "head_T", "head_q",
                                                "head_k", "head_scores", "head_masked", "head_max", "head_exp", "head_p",
                                                "head_pT", "head_pcopy", "head_o", "head_ohi", "head_olo")}

        def attention_stage(n, **kw):
            f_sems = attention_sems(n)
            stage("attention", n=n, sems=f_sems, **kw)
            return f_sems

        conv_lo = sem("conv_lo")
        A, B = (actA_hi, actA_lo), (actB_hi, actB_lo)

        def conv_mixer():
            norm_stage((V_MIX, 0))
            stage("conv_in", slabs=12)
            out_stage(a["conv_w_out"][0], B, (conv_lo, 4))

        def latent_mixer():
            norm_stage((V_MIX, 8))
            stage("mla_down", slabs=4, tp=3, hi=3)
            stage("mla_up", slabs=7)
            q = attention_stage(1, Dh=QK_NOPE + QK_ROPE, half=QK_ROPE // 2, rope0=QK_NOPE, angle0=0, gain0=0,
                                parts=[(0, QK_NOPE), (QK_NOPE, QK_ROPE)], mem=mla_mem)
            out_stage(a["mla_w_o"][0], A, (q["head_olo"], HEADS))

        def block_attention_mixer():
            norm_stage((V_MIX2, 0))
            stage("qkv", slabs=12)
            q = attention_stage(2, Dh=HEAD, half=HEAD // 2, rope0=0, angle0=QK_ROPE // 2, gain0=2 * (QK_NOPE + QK_ROPE),
                                parts=[(0, HEAD)], mem=moba_mem)
            out_stage(a["attn_w_o_2"][0], A, (q["head_olo"], HEADS))

        def experts_mixture():
            norm_stage((V_FFN, 8))
            stage("router")
            ffn_stage(a["moe_w_gate"][0], a["moe_w_up"][0], a["moe_w_down"][0], None, EXPERTS, gates)

        def state_space_mixer():
            norm_stage((V_MIX2, 8))
            stage("ssm_in", slabs=25, tp=8)
            stage("ssd")
            stage("ssm_out", slabs=8, tp=8, hi=8, x=2)

        def swiglu(gain, names, layer, scale):
            norm_stage(gain)
            ffn_stage(*[a[n][layer] for n in names], scale)

        FFN0 = ("ffn_w_gate", "ffn_w_up", "ffn_w_down")
        FFN1 = ("ffn1_w_gate_2", "ffn1_w_up_2", "ffn1_w_down_2")
        FFN2 = ("ffn2_w_gate_2", "ffn2_w_up_2", "ffn2_w_down_2")

        def area(at, n):
            return big[:, at:at + n]

        mla_dn = area(0, NT * DOWN).rearrange("p (t n) -> p t n", t=NT)
        mla_cn = area(9600, NT * LATENT).rearrange("p (t n) -> p t n", t=NT)
        mla_qk = [area(1408 + 3072 * w, 3072).rearrange("p (t h n) -> p t h n", t=NT, h=HEADS) for w in range(2)]
        mla_v = area(7552, 2048).rearrange("p (t n) -> p t n", t=NT)
        mla_mem = dict(qk=mla_qk, v=mla_v, s=area(9600, 3072), pT=area(1408, 3072),
                       stage=[(h_tok[:, :, :].rearrange("p t n -> p (t n)"), silu_g[:, :, :].rearrange("p t n -> p (t n)")),
                              (area(0, 512), area(512, 512))])
        qkv = area(0, 6144).rearrange("p (t n) -> p t n", t=NT)
        moba_mem = dict(qk=[qkv[:, :, 1024 * w:1024 * (w + 1)].rearrange("p t (h n) -> p t h n", h=HEADS) for w in range(2)],
                        v=qkv[:, :, 2048:3072], s=area(6144, 3072), pT=area(9216, 3072),
                        stage=[(h_tok[:, :, :].rearrange("p t n -> p (t n)"), silu_g[:, :, :].rearrange("p t n -> p (t n)")),
                               (area(12288, 256), area(12544, 256))])

        plan = [conv_mixer,
                lambda: swiglu((V_FFN, 0), FFN0, 0, 1.0),
                latent_mixer,
                experts_mixture,
                lambda: swiglu((V_FFN1, 0), FFN1, 0, 0.5),
                block_attention_mixer,
                lambda: swiglu((V_FFN2, 0), FFN2, 0, 0.5),
                lambda: swiglu((V_FFN1, 8), FFN1, 1, 0.5),
                state_space_mixer,
                lambda: swiglu((V_FFN2, 8), FFN2, 1, 0.5)]
        for step in plan[START:STOP]:
            step()
        stages_used = stages
        total_slabs = count["slab"]
        x_total = count["x"]

        vT = big[:, 0:2 * (SEQ + 2)].rearrange("p (b n) -> p b n", b=2)
        cT = big[:, 600:600 + 512]
        convT = big[:, 1200:1200 + 512]
        gT = big[:, 1800:1800 + 512]
        hn = big[:, 4096:4096 + NT * D].rearrange("p (t d) -> p t d", t=NT)

        conv_c = sem("conv_c")
        conv_read = sem("conv_read")
        conv_g = sem("conv_g")
        conv_hi = sem("conv_hi")

        def small(n, at=0):
            return silu_g[:, :, :].rearrange("p t n -> p (t n)")[:, at:at + n]

        def small2(n, at=0):
            return h_tok[:, :, :].rearrange("p t n -> p (t n)")[:, at:at + n]

        rt = [area(8192 + 16 * n, 16).rearrange("p (t e) -> p t e", t=NT) for n in range(8)]
        rt_row = [area(8320 + 2 * n, 2) for n in range(10)]
        rank8 = area(8352, 16).rearrange("p (t e) -> p t e", t=NT)
        router_loaded, router_split, router_logits = sem("router_loaded"), sem("router_split"), sem("router_logits")
        router_shift, router_exp, router_done = sem("router_shift"), sem("router_exp"), sem("router_done")
        rank_ready = sem("rank_ready")

        ssm_x = area(0, 4096).rearrange("p (t n) -> p t n", t=NT)
        ssm_bc = area(4096, 4096).rearrange("p (b n) -> p b n", b=16)
        ssm_z = area(8192, 4096).rearrange("p (t n) -> p t n", t=NT)
        pad_x = [area(8192 + 520 * n, 518).rearrange("p (b n) -> p b n", b=2) for n in range(2)]
        cv_x = [area(9240 + 512 * n, 512) for n in range(2)]
        si_x = [area(10264 + 512 * n, 512) for n in range(2)]
        tri, ones = small2(128, 0), small2(128, 128)
        skip_bc, bias_bc, alog_bc, decay_rate = [small2(32, 256 + 32 * n) for n in range(4)]
        dt_tok, a_tok = small2(64, 384), small2(64, 448)
        dt_in, dt_abs, dt_exp, dt_z, dt_z2, dt_poly, neg_cum = [small(64, 64 * n) for n in range(7)]
        decay0, exp_cum1 = small(32, 448), small(32, 480)
        m_buf = [aux[:, 0:512], aux[:, 512:1024]]
        cb_buf = [aux[:, 1024:1152], aux[:, 1152:1280]]
        b_tok = aux[:, 1280:1408]
        xdt_buf = [area(12288, 256), area(12544, 256)]
        xdecay, state = aux2[:, 0:256], aux2[:, 256:512]
        ssm_const, ssm_rows, dt_ready, dt_e, a_ready, a_rate, cum_full, cum_neg, cum_exp = [sem(n) for n in (
            "ssm_const", "ssm_rows", "dt_ready", "dt_e", "a_ready", "a_rate", "cum_full", "cum_neg", "cum_exp")]
        sx_copy, sx_conv, sx_silu, sz_silu = sem("sx_copy"), sem("sx_conv"), sem("sx_silu"), sem("sz_silu")
        sd_cb, sd_seg, sd_cbe, sd_exp, sd_x, sd_m, sd_y, sd_st, sd_read, sd_sq, sd_root, sd_tok = [sem(n) for n in (
            "sd_cb", "sd_seg", "sd_cbe", "sd_exp", "sd_x", "sd_m", "sd_y", "sd_st", "sd_read", "sd_sq", "sd_root", "sd_tok")]

        sq_junk, y_off = small(256, 0), sb("y_off", [P, 256])[:, :]
        mla_evac = sem("mla_evac")
        qkv_evac = sem("qkv_evac")
        inv_freq = area(7168, 96)
        pos_int = area(7296, 4).bitcast(I32).rearrange("p (w t) -> p w t", w=2)
        pos_f = area(7312, 4).rearrange("p (w t) -> p w t", w=2)
        ang = area(7328, 3 * 192).rearrange("p (a n) -> p a n", a=3)
        banks_pair = [acc[:, 0:2, :], acc[:, 2:4, :], gu[:, :, :]]

        def banks_pair_of(n):
            return [banks_pair[n][:, 0], banks_pair[n][:, 1]]

        block = ctx.enter_context(nc.Block())

        def used(e, base, k, i=0, per=0):
            e.wait_ge(slab_used, base + k + 1 + SPLIT + RAW * i + RAW * per)

        def positions(e, f, fn):
            C = f.C
            fn(0, 0)
            fn(1, 0)
            trips = (C - 1) // 2 - (f is stages_used[-1])
            with e.Fori(0, trips) as i:
                for k in range(2, 8):
                    fn(k, i)
            for k in range(2 + 6 * trips, 3 * C):
                fn(k, 0)

        def ffn_kind(k, C):
            if k < 2:
                return ("up_a", "up_b")[k], 0
            if k == 3 * C - 1:
                return "down", C - 1
            return (("up_a", (k + 1) // 3), ("up_b", k // 3), ("down", (k - 4) // 3))[(k - 2) % 3]

        def over_experts(e, f, fn):
            if f.experts == 1:
                fn(0)
            else:
                with e.Fori(0, f.experts) as ex:
                    fn(ex)

        @block.sync
        def _(sp):
            def load(s, slot, first, halves):
                sp.wait_ge(slab_split, s + 1)
                for dst, src in halves(raw[:, slot]):
                    sp.dma_start(dst, src).then_inc(raw_full[slot], 16)

            def in_cols(w, c0, n, kts):
                kh = (kts[0] + kts[-1] + 1) // 2 if len(kts) > 1 else None

                def halves(slot):
                    v = slot[:, 0:len(kts) * n].rearrange("p (k n) -> p k n", n=n)
                    src = w.rearrange("(k p) n -> p k n", p=P)
                    if kh is None:
                        h = n // 2
                        return [(v[:, :, 0:h], src[:, kts[0]:kts[-1] + 1, c0:c0 + h]),
                                (v[:, :, h:n], src[:, kts[0]:kts[-1] + 1, c0 + h:c0 + n])]
                    a0 = kh - kts[0]
                    cols = slice(c0, c0 + n) if isinstance(c0, int) else bass.ds(c0, n)
                    return [(v[:, 0:a0], src[:, kts[0]:kh, cols]),
                            (v[:, a0:], src[:, kh:kts[-1] + 1, cols])]
                return halves

            def ffn_loads(f):
                def expert(ex):
                    def w_of(w):
                        return w if f.experts == 1 else w[bass.ds(ex, 1)].rearrange("e k n -> (e k) n")

                    def at(k, i):
                        kind, c = ffn_kind(k, f.C)
                        c = c + 2 * i
                        s = f.s0 + k + 6 * i + 3 * f.C * ex

                        def halves(slot):
                            if kind == "down":
                                v = slot.rearrange("p (j n) -> p j n", j=2)
                                src = w_of(f.down)[bass.ds(c * FC, FC), :].rearrange("(j p) n -> p j n", p=P)
                                return [(v[:, j], src[:, j]) for j in range(2)]
                            k0 = 0 if kind == "up_a" else 4
                            v = slot.rearrange("p (k n) -> p k n", k=4)
                            return [(v[:, :, h * FC:(h + 1) * FC],
                                     w_of(w).rearrange("(k p) n -> p k n", p=P)[:, k0:k0 + 4, bass.ds(c * FC, FC)])
                                    for h, w in enumerate((f.gate, f.up))]
                        load(s, (f.s0 + k) % RAW, k, halves)
                    positions(sp, f, at)
                over_experts(sp, f, expert)

            sp.dma_start(x[:, :, :], a["x"].rearrange("(t p) d -> p t d", p=P)).then_inc(x_loaded, 16)
            for f in stages_used:
                if f.kind == "conv_in":
                    for n in range(12):
                        c0 = (1024, 2048, 0)[n % 3] + 256 * (n // 3)
                        load(f.s0 + n, (f.s0 + n) % RAW, n, in_cols(a["conv_w_in"][0], c0, 256, list(range(8))))
                elif f.kind == "out":
                    for n in range(4):
                        load(f.s0 + n, (f.s0 + n) % RAW, n,
                             in_cols(f.w, 512 * (n // 2), 512, list(range(4 * (n % 2), 4 * (n % 2) + 4))))
                elif f.kind == "mla_down":
                    for n in range(4):
                        load(f.s0 + n, (f.s0 + n) % RAW, n,
                             in_cols(a["mla_w_down"][0], 352 * (n // 2), 352, list(range(4 * (n % 2), 4 * (n % 2) + 4))))
                elif f.kind == "mla_up":
                    for n in range(7):
                        w, kts, c = (a["mla_w_uq"][0], [0, 1, 2], n) if n < 3 else (a["mla_w_ukv"][0], [0, 1], n - 3)
                        load(f.s0 + n, (f.s0 + n) % RAW, n, in_cols(w, 512 * c, 512, kts))
                elif f.kind == "qkv":
                    with sp.Fori(0, 2) as i:
                        for n in range(6):
                            load(f.s0 + n + 6 * i, (f.s0 + n) % RAW, n,
                                 in_cols(a["attn_w_qkv_2"][0], 512 * (n // 2) + 1536 * i, 512,
                                         list(range(4 * (n % 2), 4 * (n % 2) + 4))))
                elif f.kind == "ssm_in":
                    w = a["ssm_w_in_2"][0]
                    for n in range(25):
                        if n == 0:
                            h = in_cols(w, 3 * D_INNER, SSM_HEADS, list(range(8)))
                        elif n <= 16:
                            h = in_cols(w, D_INNER + 256 * (n - 1), 256, list(range(8)))
                        else:
                            k4 = 4 * ((n - 17) % 2)
                            h = in_cols(w, 512 * ((n - 17) // 2), 512, list(range(k4, k4 + 4)))
                        load(f.s0 + n, (f.s0 + n) % RAW, n, h)
                elif f.kind == "ssm_out":
                    for n in range(8):
                        load(f.s0 + n, (f.s0 + n) % RAW, n,
                             in_cols(a["ssm_w_out_2"][0], 512 * (n // 4), 512, list(range(4 * (n % 4), 4 * (n % 4) + 4))))
                elif f.kind == "ffn":
                    ffn_loads(f)
            sp.wait_ge(x_ready, x_total)
            sp.dma_start(out.rearrange("(t p) d -> p t d", p=P), x[:, :, :]).then_inc(out_done, 16)
            sp.wait_ge(out_done, 16)

        @block.gpsimd
        def _(pool):
            pool.memset(vec_rows[:, :, :], 0.0).then_inc(rows_zero, 1)
            pool.memset(ident[:, :], 0.0)
            pool.memset(zero_r[:, :].bitcast(F32), 0.0)
            pool.memset(n_half[:, :], -0.5)
            pool.memset(mask[:, :], 0.0)
            later_f = aux2[:, 0:P]
            pool.memset(later_f, 0.0)
            pool.drain()
            pool.affine_select(out=later_f, in_=later_f, compare_op=ALU.is_ge, fill=-1e30, base=0,
                               pattern=[[1, P]], channel_multiplier=-1).then_inc(masks_ready, 1)
            pool.affine_select(out=ident[:, :], in_=ident[:, :], compare_op=ALU.not_equal, fill=1.0, base=0,
                               pattern=[[-1, P]], channel_multiplier=1).then_inc(masks_ready, 1)
            pool.wait_ge(rows_zero, 1)
            for v, n, src in row_loads:
                flat = src.rearrange("a b -> (a b)") if len(src.shape) == 2 else src.rearrange("a b c -> (a b c)")
                pool.dma_start(vec_rows[v[1]:v[1] + n, v[0], :], flat.rearrange("(r c) -> r c", c=P)).then_inc(rows_loaded, 16)
            at = 0
            for name in ("mla_q_norm", "mla_k_norm", "attn_q_norm_2", "attn_k_norm_2"):
                n = a[name].shape[-1]
                pool.dma_start(gains[:, at:at + n], a[name].broadcast_to([P, n])).then_inc(gains_loaded, 16)
                at += n
            pool.dma_start(inv_freq[:, :], a["inv_freq"].broadcast_to([P, 96])).then_inc(pos_loaded, 16)
            with nc.allow_non_contiguous_dma(reason="256 positions"):
                for w, name in enumerate(("positions", "positions_2")):
                    pool.dma_start(pos_int[:, w], a[name].rearrange("a (t p) -> p (a t)", p=P)).then_inc(pos_loaded, 16)
            pool.affine_select(out=mask[:, 0:P], in_=mask[:, 0:P], compare_op=ALU.is_ge, fill=-3e38, base=0,
                               pattern=[[-1, P]], channel_multiplier=1).then_inc(mask_ready, 1)
            pool.affine_select(out=mask[:, 2 * P:3 * P], in_=mask[:, 2 * P:3 * P], compare_op=ALU.is_ge, fill=-3e38, base=0,
                               pattern=[[-1, P]], channel_multiplier=1).then_inc(mask_ready, 1)
            pool.dma_start(router_w[:, :].rearrange("p (k e) -> p k e", e=EXPERTS),
                           a["moe_router"][0].rearrange("(k p) e -> p k e", p=P)).then_inc(router_loaded, 16)
            for f in stages_used:
                if f.kind == "router":
                    for e in range(EXPERTS):
                        pool.memset(rank8[:, :, e:e + 1], float(EXPERTS - e)).then_inc(rank_ready, 1)
                if f.kind == "ssm_in":
                    pool.memset(tri, 1.0)
                    pool.memset(ones, 1.0)
                    pool.drain()
                    pool.affine_select(out=tri, in_=tri, compare_op=ALU.is_ge, fill=0.0, base=0, pattern=[[1, P]],
                                       channel_multiplier=-1).then_inc(ssm_const, 1)
                    for v, name in ((skip_bc, "ssm_d_2"), (bias_bc, "ssm_dt_bias_2"), (alog_bc, "ssm_a_log_2")):
                        pool.dma_start(v, a[name].broadcast_to([P, SSM_HEADS])).then_inc(ssm_rows, 16)
                if f.kind == "ssd":
                    pool.wait_ge(sd_sq, 16)
                    ss = qk_ss[:, 0, :]
                    pool.tensor_scalar(ss, ss, 1.0 / (D_INNER // GROUPS), EPS, ALU.mult, ALU.add)
                    pool.drain()
                    pool.tensor_tensor(qk_rstd[:, 0, :], ss, n_half[:, 0:16], ALU.pow).then_inc(sd_root, 1)
                if f.kind == "norm":
                    m = f.m
                    pool.wait_ge(norm_sum, 2 * (m + 1))
                    pool.tensor_scalar(n_ms[:, m, :], n_sum[:, m, :], 1.0 / D, EPS, ALU.mult, ALU.add)
                    pool.drain()
                    pool.tensor_tensor(n_rstd[:, m, :], n_ms[:, m, :], n_half[:, 0:NT], ALU.pow).then_inc(norm_rstd, 1)
                elif f.kind == "mla_down":
                    pool.wait_ge(lat_sum, 4)
                    for w, n in enumerate((Q_RANK, KV_RANK)):
                        pool.tensor_scalar(lat_ss[:, w, :], lat_ss[:, w, :], 1.0 / n, EPS, ALU.mult, ALU.add)
                        pool.drain()
                        pool.tensor_tensor(lat_rstd[:, w, :], lat_ss[:, w, :], n_half[:, 0:NT], ALU.pow).then_inc(lat_root, 1)
                elif f.kind == "attention":
                    for w in range(2):
                        pool.wait_ge(f.sems["qk_sum"], w + 1)
                        pool.tensor_scalar(qk_ss[:, w, :], qk_ss[:, w, :], 1.0 / f.Dh, EPS, ALU.mult, ALU.add)
                        pool.drain()
                        pool.tensor_tensor(qk_rstd[:, w, :], qk_ss[:, w, :], n_half[:, 0:16], ALU.pow).then_inc(f.sems["qk_root"], 1)

        @block.scalar
        def _(act):
            def split_hi(base, k, i, per):
                n0 = base + k
                act.wait_ge(raw_full[n0 % RAW], 32 * (n0 // RAW + 1) + 32 * i + 32 * per)
                act.wait_ge(slab_used, n0 + 1 + RAW * i + RAW * per)
                act.activation(whi[:, n0 % SPLIT], raw[:, n0 % RAW], ACT.Copy).then_inc(slab_hi, 1)

            def ahead(base, k, i=0, per=0):
                if base + k + 2 < total_slabs:
                    split_hi(base, k + 2, i, per)

            def norm(f):
                m = f.m
                if m == 0:
                    act.wait_ge(x_loaded, 16)
                else:
                    act.wait_ge(x_ready, f.x0)
                for t in range(NT):
                    act.activation(hn[:, t], x[:, t], ACT.Square, accum_out=n_sum[:, m, t:t + 1]).then_inc(norm_sum, 1)
                if m == 0:
                    act.wait_ge(vecs_ready, 1)
                v, g0 = f.gain
                for b in range(4):
                    act.wait_ge(tp_full, f.u0 + b + 1)
                    for j in range(2):
                        r = act.activation(actA_hi[:, 2 * b + j, :], tp[:, (f.u0 + b) % 2, j * SEQ:(j + 1) * SEQ],
                                           ACT.Copy, scale=col(v, g0 + 2 * b + j))
                    r.then_inc(tp_hi, 1)

            def ffn(f):
                C = f.C

                def t_hi(k, c, i, ex):
                    act.wait_ge(tp_full, f.u0 + c + 1 + 2 * i + C * ex)
                    act.activation(hT_hi[:, :], tp[:, (f.u0 + c) % 2], ACT.Copy).then_inc(tp_hi, 1)

                def expert(ex):
                    def at(k, i):
                        kind, c = ffn_kind(k, C)
                        ahead(f.s0, k, i, C // 2 * ex)
                        if kind == "up_b":
                            used(act, f.s0, k, i, C // 2 * ex)
                            act.activation(silu_g[:, :, :], gu[:, :, 0:FC], ACT.Silu).then_inc(gu_silu, 1)
                            if c == 0:
                                t_hi(k, 0, 0, ex)
                        elif kind == "down" and c < C - 1:
                            t_hi(k, c + 1, i, ex)
                    positions(act, f, at)
                over_experts(act, f, expert)

            def attention(f):
                q = f.sems
                mem = f.mem
                Dh, s = f.Dh, mem["s"]
                for w in range(2):
                    if w:
                        act.wait_ge(q["qk_sum"], w)
                    if f.n == 1:
                        act.wait_ge(q["qk_evac"], 1)
                    else:
                        act.drain()
                    act.activation(s[:, 0:16 * Dh].rearrange("p (t h n) -> p t h n", t=NT, h=HEADS), mem["qk"][w],
                                   ACT.Square).then_inc(q["qk_square"], 1)

                def softmax(h):
                    act.wait_ge(q["head_max"], h + 1)
                    for t in range(NT):
                        v = s[:, h * 384 + t * P:h * 384 + (t + 1) * P + t * P]
                        act.activation(v, v, ACT.Exp, bias=s_neg[:, h, t:t + 1],
                                       accum_out=s_sum[:, h, t:t + 1]).then_inc(q["head_exp"], 1)

                for h in range(HEADS + 1):
                    if h < HEADS:
                        act.wait_ge(q["head_T"], h + 1)
                        if h >= 2:
                            act.wait_ge(q["head_scores"], h - 1)
                        for n, (d0, dn) in enumerate(f.parts):
                            r = act.activation(mem["stage"][h % 2][0][0:dn, n * SEQ:(n + 1) * SEQ],
                                               gu[0:dn, 0, n * SEQ:(n + 1) * SEQ], ACT.Copy)
                        r.then_inc(q["head_q"], 1)
                    if h:
                        softmax(h - 1)
                for h in range(HEADS + 1):
                    if h < HEADS:
                        act.wait_ge(q["head_pT"], h + 1)
                        act.activation(mem["pT"][:, h * 384:(h + 1) * 384], gu[:, h % 2, 0:384],
                                       ACT.Copy).then_inc(q["head_pcopy"], 1)
                    if h:
                        act.wait_ge(q["head_o"], h)
                        act.activation(actA_hi[:, h - 1, :], acc[:, (h - 1) % 4, 0:SEQ], ACT.Copy).then_inc(q["head_ohi"], 1)

            def ssm_in(f):
                def silu_conv(p):
                    act.wait_ge(sx_conv, p + 1)
                    if 2 <= p < 8:
                        act.wait_ge(tp_full, f.u0 + p - 1)
                    for b in range(2):
                        o = si_x[p % 2][:, b * SEQ:(b + 1) * SEQ] if p < 8 else ssm_bc[:, 2 * (p - 8) + b, :]
                        r = act.activation(o, cv_x[p % 2][:, b * SEQ:(b + 1) * SEQ], ACT.Silu, bias=col(V_SBIAS, 2 * p + b))
                    r.then_inc(sx_silu, 1)

                for n in range(25):
                    ahead(f.s0, n)
                    if n == 0:
                        act.wait_ge(ssm_rows, 48)
                        act.activation(decay_rate, alog_bc, ACT.Exp).then_inc(a_rate, 1)
                        act.wait_ge(dt_ready, 1)
                        act.activation(dt_exp, dt_abs, ACT.Exp, scale=-1.0).then_inc(dt_e, 1)
                    elif n <= 16:
                        p = n - 1
                        used(act, f.s0, n)
                        if p >= 2:
                            act.wait_ge(sx_conv, p - 1)
                        else:
                            act.wait_ge(a_ready, 1)
                        act.activation(pad_x[p % 2][:, :, TAPS - 1:], banks6[p % 3].rearrange("p (b n) -> p b n", b=2),
                                       ACT.Copy).then_inc(sx_copy, 1)
                        if p:
                            silu_conv(p - 1)
                    if n == 17:
                        silu_conv(15)
                        act.wait_ge(cum_neg, 2)
                        act.activation(decay0, decay0, ACT.Exp)
                        act.activation(exp_cum1, exp_cum1, ACT.Exp).then_inc(cum_exp, 1)
                        act.wait_ge(tp_full, f.u0 + 8)
                        act.drain()
                    if n >= 17 and (n - 17) % 2:
                        c = (n - 17) // 2
                        used(act, f.s0, n)
                        act.activation(ssm_z[:, :, 512 * c:512 * (c + 1)], banks_pair[c % 2], ACT.Silu).then_inc(sz_silu, 1)

            def ssd(f):
                def squares(n):
                    g, t = n // 2, n % 2
                    act.wait_ge(sd_read, n + 1)
                    act.activation(sq_junk, ssm_x[:, t, 256 * g:256 * (g + 1)], ACT.Square,
                                   accum_out=qk_ss[:, 0, 8 * t + g:8 * t + g + 1]).then_inc(sd_sq, 1)
                    act.drain()

                for n in range(16):
                    g, t = n // 2, n % 2
                    act.wait_ge(sd_cb, n + 1)
                    if n >= 2:
                        act.wait_ge(sd_m, n - 1)
                        act.wait_ge(sd_y, n - 1)
                    if t == 0:
                        act.activation(b_tok, gu[:, 0, P:2 * P], ACT.Copy)
                    act.activation(cb_buf[n % 2], gu[:, 0, 0:P], ACT.Copy).then_inc(sd_cbe, 1)
                    act.wait_ge(sd_seg, n + 1)
                    for r in range(PER_GROUP):
                        h = PER_GROUP * g + r
                        i = act.activation(m_buf[n % 2][:, r * P:(r + 1) * P], acc[:, n % 2, r * P:(r + 1) * P], ACT.Exp,
                                           bias=neg_cum[:, SSM_HEADS * t + h:SSM_HEADS * t + h + 1])
                    i.then_inc(sd_exp, 1)
                    if t == 1:
                        act.wait_ge(sd_y, n)
                        act.activation(state, gu[:, 1, 0:256], ACT.Copy).then_inc(sd_st, 1)
                    if n >= 2:
                        squares(n - 2)
                squares(14)
                squares(15)

            def ssm_out(f):
                for b in range(8):
                    act.wait_ge(tp_full, f.u0 + b + 1)
                    hi_t = actA_hi if b < 4 else actB_hi
                    for j in range(2):
                        r = act.activation(hi_t[:, (2 * b + j) % KT, :], tp[:, (f.u0 + b) % 2, j * SEQ:(j + 1) * SEQ],
                                           ACT.Copy, scale=col(V_SNORM, 2 * b + j))
                    r.then_inc(tp_hi, 1)
                for n in range(8):
                    ahead(f.s0, n)

            act.wait_ge(masks_ready, 2)
            act.activation(ident_r[:, :], ident[:, :], ACT.Copy)
            act.activation(later_r[:, :], aux2[:, 0:P], ACT.Copy)
            act.wait_ge(router_loaded, 16)
            act.activation(router_hi[:, :], router_w[:, :], ACT.Copy).then_inc(router_split, 1)
            act.wait_ge(angles, 1)
            act.activation(rope_sin[:, :, :].rearrange("p t n -> p (t n)"), ang[:, 0], ACT.Sin)
            act.activation(rope_cos[:, :, :].rearrange("p t n -> p (t n)"), ang[:, 1], ACT.Sin).then_inc(tables_ready, 1)
            ahead(0, -2)
            ahead(0, -1)
            for f in stages_used:
                if f.kind == "norm":
                    norm(f)
                elif f.kind == "attention":
                    attention(f)
                elif f.kind == "router":
                    act.wait_ge(router_shift, 1)
                    act.activation(rt[1], rt[0], ACT.Exp).then_inc(router_exp, 1)
                elif f.kind == "ssm_in":
                    ssm_in(f)
                elif f.kind == "ssd":
                    ssd(f)
                elif f.kind == "ssm_out":
                    ssm_out(f)
                elif f.kind == "mla_down":
                    for n in range(4):
                        ahead(f.s0, n)
                        if n % 2:
                            c = n // 2
                            used(act, f.s0, n)
                            act.activation(mla_dn[:, :, 352 * c:352 * (c + 1)], acc[:, 2 * c:2 * c + 2, 0:352],
                                           ACT.Copy).then_inc(lat_full, 1)
                    act.drain()
                    for w, (c0, n) in enumerate(((0, Q_RANK), (Q_RANK, KV_RANK))):
                        for t in range(NT):
                            act.activation(area(9600 + LATENT * t + c0, n), mla_dn[:, t, c0:c0 + n], ACT.Square,
                                           accum_out=lat_ss[:, w, t:t + 1]).then_inc(lat_sum, 1)
                    for b in range(3):
                        act.wait_ge(tp_full, f.u0 + b + 1)
                        for kt in range(2 * b, min(2 * b + 2, 5)):
                            v = col(V_QA, kt) if kt < 3 else col(V_KVA, kt - 3)
                            r = act.activation(actB_hi[:, kt, :], tp[:, (f.u0 + b) % 2, (kt % 2) * SEQ:(kt % 2 + 1) * SEQ],
                                               ACT.Copy, scale=v)
                        r.then_inc(tp_hi, 1)
                elif f.kind == "mla_up":
                    for n in range(7):
                        ahead(f.s0, n)
                        used(act, f.s0, n)
                        bank = acc[:, 2 * (n % 2):2 * (n % 2) + 2, :]
                        if n < 3:
                            r = act.activation(area(1408, 3072).rearrange("p (t n) -> p t n", t=NT)[:, :, 512 * n:512 * (n + 1)],
                                               bank, ACT.Copy)
                        else:
                            for t in range(NT):
                                kv = bank[:, t].rearrange("p (h n) -> p h n", h=2)
                                h0 = 2 * (n - 3)
                                act.activation(mla_qk[1][:, t, h0:h0 + 2, 0:QK_NOPE], kv[:, :, 0:HEAD], ACT.Copy)
                                r = act.activation(mla_v[:, t, h0 * HEAD:(h0 + 2) * HEAD].rearrange("p (h n) -> p h n", h=2),
                                                   kv[:, :, HEAD:], ACT.Copy)
                        r.then_inc(mla_evac, 1)
                elif f.kind == "qkv":
                    act.sem_inc(qkv_evac, 3)
                    with act.Fori(0, 2) as i:
                        for n in range(6):
                            ahead(f.s0, n, i)
                            if n % 2:
                                c = n // 2
                                used(act, f.s0, n, i)
                                act.activation(qkv[:, :, bass.ds(512 * c + 1536 * i, 512)], banks_pair[c],
                                               ACT.Copy).then_inc(qkv_evac, 1)
                elif f.kind == "conv_in":
                    for n in range(12):
                        ahead(f.s0, n)
                        g = n // 3
                        if n % 3 == 0:
                            used(act, f.s0, n)
                            act.activation(cT, banks6[n % 3], ACT.Copy).then_inc(conv_c, 1)
                        if n % 3 == 2:
                            act.wait_ge(conv_g, g + 1)
                            act.activation(actB_hi[:, 2 * g:2 * g + 2, :].rearrange("p b n -> p (b n)"), gT,
                                           ACT.Copy).then_inc(conv_hi, 1)
                elif f.kind == "out":
                    for n in range(4):
                        ahead(f.s0, n)
                elif f.kind == "ffn":
                    ffn(f)

        @block.vector
        def _(dve):
            def split_lo(base, k, i, per):
                n0 = base + k
                dve.wait_ge(slab_hi, n0 + 1 + RAW * i + RAW * per)
                dve.tensor_tensor(wlo[:, n0 % SPLIT], raw[:, n0 % RAW], whi[:, n0 % SPLIT].bitcast(F32),
                                  ALU.subtract).then_inc(slab_split, 1)

            def ahead(base, k, i=0, per=0):
                if base + k + 2 < total_slabs:
                    split_lo(base, k + 2, i, per)

            def norm(f):
                m = f.m
                dve.wait_ge(norm_rstd, m + 1)
                for t in range(NT):
                    dve.tensor_scalar(hn[:, t], x[:, t], n_rstd[:, m, t:t + 1], None, ALU.mult).then_inc(norm_tok, 1)
                v, g0 = f.gain
                for b in range(4):
                    dve.wait_ge(tp_hi, f.h0 + b + 1)
                    for j in range(2):
                        r = dve.scalar_tensor_tensor(actA_lo[:, 2 * b + j, :], tp[:, (f.u0 + b) % 2, j * SEQ:(j + 1) * SEQ],
                                                     col(v, g0 + 2 * b + j),
                                                     actA_hi[:, 2 * b + j, :].bitcast(F32), ALU.mult, ALU.subtract)
                    r.then_inc(tp_read, 1)

            def ffn(f):
                C = f.C

                def t_lo(c, i, ex):
                    dve.wait_ge(tp_hi, f.h0 + c + 1 + 2 * i + C * ex)
                    dve.tensor_tensor(hT_lo[:, :], tp[:, (f.u0 + c) % 2], hT_hi[:, :].bitcast(F32),
                                      ALU.subtract).then_inc(tp_read, 1)

                def expert(ex):
                    def at(k, i):
                        kind, c = ffn_kind(k, C)
                        ahead(f.s0, k, i, C // 2 * ex)
                        if kind == "up_b":
                            dve.wait_ge(gu_silu, f.c0 + c + 1 + 2 * i + C * ex)
                            dve.tensor_tensor(h_tok[:, :, :], gu[:, :, FC:2 * FC], silu_g[:, :, :],
                                              ALU.mult).then_inc(gu_read, 1)
                            if c == 0:
                                t_lo(0, 0, ex)
                        elif kind == "down" and c < C - 1:
                            t_lo(c + 1, i, ex)
                        elif kind == "down":
                            used(dve, f.s0, k, i, C // 2 * ex)
                            for t in range(NT):
                                g = f.scale if f.gates is None else f.gates[:, t, bass.ds(ex, 1)]
                                r = dve.scalar_tensor_tensor(x[:, t], acc[:, 2 * t:2 * t + 2, :].rearrange("p b n -> p (b n)"),
                                                             g, x[:, t], ALU.mult, ALU.add)
                            r.then_inc(x_ready, 1)
                    positions(dve, f, at)
                over_experts(dve, f, expert)

            def attention(f):
                q = f.sems
                mem = f.mem
                Dh, s, half, r0 = f.Dh, mem["s"], f.half, f.rope0
                scale = float(Dh) ** -0.5
                if f.n == 1:
                    dve.wait_ge(mla_evac, 7)
                    dve.tensor_copy(mem["qk"][1][:, :, :, QK_NOPE:],
                                    mla_dn[:, :, LATENT:].unsqueeze(2).broadcast_to([P, NT, HEADS, QK_ROPE])).then_inc(q["qk_evac"], 1)
                for w in range(2):
                    dve.wait_ge(q["qk_square"], w + 1)
                    dve.tensor_reduce(qk_ss[:, w, :], s[:, 0:16 * Dh].rearrange("p (g n) -> p g n", n=Dh), AX.X,
                                      ALU.add).then_inc(q["qk_sum"], 1)
                if f.n == 1:
                    dve.wait_ge(gains_loaded, 64)
                    dve.wait_ge(tables_ready, 1)
                cos, sin = [z[:, :, f.angle0:f.angle0 + half].unsqueeze(2).broadcast_to([P, NT, HEADS, half])
                            for z in (rope_cos, rope_sin)]
                n = NT * HEADS * half
                t0, t1, t2 = [s[:, j * n:(j + 1) * n].rearrange("p (t h n) -> p t h n", t=NT, h=HEADS) for j in range(3)]
                for w in range(2):
                    v = mem["qk"][w]
                    dve.wait_ge(q["qk_root"], w + 1)
                    g = gains[:, f.gain0 + w * Dh:f.gain0 + (w + 1) * Dh]
                    for t in range(NT):
                        dve.tensor_tensor(v[:, t], v[:, t], qk_rstd[:, w, t * HEADS:(t + 1) * HEADS].unsqueeze(2).broadcast_to(
                            [P, HEADS, Dh]), ALU.mult)
                    dve.drain()
                    for t in range(NT):
                        dve.tensor_tensor(v[:, t], v[:, t], g.unsqueeze(1).broadcast_to([P, HEADS, Dh]), ALU.mult)
                    dve.drain()
                    x1, x2 = v[:, :, :, r0:r0 + half], v[:, :, :, r0 + half:r0 + 2 * half]
                    dve.tensor_tensor(t0, x1, cos, ALU.mult)
                    dve.tensor_tensor(t1, x1, sin, ALU.mult)
                    dve.tensor_tensor(t2, x2, sin, ALU.mult)
                    dve.drain()
                    dve.tensor_tensor(x1, t0, t2, ALU.subtract)
                    dve.drain()
                    dve.tensor_tensor(t0, x2, cos, ALU.mult)
                    dve.drain()
                    dve.tensor_tensor(x2, t0, t1, ALU.add).then_inc(q["qk_done"], 1)
                dve.drain()
                if f.n == 1:
                    dve.wait_ge(mask_ready, 2)

                def masked(h):
                    dve.wait_ge(q["head_scores"], h + 1)
                    dve.scalar_tensor_tensor(s[:, h * 384:(h + 1) * 384], acc[:, h % 4, 0:384], scale, mask[:, :], ALU.mult,
                                             ALU.add).then_inc(q["head_masked"], 1)
                    dve.drain()
                    for t in range(NT):
                        dve.tensor_reduce(s_max[:, h, t:t + 1], s[:, h * 384 + t * P:h * 384 + (2 * t + 1) * P], AX.X, ALU.max)
                    dve.drain()
                    dve.tensor_scalar(s_neg[:, h, :], s_max[:, h, :], -1.0, None, ALU.mult).then_inc(q["head_max"], 1)

                def normalised(h):
                    dve.wait_ge(q["head_exp"], 2 * (h + 1))
                    dve.reciprocal(s_inv[:, h, :], s_sum[:, h, :])
                    dve.drain()
                    for t in range(NT):
                        v = s[:, h * 384 + t * P:h * 384 + (2 * t + 1) * P]
                        r = dve.tensor_scalar(v, v, s_inv[:, h, t:t + 1], None, ALU.mult)
                    r.then_inc(q["head_p"], 1)

                for h in range(HEADS + 2):
                    if h < HEADS:
                        dve.wait_ge(q["head_T"], h + 1)
                        if h >= 2:
                            dve.wait_ge(q["head_scores"], h - 1)
                        for n, (d0, dn) in enumerate(f.parts):
                            r = dve.tensor_copy(mem["stage"][h % 2][1][0:dn, n * SEQ:(n + 1) * SEQ],
                                                gu[0:dn, 1, n * SEQ:(n + 1) * SEQ])
                        r.then_inc(q["head_k"], 1)
                    if 1 <= h <= HEADS:
                        masked(h - 1)
                    if h >= 2:
                        normalised(h - 2)
                for h in range(HEADS):
                    dve.wait_ge(q["head_ohi"], h + 1)
                    dve.tensor_tensor(actA_lo[:, h, :], acc[:, h % 4, 0:SEQ], actA_hi[:, h, :].bitcast(F32),
                                      ALU.subtract).then_inc(q["head_olo"], 1)

            def router():
                def row(v):
                    return v.unsqueeze(2).broadcast_to([P, NT, EXPERTS])

                dve.wait_ge(router_logits, 1)
                logits = acc[:, 0, 0:NT * EXPERTS].rearrange("p (t e) -> p t e", t=NT)
                shifted, e, p, c1, one1, p2, one2, g = rt
                mx, total, inv, m1, c1m, m2, c2m, den, rden, _ = rt_row
                dve.tensor_reduce(mx, logits, AX.X, ALU.max)
                dve.drain()
                dve.tensor_tensor(shifted, logits, row(mx), ALU.subtract).then_inc(router_shift, 1)
                dve.wait_ge(router_exp, 1)
                dve.tensor_reduce(total, e, AX.X, ALU.add)
                dve.drain()
                dve.reciprocal(inv, total)
                dve.drain()
                dve.tensor_tensor(p, e, row(inv), ALU.mult)
                dve.drain()
                dve.wait_ge(rank_ready, EXPERTS)
                for src, m, cm, one in ((p, m1, c1m, one1), (p2, m2, c2m, one2)):
                    dve.tensor_reduce(m, src, AX.X, ALU.max)
                    dve.drain()
                    dve.tensor_tensor(c1, src, row(m), ALU.is_equal)
                    dve.drain()
                    dve.tensor_tensor(c1, c1, rank8, ALU.mult)
                    dve.drain()
                    dve.tensor_reduce(cm, c1, AX.X, ALU.max)
                    dve.drain()
                    dve.tensor_tensor(one, c1, row(cm), ALU.is_equal)
                    dve.drain()
                    if src is p:
                        dve.scalar_tensor_tensor(p2, one, -2.0, p, ALU.mult, ALU.add)
                        dve.drain()
                dve.tensor_tensor(den, m1, m2, ALU.add)
                dve.tensor_tensor(g, one1, row(m1), ALU.mult)
                dve.tensor_tensor(one2, one2, row(m2), ALU.mult)
                dve.drain()
                dve.reciprocal(rden, den)
                dve.tensor_tensor(g, g, one2, ALU.add)
                dve.drain()
                dve.tensor_tensor(gates[:, :, :], g, row(rden), ALU.mult)
                dve.drain()

            def step_sizes(f):
                used(dve, f.s0, 0)
                dve.wait_ge(ssm_rows, 48)
                v = dt_in.rearrange("p (t h) -> p t h", t=NT)
                dve.tensor_tensor(v, gu[:, :, 0:SSM_HEADS], bias_bc.unsqueeze(1).broadcast_to([P, NT, SSM_HEADS]), ALU.add)
                dve.drain()
                dve.tensor_scalar(dt_abs, dt_in, -1.0, None, ALU.mult)
                dve.drain()
                dve.tensor_tensor(dt_abs, dt_abs, dt_in, ALU.max).then_inc(dt_ready, 1)
                dve.wait_ge(dt_e, 1)
                dve.tensor_scalar(dt_z2, dt_exp, 2.0, None, ALU.add)
                dve.drain()
                dve.reciprocal(dt_z2, dt_z2)
                dve.drain()
                dve.tensor_tensor(dt_z, dt_exp, dt_z2, ALU.mult)
                dve.drain()
                dve.tensor_tensor(dt_z2, dt_z, dt_z, ALU.mult)
                dve.drain()
                dve.tensor_scalar(dt_poly, dt_z2, 2.0 / 19, 2.0 / 17, ALU.mult, ALU.add)
                for k in range(15, 0, -2):
                    dve.drain()
                    dve.tensor_tensor(dt_poly, dt_poly, dt_z2, ALU.mult)
                    dve.drain()
                    dve.tensor_scalar(dt_poly, dt_poly, 2.0 / k, None, ALU.add)
                dve.drain()
                dve.tensor_tensor(dt_poly, dt_poly, dt_z, ALU.mult)
                dve.tensor_scalar(dt_in, dt_in, 0.0, None, ALU.max)
                dve.drain()
                dve.tensor_tensor(dt_tok, dt_in, dt_poly, ALU.add)
                dve.wait_ge(a_rate, 1)
                dve.tensor_scalar(decay_rate, decay_rate, -1.0, None, ALU.mult)
                dve.drain()
                for n in range(2):
                    dve.memset(pad_x[n][:, :, 0:TAPS - 1], 0.0)
                dve.tensor_tensor(a_tok.rearrange("p (t h) -> p t h", t=NT), dt_tok.rearrange("p (t h) -> p t h", t=NT),
                                  decay_rate.unsqueeze(1).broadcast_to([P, NT, SSM_HEADS]), ALU.mult).then_inc(a_ready, 1)

            def ssm_in(f):
                def x_tokens(p):
                    dve.wait_ge(tp_full, f.u0 + p + 1)
                    dve.tensor_copy(ssm_x[:, :, 256 * p:256 * (p + 1)], tp[:, (f.u0 + p) % 2].rearrange("p (t n) -> p t n", t=NT)
                                    ).then_inc(tp_read, 1)

                for n in range(25):
                    ahead(f.s0, n)
                    if n == 0:
                        step_sizes(f)
                    elif n <= 16:
                        p = n - 1
                        dve.wait_ge(sx_copy, p + 1)
                        if p >= 2:
                            dve.wait_ge(sx_silu, p - 1)
                        for j in range(TAPS):
                            if j:
                                dve.drain()
                            for b in range(2):
                                o = cv_x[p % 2][:, b * SEQ:(b + 1) * SEQ]
                                src = pad_x[p % 2][:, b, j:j + SEQ]
                                w = col(V_SCONV, 32 * j + 2 * p + b)
                                if j == 0:
                                    r = dve.tensor_scalar(o, src, w, None, ALU.mult)
                                else:
                                    r = dve.scalar_tensor_tensor(o, src, w, o, ALU.mult, ALU.add)
                        r.then_inc(sx_conv, 1)
                        if 2 <= p < 10:
                            x_tokens(p - 2)
                        if n == 6:
                            dve.wait_ge(cum_full, 1)
                            dve.tensor_scalar(neg_cum, gu[:, 1, 0:64], -1.0, None, ALU.mult)
                            dve.tensor_copy(exp_cum1, gu[:, 1, 32:64])
                            dve.drain()
                            dve.tensor_tensor(decay0, gu[:, 1, 64:96], neg_cum[:, 0:32], ALU.add).then_inc(cum_neg, 2)

            def ssd(f):
                heads = "p (h n) -> p h n"

                def per_head(v):
                    return v.unsqueeze(2).broadcast_to([P, PER_GROUP, SSM_HEAD])

                def combine(n):
                    g, t = n // 2, n % 2
                    gs = slice(256 * g, 256 * (g + 1))
                    hs = slice(PER_GROUP * g, PER_GROUP * (g + 1))
                    xs = ssm_x[:, t, gs]
                    dve.tensor_tensor(xs.rearrange(heads, h=PER_GROUP), xs.rearrange(heads, h=PER_GROUP), per_head(skip_bc[:, hs]),
                                      ALU.mult)
                    dve.wait_ge(sd_y, n + 1)
                    dve.drain()
                    dve.tensor_tensor(xs, xs, acc[:, 2 + n % 2, 0:256], ALU.add)
                    if t:
                        dve.tensor_tensor(y_off.rearrange(heads, h=PER_GROUP),
                                          acc[:, 2 + n % 2, 256:512].rearrange(heads, h=PER_GROUP), per_head(exp_cum1[:, hs]),
                                          ALU.mult)
                        dve.drain()
                        dve.tensor_tensor(xs, xs, y_off, ALU.add)
                    dve.drain()
                    dve.tensor_tensor(xs, xs, ssm_z[:, t, gs], ALU.mult).then_inc(sd_read, 1)

                dve.wait_ge(sz_silu, 4)
                dve.wait_ge(cum_exp, 1)
                for n in range(16):
                    g, t = n // 2, n % 2
                    hs = slice(SSM_HEADS * t + PER_GROUP * g, SSM_HEADS * t + PER_GROUP * (g + 1))
                    if n >= 2:
                        dve.wait_ge(sd_y, n - 1)
                    r = dve.tensor_tensor(xdt_buf[n % 2].rearrange(heads, h=PER_GROUP),
                                          ssm_x[:, t, 256 * g:256 * (g + 1)].rearrange(heads, h=PER_GROUP), per_head(dt_tok[:, hs]),
                                          ALU.mult)
                    if t == 0:
                        dve.drain()
                        r = dve.tensor_tensor(xdecay.rearrange(heads, h=PER_GROUP), xdt_buf[n % 2].rearrange(heads, h=PER_GROUP),
                                              per_head(decay0[:, hs]), ALU.mult)
                    r.then_inc(sd_x, 1)
                    dve.wait_ge(sd_cbe, n + 1)
                    dve.wait_ge(sd_exp, n + 1)
                    m = m_buf[n % 2].rearrange(heads, h=PER_GROUP)
                    dve.tensor_tensor(m, m, cb_buf[n % 2].unsqueeze(1).broadcast_to([P, PER_GROUP, P]), ALU.mult).then_inc(sd_m, 1)
                    if n:
                        combine(n - 1)
                combine(15)

            def ssm_out(f):
                dve.wait_ge(sd_root, 1)
                for b in range(8):
                    for t in range(NT):
                        v = ssm_x[:, t, 256 * b:256 * (b + 1)]
                        r = dve.tensor_scalar(v, v, qk_rstd[:, 0, 8 * t + b:8 * t + b + 1], None, ALU.mult)
                    r.then_inc(sd_tok, 1)
                for b in range(8):
                    dve.wait_ge(tp_hi, f.h0 + b + 1)
                    hi_t, lo_t = A if b < 4 else B
                    for j in range(2):
                        kt = (2 * b + j) % KT
                        r = dve.scalar_tensor_tensor(lo_t[:, kt, :], tp[:, (f.u0 + b) % 2, j * SEQ:(j + 1) * SEQ],
                                                     col(V_SNORM, 2 * b + j), hi_t[:, kt, :].bitcast(F32), ALU.mult, ALU.subtract)
                    r.then_inc(tp_read, 1)
                for n in range(8):
                    ahead(f.s0, n)
                    if n % 4 == 3:
                        c = n // 4
                        used(dve, f.s0, n)
                        for t in range(NT):
                            xs = x[:, t, c * 512:(c + 1) * 512]
                            r = dve.tensor_tensor(xs, acc[:, 2 * c + t], xs, ALU.add)
                        r.then_inc(x_ready, 1)

            def tables():
                dve.wait_ge(pos_loaded, 48)
                dve.tensor_copy(pos_f[:, :, :], pos_int[:, :, :])
                dve.drain()
                a0, a1, turns = ang[:, 0], ang[:, 1], ang[:, 2]
                for w, (c0, c1) in enumerate(((0, 32), (32, 96))):
                    for t in range(NT):
                        dve.tensor_scalar(a0[:, t * 96 + c0:t * 96 + c1], inv_freq[:, c0:c1], pos_f[:, w, t:t + 1], None, ALU.mult)
                dve.drain()
                dve.tensor_scalar(turns, a0, 1.0 / (2 * np.pi), 12582912.0, ALU.mult, ALU.add)
                dve.drain()
                dve.tensor_scalar(turns, turns, 12582912.0, None, ALU.subtract)
                rest = 2 * np.pi
                for bits in (8, 11, 24):
                    exponent = np.floor(np.log2(rest))
                    part = float(np.float32(np.floor(rest / 2.0 ** (exponent - bits)) * 2.0 ** (exponent - bits)))
                    rest -= part
                    dve.drain()
                    dve.scalar_tensor_tensor(a0, turns, -part, a0, ALU.mult, ALU.add)
                dve.drain()
                dve.tensor_scalar(a0, a0, 3.1415925, -3.1415925, ALU.min, ALU.max)
                dve.drain()
                dve.tensor_scalar(a1, a0, -1.0, None, ALU.mult)
                dve.drain()
                dve.tensor_tensor(a1, a1, a0, ALU.min)
                dve.drain()
                dve.tensor_scalar(a1, a1, float(np.pi / 2), None, ALU.add).then_inc(angles, 1)

            dve.memset(vT[:, :, 0:2], 0.0).then_inc(slab_split, RAW)
            tables()
            dve.wait_ge(router_split, 1)
            dve.tensor_tensor(router_lo[:, :], router_w[:, :], router_hi[:, :].bitcast(F32), ALU.subtract).then_inc(router_done, 1)
            dve.wait_ge(vecs_full, 1)
            dve.tensor_copy(vecs[:, :, :].rearrange("p a b -> p (a b)"), gu[:, 1, 0:3 * P]).then_inc(vecs_ready, 1)
            ahead(0, -2)
            ahead(0, -1)
            for f in stages_used:
                if f.kind == "norm":
                    norm(f)
                elif f.kind == "attention":
                    attention(f)
                elif f.kind == "router":
                    router()
                elif f.kind == "ssm_in":
                    ssm_in(f)
                elif f.kind == "ssd":
                    ssd(f)
                elif f.kind == "ssm_out":
                    ssm_out(f)
                elif f.kind == "mla_down":
                    for n in range(4):
                        ahead(f.s0, n)
                    dve.wait_ge(lat_sum, 4)
                    for w, (c0, n) in enumerate(((0, Q_RANK), (Q_RANK, KV_RANK))):
                        dve.wait_ge(lat_root, w + 1)
                        for t in range(NT):
                            dve.tensor_scalar(mla_cn[:, t, c0:c0 + n], mla_dn[:, t, c0:c0 + n], lat_rstd[:, w, t:t + 1], None,
                                              ALU.mult).then_inc(lat_tok, 1)
                    for b in range(3):
                        dve.wait_ge(tp_hi, f.h0 + b + 1)
                        for kt in range(2 * b, min(2 * b + 2, 5)):
                            v = col(V_QA, kt) if kt < 3 else col(V_KVA, kt - 3)
                            r = dve.scalar_tensor_tensor(actB_lo[:, kt, :], tp[:, (f.u0 + b) % 2, (kt % 2) * SEQ:(kt % 2 + 1) * SEQ],
                                                         v, actB_hi[:, kt, :].bitcast(F32), ALU.mult, ALU.subtract)
                        r.then_inc(tp_read, 1)
                elif f.kind == "mla_up":
                    for n in range(7):
                        ahead(f.s0, n)
                elif f.kind == "qkv":
                    with dve.Fori(0, 2) as i:
                        for n in range(6):
                            ahead(f.s0, n, i)
                elif f.kind == "conv_in":
                    for n in range(12):
                        ahead(f.s0, n)
                        g = n // 3
                        bank = banks6[n % 3].rearrange("p (b n) -> p b n", b=2)
                        if n % 3 == 1:
                            dve.wait_ge(conv_c, g + 1)
                            used(dve, f.s0, n)
                            dve.tensor_tensor(vT[:, :, 2:], bank, cT.rearrange("p (b n) -> p b n", b=2),
                                              ALU.mult).then_inc(conv_read, 1)
                            for b in range(2):
                                kt = 2 * g + b
                                cv = convT[:, b * SEQ:(b + 1) * SEQ]
                                dve.drain()
                                dve.tensor_scalar(cv, vT[:, b, 0:SEQ], col(V_CONV, kt), None, ALU.mult)
                                for j in (1, 2):
                                    dve.drain()
                                    dve.scalar_tensor_tensor(cv, vT[:, b, j:j + SEQ], col(V_CONV, j * KT + kt), cv,
                                                             ALU.mult, ALU.add)
                        if n % 3 == 2:
                            used(dve, f.s0, n)
                            dve.drain()
                            if g:
                                dve.wait_ge(conv_hi, g)
                            dve.tensor_tensor(gT, banks6[n % 3], convT, ALU.mult).then_inc(conv_g, 1)
                            dve.wait_ge(conv_hi, g + 1)
                            dve.tensor_tensor(actB_lo[:, 2 * g:2 * g + 2, :].rearrange("p b n -> p (b n)"), gT,
                                              actB_hi[:, 2 * g:2 * g + 2, :].rearrange("p b n -> p (b n)").bitcast(F32),
                                              ALU.subtract).then_inc(conv_lo, 1)
                elif f.kind == "out":
                    for n in range(4):
                        ahead(f.s0, n)
                        if n % 2:
                            c = n // 2
                            used(dve, f.s0, n)
                            for t in range(NT):
                                xs = x[:, t, c * 512:(c + 1) * 512]
                                r = dve.tensor_tensor(xs, acc[:, 2 * c + t], xs, ALU.add)
                            r.then_inc(x_ready, 1)
                elif f.kind == "ffn":
                    ffn(f)

        @block.tensor
        def _(pe):
            def wait_slab(base, k, i=0, per=0):
                pe.wait_ge(slab_split, base + k + 1 + RAW + RAW * i + RAW * per)

            def three(o, xh, xl, wh, wl, start, stop):
                pe.matmul(o, xh, wh, start=start, stop=False)
                pe.matmul(o, xh, wl, start=False, stop=False)
                return pe.matmul(o, xl, wh, start=False, stop=stop)

            def norm(f):
                pe.wait_ge(norm_tok, 2 * (f.m + 1))
                for b in range(4):
                    u = f.u0 + b
                    if u >= 2:
                        pe.wait_ge(tp_read, u - 1)
                    for j in range(2):
                        for t in range(NT):
                            r = pe.transpose(tp[:, u % 2, (2 * j + t) * P:(2 * j + t + 1) * P],
                                             hn[:, t, (2 * b + j) * P:(2 * b + j + 1) * P], ident[:, :])
                    r.then_inc(tp_full, 1)

            def rows_slab(f, n, aT_hi, aT_lo, kts, width, banks, start, stop):
                sl = (f.s0 + n) % SPLIT
                w = [z[:, sl, 0:len(kts) * width].rearrange("p (k n) -> p k n", n=width) for z in (whi, wlo)]
                for j, kt in enumerate(kts):
                    for t in range(NT):
                        ts = slice(t * P, (t + 1) * P)
                        r = three(banks[t][:, 0:width], aT_hi[:, kt, ts], aT_lo[:, kt, ts], w[0][:, j], w[1][:, j],
                                  start and j == 0, stop and j == len(kts) - 1)
                return r.then_inc(slab_used, 1)

            def cols_slab(f, n, bank, aT_hi, aT_lo):
                sl = (f.s0 + n) % SPLIT
                w = [z[:, sl].rearrange("p (k n) -> p k n", n=2 * P) for z in (whi, wlo)]
                for b in range(2):
                    bs = slice(b * P, (b + 1) * P)
                    for kt in range(KT):
                        o = bank[:, b * SEQ:(b + 1) * SEQ]
                        pe.matmul(o, w[0][:, kt, bs], aT_hi[:, kt], start=kt == 0, stop=False)
                        pe.matmul(o, w[0][:, kt, bs], aT_lo[:, kt], start=False, stop=False)
                        r = pe.matmul(o, w[1][:, kt, bs], aT_hi[:, kt], start=False, stop=kt == KT - 1)
                return r.then_inc(slab_used, 1)

            def ffn(f):
                C = f.C
                ups = f.c0, f.u0

                def transposes(c, i, ex):
                    pe.wait_ge(gu_read, f.c0 + c + 1 + 2 * i + C * ex)
                    pe.wait_ge(tp_read, f.u0 + c - 1 + 2 * i + C * ex)
                    for j in range(2):
                        for t in range(NT):
                            r = pe.transpose(tp[:, (f.u0 + c) % 2, (2 * j + t) * P:(2 * j + t + 1) * P],
                                             h_tok[:, t, j * P:(j + 1) * P], ident[:, :])
                    r.then_inc(tp_full, 1)

                def expert(ex):
                    def at(k, i):
                        kind, c = ffn_kind(k, C)
                        per = C // 2 * ex
                        wait_slab(f.s0, k, i, per)
                        sl = (f.s0 + k) % SPLIT
                        if kind == "down":
                            pe.wait_ge(tp_read, f.u0 + c + 1 + 2 * i + C * ex)
                            w = [z[:, sl].rearrange("p (j n) -> p j n", j=2) for z in (whi, wlo)]
                            last = c == C - 1
                            for j in range(2):
                                for t in range(NT):
                                    cs = slice((2 * j + t) * P, (2 * j + t + 1) * P)
                                    for n in range(2):
                                        ns = slice(n * 512, (n + 1) * 512)
                                        r = three(acc[:, 2 * t + n], hT_hi[:, cs], hT_lo[:, cs],
                                                  w[0][:, j, ns], w[1][:, j, ns], False, last and j == 1)
                            r.then_inc(slab_used, 1)
                            if not last:
                                transposes(c + 1, i, ex)
                            return
                        w = [z[:, sl].rearrange("p (k n) -> p k n", k=4) for z in (whi, wlo)]
                        k0 = 0 if kind == "up_a" else 4
                        if kind == "up_a":
                            if k == 0:
                                pe.wait_ge(tp_read, f.u0)
                            if f.c0 + c > 0:
                                pe.wait_ge(gu_read, f.c0 + c + 2 * i + C * ex)
                        for kt in range(4):
                            for t in range(NT):
                                ts = slice(t * P, (t + 1) * P)
                                r = three(gu[:, t], actA_hi[:, k0 + kt, ts], actA_lo[:, k0 + kt, ts], w[0][:, kt], w[1][:, kt],
                                          kind == "up_a" and kt == 0, kind == "up_b" and kt == 3)
                        r.then_inc(slab_used, 1)
                        if kind == "up_b" and c == 0 and k < 2:
                            pe.wait_ge(x_ready, f.x0 + ex)
                            if f.gates is not None:
                                pe.wait_ge(router_shift, 1)
                            for b in range(4):
                                pe.matmul(acc[:, b].rearrange("p (a n) -> p a n", a=4), zero_r[:, :],
                                          zero_r[:, :].unsqueeze(1).broadcast_to([P, 4, P]), start=True, stop=False)
                            transposes(0, 0, ex)
                    positions(pe, f, at)
                over_experts(pe, f, expert)

            def attention(f):
                q = f.sems
                mem = f.mem
                pe.wait_ge(q["qk_done"], 2)

                def to_staging(h):
                    for w in range(2):
                        if h:
                            pe.wait_ge((q["head_q"], q["head_k"])[w], h)
                        for n, (d0, dn) in enumerate(f.parts):
                            for t in range(NT):
                                r = pe.transpose(gu[0:dn, w, n * SEQ + t * P:n * SEQ + (t + 1) * P],
                                                 mem["qk"][w][:, t, h, d0:d0 + dn], ident[:, :])
                    r.then_inc(q["head_T"], 1)

                def scores(h):
                    pe.wait_ge(q["head_q"], h + 1)
                    pe.wait_ge(q["head_k"], h + 1)
                    if h >= 4:
                        pe.wait_ge(q["head_masked"], h - 3)
                    qT, kT = mem["stage"][h % 2]
                    for t in range(NT):
                        for n, (d0, dn) in enumerate(f.parts):
                            r = pe.matmul(acc[:, h % 4, t * P:(2 * t + 1) * P],
                                          qT[0:dn, n * SEQ + t * P:n * SEQ + (t + 1) * P], kT[0:dn, n * SEQ:n * SEQ + (t + 1) * P],
                                          start=n == 0, stop=n == len(f.parts) - 1)
                    r.then_inc(q["head_scores"], 1)

                def probs(h):
                    pe.wait_ge(q["head_p"], h + 1)
                    if h >= 2:
                        pe.wait_ge(q["head_pcopy"], h - 1)
                    for b in range(3):
                        r = pe.transpose(gu[:, h % 2, b * P:(b + 1) * P],
                                         mem["s"][:, h * 384 + b * P:h * 384 + (b + 1) * P], ident[:, :])
                    r.then_inc(q["head_pT"], 1)

                def values(h):
                    pe.wait_ge(q["head_pcopy"], h + 1)
                    if h >= 4:
                        pe.wait_ge(q["head_olo"], h - 3)
                    pT = mem["pT"][:, h * 384:(h + 1) * 384]
                    hs = slice(h * HEAD, (h + 1) * HEAD)
                    pe.matmul(acc[:, h % 4, 0:SEQ], mem["v"][:, 0, hs], pT[:, 0:SEQ], start=True, stop=False)
                    pe.matmul(acc[:, h % 4, P:SEQ], mem["v"][:, 1, hs], pT[:, SEQ:], start=False,
                              stop=True).then_inc(q["head_o"], 1)

                to_staging(0)
                for h in range(HEADS):
                    if h + 1 < HEADS:
                        to_staging(h + 1)
                    scores(h)
                probs(0)
                for h in range(HEADS):
                    if h + 1 < HEADS:
                        probs(h + 1)
                    values(h)

            def router(f):
                pe.wait_ge(router_done, 1)
                pe.wait_ge(tp_read, f.u0)
                for t in range(NT):
                    ts = slice(t * P, (t + 1) * P)
                    for kt in range(KT):
                        es = slice(kt * EXPERTS, (kt + 1) * EXPERTS)
                        r = three(acc[:, 0, t * EXPERTS:(t + 1) * EXPERTS], actA_hi[:, kt, ts], actA_lo[:, kt, ts], router_hi[:, es],
                                  router_lo[:, es], kt == 0, kt == KT - 1)
                r.then_inc(router_logits, 1)

            def ssm_in(f):
                pe.wait_ge(tp_read, f.u0)

                def x_tokens(p):
                    pe.wait_ge(sx_silu, p + 1)
                    pe.wait_ge(tp_read, f.u0 + p - 1)
                    for t in range(NT):
                        for b in range(2):
                            r = pe.transpose(tp[:, (f.u0 + p) % 2, (2 * t + b) * P:(2 * t + b + 1) * P],
                                             si_x[p % 2][:, b * SEQ + t * P:b * SEQ + (t + 1) * P], ident[:, :])
                    r.then_inc(tp_full, 1)

                for n in range(25):
                    wait_slab(f.s0, n)
                    if n == 0:
                        rows_slab(f, n, *A, list(range(8)), SSM_HEADS, banks_pair_of(2), True, True)
                    elif n <= 16:
                        p = n - 1
                        if p >= 3:
                            pe.wait_ge(sx_copy, p - 2)
                        cols_slab(f, n, banks6[p % 3], *A)
                        if 2 <= p < 10:
                            x_tokens(p - 2)
                        if n == 3:
                            pe.wait_ge(a_ready, 1)
                            pe.wait_ge(ssm_const, 1)
                            for t in range(NT):
                                pe.matmul(gu[:, 1, 32 * t:32 * (t + 1)], tri, a_tok[:, 32 * t:32 * (t + 1)], start=True, stop=True)
                            pe.matmul(gu[:, 1, 64:96], ones, a_tok[:, 0:32], start=True, stop=True).then_inc(cum_full, 1)
                    else:
                        c = (n - 17) // 2
                        if n == 17:
                            pe.wait_ge(sx_copy, 16)
                        if c >= 2 and n % 2:
                            pe.wait_ge(sz_silu, c - 1)
                        k4 = 4 * ((n - 17) % 2)
                        rows_slab(f, n, *A, list(range(k4, k4 + 4)), 512, banks_pair_of(c % 2), k4 == 0, k4 == 4)

            def ssd(f):
                def first(n):
                    g, t = n // 2, n % 2
                    ts = slice(t * P, (t + 1) * P)
                    if n:
                        pe.wait_ge(sd_cbe, n)
                    r = pe.matmul(gu[:, 0, 0:P], ssm_bc[:, g, ts], ssm_bc[:, 8 + g, ts], start=True, stop=True)
                    if t == 0:
                        r = pe.transpose(gu[:, 0, P:2 * P], ssm_bc[:, g, ts], ident[:, :])
                    r.then_inc(sd_cb, 1)
                    if n >= 2:
                        pe.wait_ge(sd_exp, n - 1)
                    for r in range(PER_GROUP):
                        h = SSM_HEADS * t + PER_GROUP * g + r
                        o = acc[:, n % 2, r * P:(r + 1) * P]
                        pe.matmul(o, a_tok[:, h:h + 1].broadcast_to([P, P]), tri, start=True, stop=False)
                        i = pe.matmul(o, ident_r[:, :], later_r[:, :], start=False, stop=True)
                    i.then_inc(sd_seg, 1)

                def second(n):
                    g, t = n // 2, n % 2
                    pe.wait_ge(sd_x, n + 1)
                    pe.wait_ge(sd_m, n + 1)
                    if n >= 2:
                        pe.wait_ge(sd_read, n - 1)
                    for r in range(PER_GROUP):
                        hs = slice(r * SSM_HEAD, (r + 1) * SSM_HEAD)
                        i = pe.matmul(acc[:, 2 + n % 2, hs], m_buf[n % 2][:, r * P:(r + 1) * P], xdt_buf[n % 2][:, hs],
                                      start=True, stop=True)
                    if t == 0:
                        i = pe.matmul(gu[:, 1, 0:256], b_tok, xdecay, start=True, stop=True)
                    else:
                        pe.wait_ge(sd_st, g + 1)
                        i = pe.matmul(acc[:, 2 + n % 2, 256:512], ssm_bc[:, 8 + g, P:2 * P], state, start=True, stop=True)
                    i.then_inc(sd_y, 1)

                pe.wait_ge(sz_silu, 4)
                for n in range(17):
                    if n < 16:
                        first(n)
                    if n:
                        second(n - 1)

            def ssm_out(f):
                for b in range(8):
                    u = f.u0 + b
                    pe.wait_ge(sd_tok, b + 1)
                    pe.wait_ge(tp_read, u - 1)
                    for j in range(2):
                        for t in range(NT):
                            r = pe.transpose(tp[:, u % 2, (2 * j + t) * P:(2 * j + t + 1) * P],
                                             ssm_x[:, t, (2 * b + j) * P:(2 * b + j + 1) * P], ident[:, :])
                    r.then_inc(tp_full, 1)
                pe.wait_ge(tp_read, f.u0 + 8)
                for n in range(8):
                    wait_slab(f.s0, n)
                    c, q4 = n // 4, n % 4
                    rows_slab(f, n, *(A if q4 < 2 else B), list(range(4 * (q4 % 2), 4 * (q4 % 2) + 4)), 512, banks_pair_of(c),
                              q4 == 0, q4 == 3)

            pe.sem_inc(slab_used, SPLIT)
            pe.wait_ge(masks_ready, 2)
            pe.wait_ge(rows_loaded, 16 * len(row_loads))
            for t in range(3):
                r = pe.transpose(gu[:, 1, t * P:(t + 1) * P], vec_rows[:, t, :], ident[:, :])
            r.then_inc(vecs_full, 1)
            pe.wait_ge(vecs_ready, 1)
            for f in stages_used:
                if f.kind == "norm":
                    norm(f)
                elif f.kind == "conv_in":
                    pe.wait_ge(tp_read, f.u0)
                    for n in range(12):
                        wait_slab(f.s0, n)
                        if n >= 3:
                            g = n // 3
                            if n % 3 == 0:
                                pe.wait_ge(conv_c, g)
                            elif n % 3 == 1:
                                pe.wait_ge(conv_read, g)
                            else:
                                pe.wait_ge(conv_g, g)
                        cols_slab(f, n, banks6[n % 3], actA_hi, actA_lo)
                elif f.kind == "out":
                    pe.wait_ge(*f.ready)
                    for n in range(4):
                        wait_slab(f.s0, n)
                        c = n // 2
                        rows_slab(f, n, *f.act, list(range(4 * (n % 2), 4 * (n % 2) + 4)), 512,
                                  [acc[:, 2 * c], acc[:, 2 * c + 1]], n % 2 == 0, n % 2 == 1)
                elif f.kind == "attention":
                    attention(f)
                elif f.kind == "router":
                    router(f)
                elif f.kind == "ssm_in":
                    ssm_in(f)
                elif f.kind == "ssd":
                    ssd(f)
                elif f.kind == "ssm_out":
                    ssm_out(f)
                elif f.kind == "mla_down":
                    pe.wait_ge(tp_read, f.u0)
                    for n in range(4):
                        wait_slab(f.s0, n)
                        c = n // 2
                        rows_slab(f, n, *A, list(range(4 * (n % 2), 4 * (n % 2) + 4)), 352,
                                  [acc[:, 2 * c], acc[:, 2 * c + 1]], n % 2 == 0, n % 2 == 1)
                    pe.wait_ge(lat_tok, 4)
                    for b in range(3):
                        u = f.u0 + b
                        pe.wait_ge(tp_read, u - 1)
                        for kt in range(2 * b, min(2 * b + 2, 5)):
                            for t in range(NT):
                                r = pe.transpose(tp[:, u % 2, (2 * (kt % 2) + t) * P:(2 * (kt % 2) + t + 1) * P],
                                                 mla_cn[:, t, kt * P:(kt + 1) * P], ident[:, :])
                        r.then_inc(tp_full, 1)
                elif f.kind == "mla_up":
                    pe.wait_ge(tp_read, f.u0)
                    for n in range(7):
                        wait_slab(f.s0, n)
                        if n >= 2:
                            pe.wait_ge(mla_evac, n - 1)
                        rows_slab(f, n, *B, [0, 1, 2] if n < 3 else [3, 4], 512, banks_pair_of(n % 2), True, True)
                elif f.kind == "qkv":
                    pe.wait_ge(tp_read, f.u0)
                    with pe.Fori(0, 2) as i:
                        for n in range(6):
                            wait_slab(f.s0, n, i)
                            c = n // 2
                            if n % 2 == 0:
                                pe.wait_ge(qkv_evac, c + 1 + 3 * i)
                            rows_slab(f, n, *A, list(range(4 * (n % 2), 4 * (n % 2) + 4)), 512, banks_pair_of(c),
                                      n % 2 == 0, n % 2 == 1)
                elif f.kind == "ffn":
                    ffn(f)


def constants():
    f = [np.float32(THETA) ** (-np.arange(0, QK_ROPE, 2, dtype=np.float32) / np.float32(QK_ROPE)),
         np.float32(THETA) ** (-np.arange(HEAD // 2, dtype=np.float32) / np.float32(HEAD // 2))]
    return {"inv_freq": np.concatenate(f).astype(np.float32)[None]}


_OUT = ((1, SEQ, D), "float32")


def kernel(**inputs):
    import concourse.bacc as bacc
    from concourse.bass_utils import run_bass_kernel_spmd

    nc = bacc.Bacc("TRN2", target_bir_lowering=False, num_devices=1)
    arrays, args = {}, {}
    for name, value in {**inputs, **constants()}.items():
        v = np.ascontiguousarray(value)
        arrays[f"in_{name}"] = v
        args[name] = nc.dram_tensor(f"in_{name}", v.shape, mybir.dt.from_np(v.dtype), kind="ExternalInput").ap()
    args["x"] = args["x"].rearrange("b s d -> (b s) d")
    out = nc.dram_tensor("out", _OUT[0], F32, kind="ExternalOutput").ap()
    program(nc, args, out.rearrange("b s d -> (b s) d"))
    r = run_bass_kernel_spmd(nc, [arrays], core_ids=[0])
    return r.results[0]["out"]
```

```python
import numpy as np
import concourse.bass as bass
from concourse import mybir
from concourse.alu_op_type import AluOpType as ALU
from contextlib import ExitStack

F32 = mybir.dt.float32
F32R = mybir.dt.float32r
I32 = mybir.dt.int32
ACT = mybir.ActivationFunctionType
AX = mybir.AxisListType

P = 128
SEQ = 256
NT = SEQ // P
D = 1024
KT = D // P
RAW = 6
SPLIT = 3
SLAB = 2048
EPS = 1e-6
F_EXPERT = 2048
EXPERTS = 8
FC = 256
HEADS = 8
QK_NOPE, QK_ROPE = 128, 64
Q_RANK, KV_RANK = 384, 256
LATENT = Q_RANK + KV_RANK
DOWN = LATENT + QK_ROPE
HEAD = 128
THETA = 10000.0
D_INNER = 2048
SSM_HEADS = 32
SSM_HEAD = 64
GROUPS = 8
PER_GROUP = SSM_HEADS // GROUPS
TAPS = 4
OPERAND_AT = 15
START, STOP = 0, 99


def program(nc, a, out):
    ctx = ExitStack()
    with ctx:
        def sb(name, shape, dt=F32):
            return ctx.enter_context(nc.sbuf_tensor(name, shape, dt))

        def sem(name):
            return ctx.enter_context(nc.semaphore(name))

        raw = sb("raw", [P, RAW, SLAB])
        whi = sb("whi", [P, SPLIT, SLAB], F32R)
        wlo = sb("wlo", [P, SPLIT, SLAB], F32R)
        raw_full = [sem(f"raw_full{n}") for n in range(RAW)]
        slab_hi = sem("slab_hi")
        slab_split = sem("slab_split")
        slab_used = sem("slab_used")

        x = sb("x", [P, NT, D])
        actA_hi = sb("actA_hi", [P, KT, SEQ], F32R)
        actA_lo = sb("actA_lo", [P, KT, SEQ], F32R)
        actB_hi = sb("actB_hi", [P, KT, SEQ], F32R)
        actB_lo = sb("actB_lo", [P, KT, SEQ], F32R)
        hT_hi = sb("hT_hi", [P, 2 * SEQ], F32R)
        hT_lo = sb("hT_lo", [P, 2 * SEQ], F32R)
        h_tok = sb("h_tok", [P, NT, FC])
        silu_g = sb("silu_g", [P, NT, FC])
        big = sb("big", [P, 12800])
        ident = sb("ident", [P, P])
        zero_r = sb("zero_r", [P, P], F32R)
        vecs = sb("vecs", [P, 3, P])
        n_sum = sb("n_sum", [P, 10, NT])
        n_ms = sb("n_ms", [P, 10, NT])
        n_rstd = sb("n_rstd", [P, 10, NT])
        n_half = sb("n_half", [P, 64])
        aux = sb("aux", [P, 1408])
        gains = aux[:, 0:640]
        rope_cos = aux[:, 640:832].rearrange("p (t n) -> p t n", t=NT)
        rope_sin = aux[:, 832:1024].rearrange("p (t n) -> p t n", t=NT)
        mask = aux[:, 1024:1408]
        aux2 = sb("aux2", [P, 512])
        ident_r = sb("ident_r", [P, P], F32R)
        later_r = sb("later_r", [P, P], F32R)
        router_w = aux2[:, 256:256 + KT * EXPERTS]
        router_hi = sb("router_hi", [P, KT * EXPERTS], F32R)
        router_lo = sb("router_lo", [P, KT * EXPERTS], F32R)
        gates = sb("gates", [P, NT, EXPERTS])
        qk_ss = sb("qk_ss", [P, 2, 16])
        qk_rstd = sb("qk_rstd", [P, 2, 16])
        lat_ss = sb("lat_ss", [P, 2, NT])
        lat_rstd = sb("lat_rstd", [P, 2, NT])
        s_max = sb("s_max", [P, HEADS, NT])
        s_neg = sb("s_neg", [P, HEADS, NT])
        s_sum = sb("s_sum", [P, HEADS, NT])
        s_inv = sb("s_inv", [P, HEADS, NT])

        acc = ctx.enter_context(nc.psum_tensor("acc", [P, 4, 512], F32))
        gu = ctx.enter_context(nc.psum_tensor("gu", [P, 2, 512], F32))
        tp = ctx.enter_context(nc.psum_tensor("tp", [P, 2, 512], F32))
        banks6 = [acc[:, 0], acc[:, 1], acc[:, 2], acc[:, 3], gu[:, 0], gu[:, 1]]

        x_loaded = sem("x_loaded")
        gains_loaded = sem("gains_loaded")
        pos_loaded = sem("pos_loaded")
        mask_ready = sem("mask_ready")
        angles = sem("angles")
        tables_ready = sem("tables_ready")
        lat_sum = sem("lat_sum")
        lat_root = sem("lat_root")
        lat_full = sem("lat_full")
        rows_loaded = sem("rows_loaded")
        rows_zero = sem("rows_zero")
        vecs_full = sem("vecs_full")
        vecs_ready = sem("vecs_ready")
        masks_ready = sem("masks_ready")
        x_ready = sem("x_ready")
        acc_half = sem("acc_half")
        norm_sum = sem("norm_sum")
        norm_rstd = sem("norm_rstd")
        norm_tok = sem("norm_tok")
        tp_full = sem("tp_full")
        tp_hi = sem("tp_hi")
        tp_read = sem("tp_read")
        gu_silu = sem("gu_silu")
        gu_read = sem("gu_read")
        out_done = sem("out_done")

        V_MIX, V_FFN, V_CONV, V_QA, V_KVA = (0, 0), (0, 16), (0, 32), (0, 56), (0, 59)
        V_FFN1, V_MIX2, V_FFN2 = (0, 61), (0, 77), (0, 93)
        V_SCONV, V_SBIAS, V_SNORM = (1, 0), (2, 0), (2, 32)

        def col(v, n):
            return vecs[:, v[0], v[1] + n:v[1] + n + 1]

        row_loads = [(V_MIX, 16, a["norm_mix"]), (V_FFN, 16, a["norm_ffn"]), (V_CONV, 24, a["conv_w"]),
                     (V_QA, 3, a["mla_q_a_norm"]), (V_KVA, 2, a["mla_kv_a_norm"]), (V_FFN1, 16, a["ffn1_norm_2"]),
                     (V_MIX2, 16, a["mix_norm_2"]), (V_FFN2, 16, a["ffn2_norm_2"]), (V_SCONV, 128, a["ssm_conv_w_2"]),
                     (V_SBIAS, 32, a["ssm_conv_b_2"]), (V_SNORM, 16, a["ssm_norm_2"])]

        class Stage:

            def __init__(self, kind, kw):
                self.kind = kind
                self.s0, self.u0, self.h0, self.x0, self.c0, self.m = [count[k] for k in (
                    "slab", "tp", "hi", "x", "chunk", "norm")]
                self.gate, self.up, self.down, self.C = kw.get("gate"), kw.get("up"), kw.get("down"), kw.get("C")
                self.scale, self.experts, self.gates = kw.get("scale"), kw.get("experts"), kw.get("gates")
                self.gain, self.w, self.act, self.ready = kw.get("gain"), kw.get("w"), kw.get("act"), kw.get("ready")
                self.n, self.sems, self.mem, self.parts = kw.get("n"), kw.get("sems"), kw.get("mem"), kw.get("parts")
                self.Dh, self.half, self.rope0 = kw.get("Dh"), kw.get("half"), kw.get("rope0")
                self.angle0, self.gain0 = kw.get("angle0"), kw.get("gain0")
                self.deferred, self.fn, self.dm = kw.get("deferred"), kw.get("fn"), kw.get("dm")
                self.early = self.late = False
                self.attention = None
                self.before = self.after = None

        stages = []
        count = dict(slab=0, tp=0, hi=0, x=0, chunk=0, norm=0)

        def stage(kind, slabs=0, tp=0, hi=0, x=0, chunk=0, norm=0, **kw):
            f = Stage(kind, kw)
            for k, n in zip(("slab", "tp", "hi", "x", "chunk", "norm"), (slabs, tp, hi, x, chunk, norm)):
                count[k] += n
            stages.append(f)

        def ffn_stage(gate, up, down, scale, experts=1, gates=None):
            C = gate.shape[-1] // FC
            stage("ffn", slabs=3 * C * experts, tp=C * experts, hi=C * experts, x=2 * experts, chunk=C * experts,
                  gate=gate, up=up, down=down, C=C, scale=scale, experts=experts, gates=gates,
                  fn=sum(f.kind == "ffn" and f.gates is None for f in stages))

        vec_rows = big[:, 6144:6144 + 3 * P].rearrange("p (a b) -> p a b", a=3)

        def norm_stage(gain, deferred=True):
            stage("norm", tp=4, hi=4, norm=1, gain=gain, deferred=deferred,
                  dm=sum(f.kind == "norm" and not f.deferred for f in stages))

        def out_stage(w, act, ready):
            stage("out", slabs=4, x=2, w=w, act=act, ready=ready)

        def attention_sems(n):
            return {k: sem(f"{k}{n}") for k in ("qk_square", "qk_sum", "qk_scaled", "qk_root", "qk_done", "head_T", "head_q",
                                                "head_k", "head_scores", "head_masked", "head_max", "head_exp", "head_p",
                                                "head_pT", "head_pcopy", "head_o", "head_ohi", "head_olo")}

        def attention_stage(n, **kw):
            f_sems = attention_sems(n)
            stage("attention", n=n, sems=f_sems, **kw)
            return f_sems

        conv_lo = sem("conv_lo")
        A, B = (actA_hi, actA_lo), (actB_hi, actB_lo)

        def conv_mixer():
            norm_stage((V_MIX, 0), deferred=False)
            stage("conv_in", slabs=12)
            out_stage(a["conv_w_out"][0], B, (conv_lo, 4))

        def latent_mixer():
            norm_stage((V_MIX, 8))
            stage("mla_down", slabs=4, tp=3, hi=3)
            stage("mla_up", slabs=7)
            q = attention_stage(1, Dh=QK_NOPE + QK_ROPE, half=QK_ROPE // 2, rope0=QK_NOPE, angle0=0, gain0=0,
                                parts=[(0, QK_NOPE), (QK_NOPE, QK_ROPE)], mem=mla_mem)
            out_stage(a["mla_w_o"][0], B, (q["head_olo"], HEADS))

        def block_attention_mixer():
            norm_stage((V_MIX2, 0))
            stage("qkv", slabs=12)
            q = attention_stage(2, Dh=HEAD, half=HEAD // 2, rope0=0, angle0=QK_ROPE // 2, gain0=2 * (QK_NOPE + QK_ROPE),
                                parts=[(0, HEAD)], mem=moba_mem)
            out_stage(a["attn_w_o_2"][0], B, (q["head_olo"], HEADS))

        def experts_mixture():
            norm_stage((V_FFN, 8))
            stage("router")
            ffn_stage(a["moe_w_gate"][0], a["moe_w_up"][0], a["moe_w_down"][0], None, EXPERTS, gates)

        def state_space_mixer():
            norm_stage((V_MIX2, 8), deferred=False)
            stage("ssm_in", slabs=25, tp=8)
            stage("ssd")
            stage("ssm_out", slabs=8, tp=8, hi=8, x=2)

        def swiglu(gain, names, layer, scale):
            norm_stage(gain)
            ffn_stage(*[a[n][layer] for n in names], scale)

        FFN0 = ("ffn_w_gate", "ffn_w_up", "ffn_w_down")
        FFN1 = ("ffn1_w_gate_2", "ffn1_w_up_2", "ffn1_w_down_2")
        FFN2 = ("ffn2_w_gate_2", "ffn2_w_up_2", "ffn2_w_down_2")

        def area(at, n):
            return big[:, at:at + n]

        mla_dn = area(0, NT * DOWN).rearrange("p (t n) -> p t n", t=NT)
        mla_qk = [area(1408 + 3072 * w, 3072).rearrange("p (t h n) -> p t h n", t=NT, h=HEADS) for w in range(2)]
        mla_v = area(7552, 2048).rearrange("p (t n) -> p t n", t=NT)
        mla_mem = dict(qk=mla_qk, v=mla_v, s=area(9600, 3072), pT=area(1408, 3072),
                       stage=[(h_tok[:, :, :].rearrange("p t n -> p (t n)"), silu_g[:, :, :].rearrange("p t n -> p (t n)")),
                              (area(0, 512), area(512, 512))])
        qkv = area(0, 6144).rearrange("p (t n) -> p t n", t=NT)
        moba_mem = dict(qk=[qkv[:, :, 1024 * w:1024 * (w + 1)].rearrange("p t (h n) -> p t h n", h=HEADS) for w in range(2)],
                        v=qkv[:, :, 2048:3072], s=area(6144, 3072), pT=area(9216, 3072),
                        stage=[(h_tok[:, :, :].rearrange("p t n -> p (t n)"), silu_g[:, :, :].rearrange("p t n -> p (t n)")),
                               (area(12288, 256), area(12544, 256))])

        head_junk, rope_key_sq, moba_junk = tp[:, 0, :], tp[:, 1, 0:NT * QK_ROPE], area(9216, 1024)
        rope_key_ss = sb("rope_key_ss", [P, NT])

        plan = [conv_mixer,
                lambda: swiglu((V_FFN, 0), FFN0, 0, 1.0),
                latent_mixer,
                experts_mixture,
                lambda: swiglu((V_FFN1, 0), FFN1, 0, 0.5),
                block_attention_mixer,
                lambda: swiglu((V_FFN2, 0), FFN2, 0, 0.5),
                lambda: swiglu((V_FFN1, 8), FFN1, 1, 0.5),
                state_space_mixer,
                lambda: swiglu((V_FFN2, 8), FFN2, 1, 0.5)]
        for step in plan[START:STOP]:
            step()
        stages_used = stages
        for f, after in zip(stages, stages[1:]):
            if after.kind == "attention":
                f.attention = after
        for before, f, after in zip([None] + stages[:-1], stages, stages[1:] + [None]):
            if f.kind == "norm" and f.deferred:
                if before is not None and before.gates is None:
                    before.after, f.early = f, True
                if after.kind in ("ffn", "mla_down", "qkv"):
                    after.before, f.late = f, True
        total_slabs = count["slab"]
        tables_at = [f for f in stages if f.kind not in ("norm", "conv_in")][0]
        x_total = count["x"]

        vT = big[:, 0:2 * (SEQ + 2)].rearrange("p (b n) -> p b n", b=2)
        cT = big[:, 600:600 + 512]
        convT = big[:, 1200:1200 + 512]
        gT = big[:, 1800:1800 + 512]
        hn = big[:, 4096:4096 + NT * D].rearrange("p (t d) -> p t d", t=NT)

        conv_c = sem("conv_c")
        conv_read = sem("conv_read")
        conv_g = sem("conv_g")
        conv_hi = sem("conv_hi")

        def small(n, at=0):
            return silu_g[:, :, :].rearrange("p t n -> p (t n)")[:, at:at + n]

        def small2(n, at=0):
            return h_tok[:, :, :].rearrange("p t n -> p (t n)")[:, at:at + n]

        rt = [area(8192 + 16 * n, 16).rearrange("p (t e) -> p t e", t=NT) for n in range(8)]
        rt_row = [area(8320 + 2 * n, 2) for n in range(10)]
        rank8 = area(8352, 16).rearrange("p (t e) -> p t e", t=NT)
        one2_mask = area(8368, 16).rearrange("p (t e) -> p t e", t=NT)
        sel = area(8384, 16)
        slot_of = area(8400, 16)
        most = area(8416, 1)
        crowded = sb("crowded", [P, 1], I32)
        r_tri, r_ones, iota = area(8448, P), area(8576, P), area(8704, P)
        rows_hi = actB_hi[:, :, :].rearrange("p k n -> p (k n)").rearrange("p (t n) -> p t n", t=NT)
        rows_lo = actB_lo[:, :, :].rearrange("p k n -> p (k n)").rearrange("p (t n) -> p t n", t=NT)
        xg_hi = [actA_hi[:, 4 * n:4 * n + 4, :].rearrange("p k n -> p (k n)") for n in range(2)]
        xg_lo = [actA_lo[:, 4 * n:4 * n + 4, :].rearrange("p k n -> p (k n)") for n in range(2)]
        yg = area(0, D)
        pick = hT_hi[:, 2 * P:4 * P]
        put = area(D, NT * P)
        route_const, route_sel, route_cum, route_flag, rows_hi_done, rows_lo_done = [sem(n) for n in (
            "route_const", "route_sel", "route_cum", "route_flag", "rows_hi_done", "rows_lo_done")]
        picked, gathered, xg_hi_done, xg_lo_done, yg_done, scattered = [sem(n) for n in (
            "picked", "gathered", "xg_hi_done", "xg_lo_done", "yg_done", "scattered")]
        iota_i = area(8832, P).bitcast(I32)
        router_loaded, router_split, router_logits = sem("router_loaded"), sem("router_split"), sem("router_logits")
        router_shift, router_exp, router_done = sem("router_shift"), sem("router_exp"), sem("router_done")
        rank_ready, router_copied, router_tokens = sem("rank_ready"), sem("router_copied"), sem("router_tokens")
        logits_T = area(8960, SEQ)[0:EXPERTS]

        ssm_x = area(0, 4096).rearrange("p (t n) -> p t n", t=NT)
        ssm_bc = area(4096, 4096).rearrange("p (b n) -> p b n", b=16)
        ssm_z = area(8192, 4096).rearrange("p (t n) -> p t n", t=NT)
        cv_x = [area(9240 + 512 * n, 512) for n in range(2)]
        si_x = [area(10264 + 512 * n, 512) for n in range(2)]
        tri, ones = small2(128, 0), small2(128, 128)
        skip_bc, bias_bc, alog_bc, decay_rate = [small2(32, 256 + 32 * n) for n in range(4)]
        dt_tok, a_tok = small2(64, 384), small2(64, 448)
        dt_in, dt_abs, dt_exp, dt_z, dt_z2, dt_poly, neg_cum = [small(64, 64 * n) for n in range(7)]
        decay0, exp_cum1 = small(32, 448), small(32, 480)
        m_buf = [aux[:, 0:512], aux[:, 512:1024]]
        cb_buf = [aux[:, 1024:1152], aux[:, 1152:1280]]
        b_tok = aux[:, 1280:1408]
        xdt_buf = [area(12288, 256), area(12544, 256)]
        xdecay, state = aux2[:, 0:256], aux2[:, 256:512]
        ssm_const, ssm_rows, dt_ready, dt_e, a_ready, a_rate, cum_full, cum_neg, cum_exp = [sem(n) for n in (
            "ssm_const", "ssm_rows", "dt_ready", "dt_e", "a_ready", "a_rate", "cum_full", "cum_neg", "cum_exp")]
        dt_heads = area(9240 + 512, SEQ)[0:SSM_HEADS]
        dt_copied, dt_tokens = sem("dt_copied"), sem("dt_tokens")
        sx_copy, sx_conv, sx_silu, sz_silu = sem("sx_copy"), sem("sx_conv"), sem("sx_silu"), sem("sz_silu")
        sd_cb, sd_seg, sd_cbe, sd_exp, sd_x, sd_m, sd_y, sd_st, sd_read, sd_sq, sd_root, sd_tok = [sem(n) for n in (
            "sd_cb", "sd_seg", "sd_cbe", "sd_exp", "sd_x", "sd_m", "sd_y", "sd_st", "sd_read", "sd_sq", "sd_root", "sd_tok")]

        sq_junk, y_off = small(256, 0), sb("y_off", [P, 256])[:, :]
        mla_evac = sem("mla_evac")
        rope_key_done = sem("rope_key_done")
        qkv_evac = sem("qkv_evac")
        inv_freq = area(7168, 96)
        pos_int = area(7296, 4).bitcast(I32).rearrange("p (w t) -> p w t", w=2)
        pos_f = area(7312, 4).rearrange("p (w t) -> p w t", w=2)
        ang = area(7328, 3 * 192).rearrange("p (a n) -> p a n", a=3)
        banks_pair = [acc[:, 0:2, :], acc[:, 2:4, :], gu[:, :, :]]

        def banks_pair_of(n):
            return [banks_pair[n][:, 0], banks_pair[n][:, 1]]

        block = ctx.enter_context(nc.Block())

        def used(e, base, k, i=0, per=0):
            e.wait_ge(slab_used, base + k + 1 + SPLIT + RAW * i + RAW * per)

        def positions(e, f, fn):
            C = f.C
            fn(0, 0, 0)
            fn(1, 0, 0)
            if f.experts > 1:
                with e.Fori(0, f.experts - 1) as ex:
                    for k in range(2, 3 * C + 2):
                        fn(k, 0, ex)
                for k in range(2, 3 * C):
                    fn(k, 0, f.experts - 1)
                return
            trips = (C - 1) // 2 - (f is stages_used[-1])
            with e.Fori(0, trips) as i:
                for k in range(2, 8):
                    fn(k, i, 0)
            for k in range(2 + 6 * trips, 3 * C):
                fn(k, 0, 0)

        def ffn_kind(f, k, ex):
            if k < 2:
                return ("up_a", "up_b")[k], 0
            if k == 3 * f.C - 1 and isinstance(ex, int) and ex == f.experts - 1:
                return "down", f.C - 1
            return (("up_a", (k + 1) // 3), ("up_b", k // 3), ("down", (k - 4) // 3))[(k - 2) % 3]

        def each_expert(e, fn):
            def body(ex, first, last, parity):
                for k in range(0 if first else 2, 3 * (F_EXPERT // FC) + (0 if last else 2)):
                    fn(k, ex, first, last, parity)

            body(0, True, False, 0)
            with e.Fori(0, EXPERTS // 2 - 1) as i:
                body(2 * i + 1, False, False, 1)
                body(2 * i + 2, False, False, 0)
            body(EXPERTS - 1, False, True, 1)

        def one_tile_or_all(e, one_tile, all_tokens):
            e.wait_ge(route_flag, 1)
            n = e.value_load(crowded[0:1, 0:1], min_val=0, max_val=SEQ)
            with e.If(n > P):
                all_tokens()
            with e.Else():
                one_tile()

        @block.sync
        def _(sp):
            def load(s, slot, halves):
                sp.wait_ge(slab_split, s + 1)
                for dst, src in halves(raw[:, slot]):
                    sp.dma_start(dst, src).then_inc(raw_full[slot], 16)

            def in_cols(w, c0, n, kts):
                kh = (kts[0] + kts[-1] + 1) // 2 if len(kts) > 1 else None

                def halves(slot):
                    v = slot[:, 0:len(kts) * n].rearrange("p (k n) -> p k n", n=n)
                    src = w.rearrange("(k p) n -> p k n", p=P)
                    if kh is None:
                        h = n // 2
                        return [(v[:, :, 0:h], src[:, kts[0]:kts[-1] + 1, c0:c0 + h]),
                                (v[:, :, h:n], src[:, kts[0]:kts[-1] + 1, c0 + h:c0 + n])]
                    a0 = kh - kts[0]
                    cols = slice(c0, c0 + n) if isinstance(c0, int) else bass.ds(c0, n)
                    return [(v[:, 0:a0], src[:, kts[0]:kh, cols]),
                            (v[:, a0:], src[:, kh:kts[-1] + 1, cols])]
                return halves

            def ffn_loads(f):
                def at(k, i, ex):
                    kind, c = ffn_kind(f, k, ex)
                    ahead_of = c // f.C
                    c = c % f.C + 2 * i

                    def w_of(w):
                        return w if f.experts == 1 else w[ahead_of:][bass.ds(ex, 1)].rearrange("e k n -> (e k) n")

                    def halves(slot):
                        if kind == "down":
                            v = slot.rearrange("p (j n) -> p j n", j=2)
                            src = w_of(f.down)[bass.ds(c * FC, FC), :].rearrange("(j p) n -> p j n", p=P)
                            return [(v[:, j], src[:, j]) for j in (1, 0)]
                        k0 = 0 if kind == "up_a" else 4
                        v = slot.rearrange("p (k n) -> p k n", k=4)
                        return [(v[:, :, h * FC:(h + 1) * FC],
                                 w_of(w).rearrange("(k p) n -> p k n", p=P)[:, k0:k0 + 4, bass.ds(c * FC, FC)])
                                for h, w in enumerate((f.gate, f.up))]
                    load(f.s0 + k + 6 * i + 3 * f.C * ex, (f.s0 + k) % RAW, halves)
                positions(sp, f, at)

            for t in range(NT):
                sp.dma_start(x[:, t, :], a["x"].rearrange("(t p) d -> p t d", p=P)[:, t]).then_inc(x_loaded, 16)
            sp.wait_ge(x_loaded, 16 * NT)
            for f in stages_used:
                if f.kind == "conv_in":
                    for n in range(12):
                        c0 = (1024, 2048, 0)[n % 3] + 256 * (n // 3)
                        load(f.s0 + n, (f.s0 + n) % RAW, in_cols(a["conv_w_in"][0], c0, 256, list(range(8))))
                elif f.kind == "out":
                    for n in range(4):
                        load(f.s0 + n, (f.s0 + n) % RAW,
                             in_cols(f.w, 512 * (n // 2), 512, list(range(4 * (n % 2), 4 * (n % 2) + 4))))
                elif f.kind == "mla_down":
                    for n in range(4):
                        load(f.s0 + n, (f.s0 + n) % RAW,
                             in_cols(a["mla_w_down"][0], 352 * (n // 2), 352, list(range(4 * (n % 2), 4 * (n % 2) + 4))))
                elif f.kind == "mla_up":
                    for n in range(7):
                        w, kts, c = (a["mla_w_uq"][0], [0, 1, 2], n) if n < 3 else (a["mla_w_ukv"][0], [0, 1], n - 3)
                        load(f.s0 + n, (f.s0 + n) % RAW, in_cols(w, 512 * c, 512, kts))
                elif f.kind == "qkv":
                    for n in range(12):
                        load(f.s0 + n, (f.s0 + n) % RAW,
                             in_cols(a["attn_w_qkv_2"][0], 512 * (n // 2), 512, list(range(4 * (n % 2), 4 * (n % 2) + 4))))
                elif f.kind == "ssm_in":
                    w = a["ssm_w_in_2"][0]
                    for n in range(25):
                        if n == 0:
                            h = in_cols(w, 3 * D_INNER, SSM_HEADS, list(range(8)))
                        elif n <= 16:
                            h = in_cols(w, D_INNER + 256 * (n - 1), 256, list(range(8)))
                        else:
                            k4 = 4 * ((n - 17) % 2)
                            h = in_cols(w, 512 * ((n - 17) // 2), 512, list(range(k4, k4 + 4)))
                        load(f.s0 + n, (f.s0 + n) % RAW, h)
                elif f.kind == "ssm_out":
                    for n in range(8):
                        load(f.s0 + n, (f.s0 + n) % RAW,
                             in_cols(a["ssm_w_out_2"][0], 512 * (n // 4), 512, list(range(4 * (n % 4), 4 * (n % 4) + 4))))
                elif f.kind == "ffn":
                    ffn_loads(f)
            for n in range(2):
                cs = slice(512 * n, 512 * (n + 1))
                sp.wait_ge(x_ready, x_total - 1 + n)
                sp.dma_start(out.rearrange("(t p) d -> p t d", p=P)[:, :, cs], x[:, :, cs]).then_inc(out_done, 16)
            sp.wait_ge(out_done, 32)

        @block.gpsimd
        def _(pool):
            def root(f):
                pool.wait_ge(norm_sum, 2 * (f.m + 1))
                pool.tensor_scalar(n_ms[:, f.m, :], n_sum[:, f.m, :], 1.0 / D, EPS, ALU.mult, ALU.add)
                pool.drain()
                pool.tensor_tensor(n_rstd[:, f.m, :], n_ms[:, f.m, :], n_half[:, 0:NT], ALU.pow).then_inc(norm_rstd, 1)

            later_f = aux2[:, 0:P]
            pool.memset(ident[:, :], 0.0)
            pool.memset(later_f, 0.0)
            pool.drain()
            pool.affine_select(out=ident[:, :], in_=ident[:, :], compare_op=ALU.not_equal, fill=1.0, base=0,
                               pattern=[[-1, P]], channel_multiplier=1).then_inc(masks_ready, 1)
            pool.affine_select(out=later_f, in_=later_f, compare_op=ALU.is_ge, fill=-1e30, base=0,
                               pattern=[[1, P]], channel_multiplier=-1).then_inc(masks_ready, 1)
            pool.memset(n_half[:, :], -0.5)
            pool.drain()
            if not stages_used[0].deferred:
                root(stages_used[0])
            pool.memset(zero_r[:, :].bitcast(F32), 0.0)
            pool.memset(mask[:, :], 0.0)
            pool.drain()
            at = 0
            for name in ("mla_q_norm", "mla_k_norm", "attn_q_norm_2", "attn_k_norm_2"):
                n = a[name].shape[-1]
                pool.dma_start(gains[:, at:at + n], a[name].broadcast_to([P, n])).then_inc(gains_loaded, 16)
                at += n
            pool.dma_start(inv_freq[:, :], a["inv_freq"].broadcast_to([P, 96])).then_inc(pos_loaded, 16)
            with nc.allow_non_contiguous_dma(reason="256 positions"):
                for w, name in enumerate(("positions", "positions_2")):
                    pool.dma_start(pos_int[:, w], a[name].rearrange("a (t p) -> p (a t)", p=P)).then_inc(pos_loaded, 16)
            pool.affine_select(out=mask[:, 0:P], in_=mask[:, 0:P], compare_op=ALU.is_ge, fill=-3e38, base=0,
                               pattern=[[-1, P]], channel_multiplier=1).then_inc(mask_ready, 1)
            pool.affine_select(out=mask[:, 2 * P:3 * P], in_=mask[:, 2 * P:3 * P], compare_op=ALU.is_ge, fill=-3e38, base=0,
                               pattern=[[-1, P]], channel_multiplier=1).then_inc(mask_ready, 1)
            pool.dma_start(router_w[:, :].rearrange("p (k e) -> p k e", e=EXPERTS),
                           a["moe_router"][0].rearrange("(k p) e -> p k e", p=P)).then_inc(router_loaded, 16)
            for f in stages_used:
                if f.kind == "router":
                    for e in range(EXPERTS):
                        pool.memset(rank8[:, :, e:e + 1], float(EXPERTS - e)).then_inc(rank_ready, 1)
                    pool.memset(r_ones, 1.0)
                    pool.memset(r_tri, 1.0)
                    pool.iota(iota_i, pattern=[[1, P]], base=0, channel_multiplier=0)
                    pool.drain()
                    pool.tensor_copy(iota, iota_i)
                    pool.affine_select(out=r_tri, in_=r_tri, compare_op=ALU.is_ge, fill=0.0, base=0, pattern=[[1, P]],
                                       channel_multiplier=-1)
                    pool.drain().then_inc(route_const, 1)
                if f.kind == "ssm_in":
                    pool.memset(tri, 1.0)
                    pool.memset(ones, 1.0)
                    pool.drain()
                    pool.affine_select(out=tri, in_=tri, compare_op=ALU.is_ge, fill=0.0, base=0, pattern=[[1, P]],
                                       channel_multiplier=-1).then_inc(ssm_const, 1)
                    for v, name in ((skip_bc, "ssm_d_2"), (bias_bc, "ssm_dt_bias_2"), (alog_bc, "ssm_a_log_2")):
                        pool.dma_start(v, a[name].broadcast_to([P, SSM_HEADS])).then_inc(ssm_rows, 16)
                if f.kind == "ssd":
                    for half in range(2):
                        pool.wait_ge(sd_sq, 8 * (half + 1))
                        ss, rstd, power = [v.rearrange("p (t g) -> p t g", t=NT)[:, :, 4 * half:4 * half + 4]
                                           for v in (qk_ss[:, 0, :], qk_rstd[:, 0, :], n_half[:, 0:16])]
                        pool.tensor_scalar(ss, ss, 1.0 / (D_INNER // GROUPS), EPS, ALU.mult, ALU.add)
                        pool.drain()
                        pool.tensor_tensor(rstd, ss, power, ALU.pow).then_inc(sd_root, 1)
                if f.kind == "norm":
                    if f.m or f.deferred:
                        root(f)
                elif f.kind == "mla_down":
                    pool.wait_ge(lat_sum, 4)
                    for w, n in enumerate((Q_RANK, KV_RANK)):
                        pool.tensor_scalar(lat_ss[:, w, :], lat_ss[:, w, :], 1.0 / n, EPS, ALU.mult, ALU.add)
                        pool.drain()
                        pool.tensor_tensor(lat_rstd[:, w, :], lat_ss[:, w, :], n_half[:, 0:NT], ALU.pow).then_inc(lat_root, 1)
                elif f.kind == "attention":
                    for w in range(2):
                        pool.wait_ge(f.sems["qk_sum"], w + 1)
                        pool.tensor_scalar(qk_ss[:, w, :], qk_ss[:, w, :], 1.0 / f.Dh, EPS, ALU.mult, ALU.add)
                        pool.drain()
                        pool.tensor_tensor(qk_rstd[:, w, :], qk_ss[:, w, :], n_half[:, 0:16], ALU.pow).then_inc(f.sems["qk_root"], 1)

        @block.scalar
        def _(act):
            def split_hi(base, k, i, per):
                n0 = base + k
                act.wait_ge(raw_full[n0 % RAW], 32 * (n0 // RAW + 1) + 32 * i + 32 * per)
                act.wait_ge(slab_used, n0 + 1 + RAW * i + RAW * per)
                act.activation(whi[:, n0 % SPLIT], raw[:, n0 % RAW], ACT.Copy).then_inc(slab_hi, 1)

            def ahead(base, k, i=0, per=0):
                if base + k + 2 < total_slabs:
                    split_hi(base, k + 2, i, per)

            def squares(f):
                if f.x0 == 0:
                    act.wait_ge(x_loaded, 16 * NT)
                else:
                    act.wait_ge(x_ready, f.x0)
                for t in range(NT):
                    act.activation(hn[:, t], x[:, t], ACT.Square, accum_out=n_sum[:, f.m, t:t + 1]).then_inc(norm_sum, 1)

            def norm_hi(f, bs):
                v, g0 = f.gain
                for b in bs:
                    act.wait_ge(tp_full, f.u0 + b + 1)
                    for j in range(2):
                        r = act.activation(actA_hi[:, 2 * b + j, :], tp[:, (f.u0 + b) % 2, j * SEQ:(j + 1) * SEQ],
                                           ACT.Copy, scale=col(v, g0 + 2 * b + j))
                    r.then_inc(tp_hi, 1)

            def norm_early(f):
                if f is not None:
                    norm_hi(f, (0, 1))

            def norm_late(f):
                if f is not None:
                    norm_hi(f, (2, 3))
                    squares(f)

            def norm(f):
                if f.m == 0:
                    act.wait_ge(vecs_ready, 1)
                if not f.deferred and f.m:
                    squares(f)
                if not f.early:
                    norm_hi(f, (0, 1))
                if not f.late:
                    norm_hi(f, (2, 3))
                    if f.deferred:
                        squares(f)

            def ffn(f):
                C = f.C

                def t_hi(k, c, i, ex):
                    act.wait_ge(tp_full, f.u0 + c + 1 + 2 * i + C * ex)
                    act.activation(hT_hi[:, :], tp[:, (f.u0 + c) % 2], ACT.Copy).then_inc(tp_hi, 1)

                def at(k, i, ex):
                    kind, c = ffn_kind(f, k, ex)
                    ahead(f.s0, k, i, C // 2 * ex)
                    if k == 0:
                        norm_late(f.before)
                    if k == 1:
                        act.wait_ge(norm_rstd, f.m)
                    if kind == "up_b":
                        used(act, f.s0, k, i, C // 2 * ex)
                        for t in range(NT):
                            r = act.activation(silu_g[:, t, :], gu[:, t, 0:FC], ACT.Silu, scale=n_rstd[:, f.m - 1, t:t + 1])
                        r.then_inc(gu_silu, 1)
                        if k == 1:
                            t_hi(k, 0, 0, ex)
                    elif kind == "down" and k != 3 * C - 1:
                        t_hi(k, c + 1, i, ex)
                    elif kind == "down":
                        norm_early(f.after)
                positions(act, f, at)

            def routed(f):
                C = f.C
                v, g0 = V_FFN, KT

                def operand(e, kt, parity):
                    if kt == 0:
                        act.wait_ge(gathered, e + 1)
                    r = act.activation(xg_hi[parity][:, kt * P:(kt + 1) * P],
                                       acc[:, 2 + kt // 4, (kt % 4) * P:(kt % 4 + 1) * P], ACT.Copy, scale=col(v, g0 + kt))
                    if kt % 4 == 3:
                        r.then_inc(xg_hi_done, 1)

                def result(e):
                    act.activation(yg, acc[:, 0:2, :], ACT.Copy).then_inc(yg_done, 1)

                def at(k, ex, first, last, parity):
                    kind, c = ffn_kind(f, k, ex)
                    ahead(f.s0, k, 0, C // 2 * ex)
                    if k == 2 and not first:
                        used(act, f.s0, 1, 0, C // 2 * ex)
                        result(ex)
                    if kind == "up_b":
                        used(act, f.s0, k, 0, C // 2 * ex)
                        act.activation(silu_g[:, 0, :], gu[:, c % 2, 0:FC], ACT.Silu).then_inc(gu_silu, 1)
                    t = 0 if k == 1 else c + 1 if kind == "down" and k != 3 * C - 1 else None
                    if t is not None:
                        act.wait_ge(tp_full, f.u0 + t + 1 + C * ex)
                        bank = tp[:, (f.u0 + t) % 2]
                        if t == 3:
                            act.activation(put, bank[:, 2 * P:4 * P], ACT.Copy)
                        act.activation(hT_hi[:, 0:2 * P], bank[:, 0:2 * P], ACT.Copy).then_inc(tp_hi, 1)
                    if not last and OPERAND_AT <= k < OPERAND_AT + KT // 2:
                        for j in range(2):
                            operand(ex + 1, 2 * (k - OPERAND_AT) + j, 1 - parity)

                for kt in range(KT):
                    operand(0, kt, 0)
                each_expert(act, at)
                used(act, f.s0, 3 * C * EXPERTS - 1)
                result(EXPERTS - 1)

            def head_squares(f, w, heads, junk):
                act.drain()
                n = QK_NOPE if f.n == 1 else f.Dh
                for t in range(NT):
                    for h in heads:
                        j = t * len(heads) + h - heads[0]
                        r = act.activation(junk[:, j * n:(j + 1) * n], f.mem["qk"][w][:, t, h, 0:n], ACT.Square,
                                           accum_out=qk_ss[:, w, t * HEADS + h:t * HEADS + h + 1])
                if heads[-1] == HEADS - 1:
                    r.then_inc(f.sems["qk_square" if f.n == 1 else "qk_sum"], 1)

            def heads_scaled(f, w, t):
                act.wait_ge(f.sems["qk_root"], w + 1)
                for h in range(HEADS):
                    v = f.mem["qk"][w][:, t, h, 0:QK_NOPE if f.n == 1 and w else f.Dh]
                    r = act.activation(v, v, ACT.Copy, scale=qk_rstd[:, w, t * HEADS + h:t * HEADS + h + 1])
                r.then_inc(f.sems["qk_scaled"], 1)

            def attention(f):
                q = f.sems
                mem = f.mem
                s = mem["s"]
                if f.n == 1:
                    heads_scaled(f, 0, 1)
                    heads_scaled(f, 1, 0)
                    heads_scaled(f, 1, 1)

                def softmax(h):
                    act.wait_ge(q["head_max"], h + 1)
                    for t in range(NT):
                        v = s[:, h * 384 + t * P:h * 384 + (t + 1) * P + t * P]
                        act.activation(v, v, ACT.Exp, bias=s_neg[:, h, t:t + 1],
                                       accum_out=s_sum[:, h, t:t + 1]).then_inc(q["head_exp"], 1)

                for h in range(HEADS + 1):
                    if h < HEADS:
                        act.wait_ge(q["head_T"], h + 1)
                        if h >= 2:
                            act.wait_ge(q["head_scores"], h - 1)
                        for n, (d0, dn) in enumerate(f.parts):
                            r = act.activation(mem["stage"][h % 2][0][0:dn, n * SEQ:(n + 1) * SEQ],
                                               gu[0:dn, 0, n * SEQ:(n + 1) * SEQ], ACT.Copy)
                        r.then_inc(q["head_q"], 1)
                    if h:
                        softmax(h - 1)
                for h in range(HEADS + 1):
                    if h < HEADS:
                        act.wait_ge(q["head_pT"], h + 1)
                        act.activation(mem["pT"][:, h * 384:(h + 1) * 384], gu[:, h % 2, 0:384],
                                       ACT.Copy).then_inc(q["head_pcopy"], 1)
                    if h:
                        act.wait_ge(q["head_o"], h)
                        act.activation(actB_hi[:, h - 1, :], acc[:, (h - 1) % 4, 0:SEQ], ACT.Copy).then_inc(q["head_ohi"], 1)

            def ssm_in(f):
                def silu_conv(p):
                    act.wait_ge(sx_conv, p + 1)
                    if 2 <= p < 8:
                        act.wait_ge(tp_full, f.u0 + p - 1)
                    for b in range(2):
                        o = si_x[p % 2][:, b * SEQ:(b + 1) * SEQ] if p < 8 else ssm_bc[:, 2 * (p - 8) + b, :]
                        r = act.activation(o, cv_x[p % 2][:, b * SEQ:(b + 1) * SEQ], ACT.Silu, bias=col(V_SBIAS, 2 * p + b))
                    r.then_inc(sx_silu, 1)

                for n in range(25):
                    ahead(f.s0, n)
                    if n == 0:
                        act.wait_ge(ssm_rows, 48)
                        act.activation(decay_rate, alog_bc, ACT.Exp).then_inc(a_rate, 1)
                        used(act, f.s0, 0)
                        act.activation(dt_heads, gu[0:SSM_HEADS, 0, 0:SEQ], ACT.Copy).then_inc(dt_copied, 1)
                    elif n <= 16:
                        p = n - 1
                        used(act, f.s0, n)
                        if p >= 2:
                            act.wait_ge(sx_silu, p - 1)
                        for b in range(2):
                            r = act.activation(cv_x[p % 2][:, b * SEQ:(b + 1) * SEQ], banks6[p % 3][:, b * SEQ:(b + 1) * SEQ],
                                               ACT.Copy, scale=col(V_SCONV, 32 * (TAPS - 1) + 2 * p + b))
                        r.then_inc(sx_copy, 1)
                        if p:
                            silu_conv(p - 1)
                        if p == 1:
                            act.wait_ge(dt_ready, 1)
                            act.activation(dt_exp, dt_abs, ACT.Exp, scale=-1.0).then_inc(dt_e, 1)
                    if n == 17:
                        silu_conv(15)
                        act.wait_ge(cum_neg, 2)
                        act.activation(decay0, decay0, ACT.Exp)
                        act.activation(exp_cum1, exp_cum1, ACT.Exp).then_inc(cum_exp, 1)
                        act.wait_ge(tp_full, f.u0 + 8)
                        act.drain()
                    if n >= 17 and (n - 17) % 2:
                        c = (n - 17) // 2
                        used(act, f.s0, n)
                        act.activation(ssm_z[:, :, 512 * c:512 * (c + 1)], banks_pair[(c + 2) % 3], ACT.Silu).then_inc(sz_silu, 1)

            def ssd(f):
                def squares(n):
                    g, t = n // 2, n % 2
                    act.wait_ge(sd_read, n + 1)
                    act.activation(sq_junk, ssm_x[:, t, 256 * g:256 * (g + 1)], ACT.Square,
                                   accum_out=qk_ss[:, 0, 8 * t + g:8 * t + g + 1]).then_inc(sd_sq, 1)
                    act.drain()

                for n in range(16):
                    g, t = n // 2, n % 2
                    act.wait_ge(sd_cb, n + 1)
                    if n >= 2:
                        act.wait_ge(sd_m, n - 1)
                        act.wait_ge(sd_y, n - 1)
                    if t == 0:
                        act.activation(b_tok, gu[:, 0, P:2 * P], ACT.Copy)
                    act.activation(cb_buf[n % 2], gu[:, 0, 0:P], ACT.Copy).then_inc(sd_cbe, 1)
                    act.wait_ge(sd_seg, n + 1)
                    for r in range(PER_GROUP):
                        h = PER_GROUP * g + r
                        i = act.activation(m_buf[n % 2][:, r * P:(r + 1) * P], acc[:, n % 2, r * P:(r + 1) * P], ACT.Exp,
                                           bias=neg_cum[:, SSM_HEADS * t + h:SSM_HEADS * t + h + 1])
                    i.then_inc(sd_exp, 1)
                    if t == 1:
                        act.wait_ge(sd_y, n)
                        act.activation(state, gu[:, 1, 0:256], ACT.Copy).then_inc(sd_st, 1)
                    if n >= 2:
                        squares(n - 2)
                squares(14)
                squares(15)

            def ssm_out(f):
                def hi(b):
                    act.wait_ge(tp_full, f.u0 + b + 1)
                    hi_t = actA_hi if b < 4 else actB_hi
                    for j in range(2):
                        r = act.activation(hi_t[:, (2 * b + j) % KT, :], tp[:, (f.u0 + b) % 2, j * SEQ:(j + 1) * SEQ],
                                           ACT.Copy, scale=col(V_SNORM, 2 * b + j))
                    r.then_inc(tp_hi, 1)

                hi(0)
                hi(1)
                for n in range(8):
                    ahead(f.s0, n)
                    if n < 3:
                        hi(2 * n + 2)
                        hi(2 * n + 3)
                norm_early(f.after)

            def tables():
                act.wait_ge(masks_ready, 2)
                act.activation(ident_r[:, :], ident[:, :], ACT.Copy)
                act.activation(later_r[:, :], aux2[:, 0:P], ACT.Copy)
                act.wait_ge(router_loaded, 16)
                act.activation(router_hi[:, :], router_w[:, :], ACT.Copy).then_inc(router_split, 1)
                act.wait_ge(angles, 1)
                act.activation(rope_sin[:, :, :].rearrange("p t n -> p (t n)"), ang[:, 0], ACT.Sin)
                act.activation(rope_cos[:, :, :].rearrange("p t n -> p (t n)"), ang[:, 1], ACT.Sin).then_inc(tables_ready, 1)

            act.wait_ge(rows_zero, 1)
            for v, n, src in row_loads:
                flat = src.rearrange("a b -> (a b)") if len(src.shape) == 2 else src.rearrange("a b c -> (a b c)")
                act.dma_start(vec_rows[v[1]:v[1] + n, v[0], :], flat.rearrange("(r c) -> r c", c=P)).then_inc(rows_loaded, 16)
            if not stages_used[0].deferred:
                squares(stages_used[0])
            ahead(0, -2)
            norm(stages_used[0])
            ahead(0, -1)
            for f in stages_used[1:]:
                if f is tables_at:
                    tables()
                if f.kind == "norm":
                    norm(f)
                elif f.kind == "attention":
                    attention(f)
                elif f.kind == "router":
                    act.wait_ge(norm_rstd, f.m)
                    act.wait_ge(router_logits, 1)
                    act.activation(logits_T, acc[0:EXPERTS, 0, 0:SEQ], ACT.Copy).then_inc(router_copied, 1)
                    act.wait_ge(router_shift, 1)
                    act.activation(rt[1], rt[0], ACT.Exp).then_inc(router_exp, 1)
                    for t in range(NT):
                        r = act.activation(rows_hi[:, t, :], x[:, t, :], ACT.Copy, scale=n_rstd[:, f.m - 1, t:t + 1])
                    r.then_inc(rows_hi_done, 1)
                elif f.kind == "ssm_in":
                    ssm_in(f)
                elif f.kind == "ssd":
                    ssd(f)
                elif f.kind == "ssm_out":
                    ssm_out(f)
                elif f.kind == "mla_down":
                    for n in range(4):
                        ahead(f.s0, n)
                        if n == 0:
                            norm_late(f.before)
                            act.wait_ge(norm_rstd, f.m)
                        if n % 2:
                            c = n // 2
                            used(act, f.s0, n)
                            for t in range(NT):
                                r = act.activation(mla_dn[:, t, 352 * c:352 * (c + 1)], (gu, acc)[c][:, t, 0:352], ACT.Copy,
                                                   scale=n_rstd[:, f.m - 1, t:t + 1])
                            r.then_inc(lat_full, 1)
                    for b in range(3):
                        act.wait_ge(tp_full, f.u0 + b + 1)
                        for kt in range(2 * b, min(2 * b + 2, 5)):
                            v = col(V_QA, kt) if kt < 3 else col(V_KVA, kt - 3)
                            r = act.activation(actB_hi[:, kt, :], tp[:, (f.u0 + b) % 2, (kt % 2) * SEQ:(kt % 2 + 1) * SEQ],
                                               ACT.Copy, scale=v)
                        r.then_inc(tp_hi, 1)
                    act.drain()
                    for w, (c0, n) in enumerate(((0, Q_RANK), (Q_RANK, KV_RANK))):
                        for t in range(NT):
                            act.activation(area(9600 + LATENT * t + c0, n), mla_dn[:, t, c0:c0 + n], ACT.Square,
                                           accum_out=lat_ss[:, w, t:t + 1]).then_inc(lat_sum, 1)
                elif f.kind == "mla_up":
                    for n in range(7):
                        ahead(f.s0, n)
                        if n == 3:
                            act.drain()
                            act.activation(f.attention.mem["s"], mla_qk[0][:, :, :, :].rearrange("p t h n -> p (t h n)"),
                                           ACT.Square).then_inc(f.attention.sems["qk_square"], 1)
                        used(act, f.s0, n)
                        bank = acc[:, 2 * (n % 2):2 * (n % 2) + 2, :]
                        act.wait_ge(lat_root, 1 if n < 3 else 2)
                        rms = lat_rstd[:, 0 if n < 3 else 1, :]
                        if n < 3:
                            for t in range(NT):
                                r = act.activation(area(1408 + 1536 * t + 512 * n, 512), bank[:, t], ACT.Copy,
                                                   scale=rms[:, t:t + 1])
                        else:
                            for t in range(NT):
                                kv = bank[:, t].rearrange("p (h n) -> p h n", h=2)
                                h0 = 2 * (n - 3)
                                act.activation(mla_qk[1][:, t, h0:h0 + 2, 0:QK_NOPE], kv[:, :, 0:HEAD], ACT.Copy,
                                               scale=rms[:, t:t + 1])
                                r = act.activation(mla_v[:, t, h0 * HEAD:(h0 + 2) * HEAD].rearrange("p (h n) -> p h n", h=2),
                                                   kv[:, :, HEAD:], ACT.Copy, scale=rms[:, t:t + 1])
                        r.then_inc(mla_evac, 1)
                        if n >= 3:
                            if n == 3:
                                for t in range(NT):
                                    r = act.activation(rope_key_sq[:, t * QK_ROPE:(t + 1) * QK_ROPE], mla_dn[:, t, LATENT:],
                                                       ACT.Square, accum_out=rope_key_ss[:, t:t + 1])
                                r.then_inc(rope_key_done, 1)
                            head_squares(f.attention, 1, [2 * (n - 3), 2 * (n - 3) + 1], head_junk)
                elif f.kind == "qkv":
                    for n in range(12):
                        ahead(f.s0, n)
                        if n == 0:
                            norm_late(f.before)
                            act.wait_ge(norm_rstd, f.m)
                        if n % 2:
                            c = n // 2
                            used(act, f.s0, n)
                            for t in range(NT):
                                r = act.activation(qkv[:, t, 512 * c:512 * (c + 1)], banks_pair[(c + 2) % 3][:, t], ACT.Copy,
                                                   scale=n_rstd[:, f.m - 1, t:t + 1])
                            r.then_inc(qkv_evac, 1)
                        if n in (2, 4, 6, 8):
                            half = (n // 2 - 1) % 2
                            head_squares(f.attention, n // 6, list(range(4 * half, 4 * half + 4)), moba_junk)
                        if n in (5, 7, 9, 10):
                            heads_scaled(f.attention, n // 9, (5, 7, 9, 10).index(n) % 2)
                elif f.kind == "conv_in":
                    for n in range(12):
                        ahead(f.s0, n)
                        g = n // 3
                        if n % 3 == 0:
                            used(act, f.s0, n)
                            act.activation(cT, banks6[n % 3], ACT.Copy).then_inc(conv_c, 1)
                        if n % 3 == 2:
                            act.wait_ge(conv_g, g + 1)
                            act.activation(actB_hi[:, 2 * g:2 * g + 2, :].rearrange("p b n -> p (b n)"), gT,
                                           ACT.Copy).then_inc(conv_hi, 1)
                elif f.kind == "out":
                    for n in range(4):
                        ahead(f.s0, n)
                    norm_early(f.after)
                elif f.kind == "ffn" and f.gates is not None:
                    one_tile_or_all(act, lambda: routed(f), lambda: ffn(f))
                elif f.kind == "ffn":
                    ffn(f)

        @block.vector
        def _(dve):
            def split_lo(base, k, i, per):
                n0 = base + k
                dve.wait_ge(slab_hi, n0 + 1 + RAW * i + RAW * per)
                dve.tensor_tensor(wlo[:, n0 % SPLIT], raw[:, n0 % RAW], whi[:, n0 % SPLIT].bitcast(F32),
                                  ALU.subtract).then_inc(slab_split, 1)

            def ahead(base, k, i=0, per=0):
                if base + k + 2 < total_slabs:
                    split_lo(base, k + 2, i, per)

            def norm_lo(f, bs):
                v, g0 = f.gain
                for b in bs:
                    dve.wait_ge(tp_hi, f.h0 + b + 1)
                    for j in range(2):
                        r = dve.scalar_tensor_tensor(actA_lo[:, 2 * b + j, :], tp[:, (f.u0 + b) % 2, j * SEQ:(j + 1) * SEQ],
                                                     col(v, g0 + 2 * b + j),
                                                     actA_hi[:, 2 * b + j, :].bitcast(F32), ALU.mult, ALU.subtract)
                    r.then_inc(tp_read, 1)

            def norm_early(f):
                if f is not None:
                    norm_lo(f, (0, 1))

            def norm_late(f):
                if f is not None:
                    norm_lo(f, (2, 3))

            def scaled(f):
                dve.wait_ge(norm_rstd, f.m + 1)
                for t in range(NT):
                    dve.tensor_scalar(hn[:, t], x[:, t], n_rstd[:, f.m, t:t + 1], None, ALU.mult).then_inc(norm_tok, 1)

            def norm(f):
                if not f.deferred and f.m:
                    scaled(f)
                if not f.early:
                    norm_lo(f, (0, 1))
                if not f.late:
                    norm_lo(f, (2, 3))

            def add_half(n, source, scale=1.0):
                for t in range(NT):
                    xs = x[:, t, n * 512:(n + 1) * 512]
                    r = dve.scalar_tensor_tensor(xs, source(t), scale if isinstance(scale, float) else scale(t), xs,
                                                 ALU.mult, ALU.add)
                r.then_inc(x_ready, 1)

            def ffn(f):
                C = f.C

                def t_lo(c, i, ex):
                    dve.wait_ge(tp_hi, f.h0 + c + 1 + 2 * i + C * ex)
                    dve.tensor_tensor(hT_lo[:, :], tp[:, (f.u0 + c) % 2], hT_hi[:, :].bitcast(F32),
                                      ALU.subtract).then_inc(tp_read, 1)

                def at(k, i, ex):
                    kind, c = ffn_kind(f, k, ex)
                    ahead(f.s0, k, i, C // 2 * ex)
                    if k == 0:
                        norm_late(f.before)
                    if k == 1:
                        dve.wait_ge(norm_rstd, f.m)
                    if kind == "up_b":
                        dve.wait_ge(gu_silu, f.c0 + c + 1 + 2 * i + C * ex)
                        for t in range(NT):
                            r = dve.scalar_tensor_tensor(h_tok[:, t, :], gu[:, t, FC:2 * FC], n_rstd[:, f.m - 1, t:t + 1],
                                                         silu_g[:, t, :], ALU.mult, ALU.mult)
                        r.then_inc(gu_read, 1)
                        if k == 1:
                            t_lo(0, 0, ex)
                        return
                    if kind != "down":
                        return
                    if f.gates is not None and c == C - 1:
                        used(dve, f.s0, k, i, C // 2 * ex)
                        for n in range(2):
                            add_half(n, lambda t: acc[:, 2 * t + n], lambda t: f.gates[:, t, bass.ds(ex, 1)])
                    if k != 3 * C - 1:
                        t_lo(c + 1, i, ex)
                    elif f.gates is None:
                        dve.wait_ge(acc_half, f.fn + 1)
                        add_half(0, lambda t: acc[:, 2 * t], f.scale)
                        norm_early(f.after)
                        used(dve, f.s0, k)
                        add_half(1, lambda t: acc[:, 2 * t + 1], f.scale)
                positions(dve, f, at)

            def rotate(x1, x2, cos, sin, temp):
                t0, t1, t2, t3 = temp
                dve.drain()
                dve.tensor_tensor(t0, x1, cos, ALU.mult)
                dve.tensor_tensor(t1, x1, sin, ALU.mult)
                dve.tensor_tensor(t2, x2, sin, ALU.mult)
                dve.tensor_tensor(t3, x2, cos, ALU.mult)
                dve.drain()
                dve.tensor_tensor(x1, t0, t2, ALU.subtract)
                return dve.tensor_tensor(x2, t3, t1, ALU.add)

            def rotate_heads(f, w, t):
                half, r0 = f.half, f.rope0
                cos, sin = [z[:, t, f.angle0:f.angle0 + half].unsqueeze(1).broadcast_to([P, HEADS, half])
                            for z in (rope_cos, rope_sin)]
                v = f.mem["qk"][w][:, t]
                n = HEADS * half
                temp = [f.mem["s"][:, j * n:(j + 1) * n].rearrange("p (h n) -> p h n", h=HEADS) for j in range(4)]
                rotate(v[:, :, r0:r0 + half], v[:, :, r0 + half:r0 + 2 * half], cos, sin, temp).then_inc(f.sems["qk_done"], 1)

            def head_gains(f, w):
                return gains[:, f.gain0 + w * f.Dh:f.gain0 + (w + 1) * f.Dh]

            def block_heads(f, w, t):
                v = f.mem["qk"][w][:, t]
                dve.wait_ge(f.sems["qk_scaled"], 2 * w + t + 1)
                dve.tensor_tensor(v, v, head_gains(f, w).unsqueeze(1).broadcast_to([P, HEADS, f.Dh]), ALU.mult)
                rotate_heads(f, w, t)

            def latent_scaled(f, w, t, n):
                dve.wait_ge(f.sems["qk_root"], w + 1)
                for h in range(HEADS):
                    v = f.mem["qk"][w][:, t, h, 0:n]
                    dve.scalar_tensor_tensor(v, v, qk_rstd[:, w, t * HEADS + h:t * HEADS + h + 1], head_gains(f, w)[:, 0:n],
                                             ALU.mult, ALU.mult)

            def attention(f):
                q = f.sems
                mem = f.mem
                s = mem["s"]
                scale = float(f.Dh) ** -0.5
                if f.n == 1:
                    dve.wait_ge(q["qk_square"], 2)
                    ss = qk_ss[:, 1, :].rearrange("p (t h) -> p t h", t=NT)
                    dve.tensor_tensor(ss, ss, rope_key_ss[:, :].unsqueeze(2).broadcast_to([P, NT, HEADS]), ALU.add
                                      ).then_inc(q["qk_sum"], 1)
                    rotate_heads(f, 0, 0)
                    for i, (w, t, n) in enumerate(((0, 1, f.Dh), (1, 0, QK_NOPE), (1, 1, QK_NOPE))):
                        dve.wait_ge(q["qk_scaled"], i + 1)
                        v = mem["qk"][w][:, t, :, 0:n]
                        dve.tensor_tensor(v, v, head_gains(f, w)[:, 0:n].unsqueeze(1).broadcast_to([P, HEADS, n]), ALU.mult)
                        if w == 0:
                            rotate_heads(f, 0, 1)
                    dve.tensor_tensor(mla_qk[1][:, :, :, QK_NOPE:],
                                      mla_dn[:, :, LATENT:].unsqueeze(2).broadcast_to([P, NT, HEADS, QK_ROPE]),
                                      qk_rstd[:, 1, :].rearrange("p (t h) -> p t h", t=NT).unsqueeze(3).broadcast_to(
                                          [P, NT, HEADS, QK_ROPE]), ALU.mult).then_inc(q["qk_done"], 2)
                dve.drain()
                if f.n == 1:
                    dve.wait_ge(mask_ready, 2)

                def masked(h):
                    dve.wait_ge(q["head_scores"], h + 1)
                    dve.scalar_tensor_tensor(s[:, h * 384:(h + 1) * 384], acc[:, h % 4, 0:384], scale, mask[:, :], ALU.mult,
                                             ALU.add).then_inc(q["head_masked"], 1)
                    dve.drain()
                    for t in range(NT):
                        dve.tensor_reduce(s_max[:, h, t:t + 1], s[:, h * 384 + t * P:h * 384 + (2 * t + 1) * P], AX.X, ALU.max)
                    dve.drain()
                    dve.tensor_scalar(s_neg[:, h, :], s_max[:, h, :], -1.0, None, ALU.mult).then_inc(q["head_max"], 1)

                def normalised(h):
                    dve.wait_ge(q["head_exp"], 2 * (h + 1))
                    dve.reciprocal(s_inv[:, h, :], s_sum[:, h, :])
                    dve.drain()
                    for t in range(NT):
                        v = s[:, h * 384 + t * P:h * 384 + (2 * t + 1) * P]
                        r = dve.tensor_scalar(v, v, s_inv[:, h, t:t + 1], None, ALU.mult)
                    r.then_inc(q["head_p"], 1)

                for h in range(HEADS + 2):
                    if h < HEADS:
                        dve.wait_ge(q["head_T"], h + 1)
                        if h >= 2:
                            dve.wait_ge(q["head_scores"], h - 1)
                        for n, (d0, dn) in enumerate(f.parts):
                            r = dve.tensor_copy(mem["stage"][h % 2][1][0:dn, n * SEQ:(n + 1) * SEQ],
                                                gu[0:dn, 1, n * SEQ:(n + 1) * SEQ])
                        r.then_inc(q["head_k"], 1)
                    if 1 <= h <= HEADS:
                        masked(h - 1)
                    if h >= 2:
                        normalised(h - 2)
                for h in range(HEADS):
                    dve.wait_ge(q["head_ohi"], h + 1)
                    dve.tensor_tensor(actB_lo[:, h, :], acc[:, h % 4, 0:SEQ], actB_hi[:, h, :].bitcast(F32),
                                      ALU.subtract).then_inc(q["head_olo"], 1)

            def routed(f):
                C = f.C
                v, g0 = V_FFN, KT

                def choose(e):
                    for t in range(NT):
                        r = dve.tensor_scalar(pick[:, t * P:(t + 1) * P], iota, slot_of[:, at_expert(t, e)], None, ALU.is_equal)
                    r.then_inc(picked, 1)

                def at_expert(t, e):
                    return bass.ds(t * EXPERTS + e, 1)

                def operand(e, kt, parity):
                    if kt % 4 == 0:
                        dve.wait_ge(xg_hi_done, 2 * e + kt // 4 + 1)
                    r = dve.scalar_tensor_tensor(xg_lo[parity][:, kt * P:(kt + 1) * P],
                                                 acc[:, 2 + kt // 4, (kt % 4) * P:(kt % 4 + 1) * P], col(v, g0 + kt),
                                                 xg_hi[parity][:, kt * P:(kt + 1) * P].bitcast(F32), ALU.mult, ALU.subtract)
                    if kt == KT - 1:
                        r.then_inc(xg_lo_done, 1)

                def add(e, t):
                    dve.wait_ge(scattered, 2 * e + 1 + t)
                    dve.scalar_tensor_tensor(x[:, t], acc[:, 2:4, :].rearrange("p b n -> p (b n)"), gates[:, t, bass.ds(e, 1)],
                                             x[:, t], ALU.mult, ALU.add).then_inc(x_ready, 1)

                def at(k, ex, first, last, parity):
                    kind, c = ffn_kind(f, k, ex)
                    ahead(f.s0, k, 0, C // 2 * ex)
                    if not first and k in (4, 6):
                        add(ex - 1, k // 5)
                    if kind == "up_b":
                        dve.wait_ge(gu_silu, f.c0 + c + 1 + C * ex)
                        dve.tensor_tensor(h_tok[:, 0, :], gu[:, c % 2, FC:2 * FC], silu_g[:, 0, :], ALU.mult).then_inc(gu_read, 1)
                    t = 0 if k == 1 else c + 1 if kind == "down" and k != 3 * C - 1 else None
                    if t is not None:
                        dve.wait_ge(tp_hi, f.h0 + t + 1 + C * ex)
                        dve.tensor_tensor(hT_lo[:, 0:2 * P], tp[:, (f.u0 + t) % 2, 0:2 * P], hT_hi[:, 0:2 * P].bitcast(F32),
                                          ALU.subtract).then_inc(tp_read, 1)
                    if not last and k == 12:
                        choose(ex + 1)
                    if not last and OPERAND_AT + 2 <= k < OPERAND_AT + 2 + KT // 2:
                        for j in range(2):
                            operand(ex + 1, 2 * (k - OPERAND_AT - 2) + j, 1 - parity)

                choose(0)
                for kt in range(KT):
                    operand(0, kt, 0)
                each_expert(dve, at)
                for n in range(2):
                    dve.wait_ge(scattered, 2 * EXPERTS - 1 + n)
                    add_half(n, lambda t: acc[:, (2, 0)[n] + t], lambda t: gates[:, t, EXPERTS - 1:])

            def router(f):
                def row(v):
                    return v.unsqueeze(2).broadcast_to([P, NT, EXPERTS])

                dve.wait_ge(router_tokens, 1)
                logits = acc[:, 2, 0:NT * EXPERTS].rearrange("p (t e) -> p t e", t=NT)
                shifted, e, p, c1, one1, p2, one2, g = rt
                mx, total, inv, m1, c1m, m2, c2m, den, rden, _ = rt_row
                dve.wait_ge(norm_rstd, f.m)
                for t in range(NT):
                    dve.tensor_scalar(p[:, t, :], logits[:, t, :], n_rstd[:, f.m - 1, t:t + 1], None, ALU.mult)
                dve.drain()
                logits = p
                dve.tensor_reduce(mx, logits, AX.X, ALU.max)
                dve.drain()
                dve.tensor_tensor(shifted, logits, row(mx), ALU.subtract).then_inc(router_shift, 1)
                dve.wait_ge(router_exp, 1)
                dve.tensor_reduce(total, e, AX.X, ALU.add)
                dve.drain()
                dve.reciprocal(inv, total)
                dve.drain()
                dve.tensor_tensor(p, e, row(inv), ALU.mult)
                dve.drain()
                dve.wait_ge(rank_ready, EXPERTS)
                for src, m, cm, one in ((p, m1, c1m, one1), (p2, m2, c2m, one2)):
                    dve.tensor_reduce(m, src, AX.X, ALU.max)
                    dve.drain()
                    dve.tensor_tensor(c1, src, row(m), ALU.is_equal)
                    dve.drain()
                    dve.tensor_tensor(c1, c1, rank8, ALU.mult)
                    dve.drain()
                    dve.tensor_reduce(cm, c1, AX.X, ALU.max)
                    dve.drain()
                    dve.tensor_tensor(one, c1, row(cm), ALU.is_equal)
                    dve.drain()
                    if src is p:
                        dve.scalar_tensor_tensor(p2, one, -2.0, p, ALU.mult, ALU.add)
                        dve.drain()
                dve.tensor_tensor(den, m1, m2, ALU.add)
                dve.tensor_tensor(g, one1, row(m1), ALU.mult)
                dve.tensor_copy(one2_mask, one2)
                dve.drain()
                dve.tensor_tensor(one2, one2, row(m2), ALU.mult)
                dve.drain()
                dve.reciprocal(rden, den)
                dve.tensor_tensor(g, g, one2, ALU.add)
                dve.drain()
                dve.tensor_tensor(gates[:, :, :], g, row(rden), ALU.mult)
                dve.tensor_tensor(sel.rearrange("p (t e) -> p t e", t=NT), one1, one2_mask, ALU.add).then_inc(route_sel, 1)
                dve.wait_ge(rows_hi_done, 1)
                for t in range(NT):
                    r = dve.scalar_tensor_tensor(rows_lo[:, t, :], x[:, t, :], n_rstd[:, f.m - 1, t:t + 1],
                                                 rows_hi[:, t, :].bitcast(F32), ALU.mult, ALU.subtract)
                r.then_inc(rows_lo_done, 1)
                dve.wait_ge(route_cum, 1)
                dve.drain()
                dve.tensor_tensor(slot_of, acc[:, 1, 0:16], sel, ALU.mult)
                dve.tensor_reduce(most, acc[:, 1, 16:24], AX.X, ALU.max)
                dve.drain()
                dve.tensor_scalar(slot_of, slot_of, -1.0, None, ALU.add)
                dve.tensor_copy(crowded[:, :], most)
                dve.drain().then_inc(route_flag, 1)

            def step_sizes_biased():
                dve.wait_ge(dt_tokens, 1)
                dve.wait_ge(ssm_rows, 48)
                v = dt_in.rearrange("p (t h) -> p t h", t=NT)
                dve.tensor_tensor(v, gu[:, :, 0:SSM_HEADS], bias_bc.unsqueeze(1).broadcast_to([P, NT, SSM_HEADS]), ALU.add)
                dve.drain()
                dve.tensor_scalar(dt_abs, dt_in, -1.0, None, ALU.mult)
                dve.drain()
                dve.tensor_tensor(dt_abs, dt_abs, dt_in, ALU.max).then_inc(dt_ready, 1)

            def step_sizes_argument():
                dve.wait_ge(dt_e, 1)
                dve.tensor_scalar(dt_z2, dt_exp, 2.0, None, ALU.add)
                dve.drain()
                dve.reciprocal(dt_z2, dt_z2)
                dve.drain()
                dve.tensor_tensor(dt_z, dt_exp, dt_z2, ALU.mult)
                dve.drain()
                dve.tensor_tensor(dt_z2, dt_z, dt_z, ALU.mult)
                dve.drain()
                dve.tensor_scalar(dt_poly, dt_z2, 2.0 / 19, 2.0 / 17, ALU.mult, ALU.add)

            def step_sizes_series(powers):
                for k in powers:
                    dve.drain()
                    dve.tensor_tensor(dt_poly, dt_poly, dt_z2, ALU.mult)
                    dve.drain()
                    dve.tensor_scalar(dt_poly, dt_poly, 2.0 / k, None, ALU.add)

            def step_sizes_done():
                dve.drain()
                dve.tensor_tensor(dt_poly, dt_poly, dt_z, ALU.mult)
                dve.tensor_scalar(dt_in, dt_in, 0.0, None, ALU.max)
                dve.drain()
                dve.tensor_tensor(dt_tok, dt_in, dt_poly, ALU.add)
                dve.wait_ge(a_rate, 1)
                dve.tensor_scalar(decay_rate, decay_rate, -1.0, None, ALU.mult)
                dve.drain()
                dve.tensor_tensor(a_tok.rearrange("p (t h) -> p t h", t=NT), dt_tok.rearrange("p (t h) -> p t h", t=NT),
                                  decay_rate.unsqueeze(1).broadcast_to([P, NT, SSM_HEADS]), ALU.mult).then_inc(a_ready, 1)

            def ssm_in(f):
                def x_tokens(p):
                    dve.wait_ge(tp_full, f.u0 + p + 1)
                    dve.tensor_copy(ssm_x[:, :, 256 * p:256 * (p + 1)], tp[:, (f.u0 + p) % 2].rearrange("p (t n) -> p t n", t=NT)
                                    ).then_inc(tp_read, 1)

                for n in range(25):
                    ahead(f.s0, n)
                    if 1 <= n <= 16:
                        p = n - 1
                        dve.wait_ge(sx_copy, p + 1)
                        for back in range(1, TAPS):
                            if back > 1:
                                dve.drain()
                            for b in range(2):
                                o = cv_x[p % 2][:, b * SEQ + back:(b + 1) * SEQ]
                                r = dve.scalar_tensor_tensor(o, banks6[p % 3][:, b * SEQ:(b + 1) * SEQ - back],
                                                             col(V_SCONV, 32 * (TAPS - 1 - back) + 2 * p + b), o,
                                                             ALU.mult, ALU.add)
                        r.then_inc(sx_conv, 1)
                        if 2 <= p < 10:
                            x_tokens(p - 2)
                        if n == 2:
                            step_sizes_biased()
                        elif n == 3:
                            step_sizes_argument()
                        elif n == 4:
                            step_sizes_series((15, 13, 11, 9))
                        elif n == 5:
                            step_sizes_series((7, 5, 3, 1))
                        elif n == 6:
                            step_sizes_done()
                        if n == 10:
                            dve.wait_ge(cum_full, 1)
                            dve.tensor_scalar(neg_cum, gu[:, 1, 0:64], -1.0, None, ALU.mult)
                            dve.tensor_copy(exp_cum1, gu[:, 1, 32:64])
                            dve.drain()
                            dve.tensor_tensor(decay0, gu[:, 1, 64:96], neg_cum[:, 0:32], ALU.add).then_inc(cum_neg, 2)

            def ssd(f):
                heads = "p (h n) -> p h n"

                def per_head(v):
                    return v.unsqueeze(2).broadcast_to([P, PER_GROUP, SSM_HEAD])

                def combine(n):
                    g, t = n // 2, n % 2
                    gs = slice(256 * g, 256 * (g + 1))
                    hs = slice(PER_GROUP * g, PER_GROUP * (g + 1))
                    xs = ssm_x[:, t, gs]
                    dve.tensor_tensor(xs.rearrange(heads, h=PER_GROUP), xs.rearrange(heads, h=PER_GROUP), per_head(skip_bc[:, hs]),
                                      ALU.mult)
                    dve.wait_ge(sd_y, n + 1)
                    dve.drain()
                    dve.tensor_tensor(xs, xs, acc[:, 2 + n % 2, 0:256], ALU.add)
                    if t:
                        dve.tensor_tensor(y_off.rearrange(heads, h=PER_GROUP),
                                          acc[:, 2 + n % 2, 256:512].rearrange(heads, h=PER_GROUP), per_head(exp_cum1[:, hs]),
                                          ALU.mult)
                        dve.drain()
                        dve.tensor_tensor(xs, xs, y_off, ALU.add)
                    dve.drain()
                    dve.tensor_tensor(xs, xs, ssm_z[:, t, gs], ALU.mult).then_inc(sd_read, 1)

                dve.wait_ge(sz_silu, 4)
                dve.wait_ge(cum_exp, 1)
                for n in range(16):
                    g, t = n // 2, n % 2
                    hs = slice(SSM_HEADS * t + PER_GROUP * g, SSM_HEADS * t + PER_GROUP * (g + 1))
                    if n >= 2:
                        dve.wait_ge(sd_y, n - 1)
                    r = dve.tensor_tensor(xdt_buf[n % 2].rearrange(heads, h=PER_GROUP),
                                          ssm_x[:, t, 256 * g:256 * (g + 1)].rearrange(heads, h=PER_GROUP), per_head(dt_tok[:, hs]),
                                          ALU.mult)
                    if t == 0:
                        dve.drain()
                        r = dve.tensor_tensor(xdecay.rearrange(heads, h=PER_GROUP), xdt_buf[n % 2].rearrange(heads, h=PER_GROUP),
                                              per_head(decay0[:, hs]), ALU.mult)
                    r.then_inc(sd_x, 1)
                    dve.wait_ge(sd_cbe, n + 1)
                    dve.wait_ge(sd_exp, n + 1)
                    m = m_buf[n % 2].rearrange(heads, h=PER_GROUP)
                    dve.tensor_tensor(m, m, cb_buf[n % 2].unsqueeze(1).broadcast_to([P, PER_GROUP, P]), ALU.mult).then_inc(sd_m, 1)
                    if n:
                        combine(n - 1)
                combine(15)

            def ssm_out(f):
                def group_scaled(b):
                    if b % 4 == 0:
                        dve.wait_ge(sd_root, b // 4 + 1)
                    for t in range(NT):
                        v = ssm_x[:, t, 256 * b:256 * (b + 1)]
                        r = dve.tensor_scalar(v, v, qk_rstd[:, 0, 8 * t + b:8 * t + b + 1], None, ALU.mult)
                    r.then_inc(sd_tok, 1)

                def lo(b):
                    dve.wait_ge(tp_hi, f.h0 + b + 1)
                    hi_t, lo_t = A if b < 4 else B
                    for j in range(2):
                        kt = (2 * b + j) % KT
                        r = dve.scalar_tensor_tensor(lo_t[:, kt, :], tp[:, (f.u0 + b) % 2, j * SEQ:(j + 1) * SEQ],
                                                     col(V_SNORM, 2 * b + j), hi_t[:, kt, :].bitcast(F32), ALU.mult, ALU.subtract)
                    r.then_inc(tp_read, 1)

                group_scaled(0)
                group_scaled(1)
                lo(0)
                lo(1)
                for n in range(8):
                    if n < 3:
                        group_scaled(2 * n + 2)
                        group_scaled(2 * n + 3)
                    ahead(f.s0, n)
                    if n < 3:
                        lo(2 * n + 2)
                        lo(2 * n + 3)
                    if n == 7:
                        norm_early(f.after)
                    if n % 4 == 3:
                        used(dve, f.s0, n)
                        add_half(n // 4, lambda t: acc[:, 2 * (n // 4) + t])

            def tables():
                dve.wait_ge(pos_loaded, 48)
                dve.tensor_copy(pos_f[:, :, :], pos_int[:, :, :])
                dve.drain()
                a0, a1, turns = ang[:, 0], ang[:, 1], ang[:, 2]
                for w, (c0, c1) in enumerate(((0, 32), (32, 96))):
                    for t in range(NT):
                        dve.tensor_scalar(a0[:, t * 96 + c0:t * 96 + c1], inv_freq[:, c0:c1], pos_f[:, w, t:t + 1], None, ALU.mult)
                dve.drain()
                dve.tensor_scalar(turns, a0, 1.0 / (2 * np.pi), 12582912.0, ALU.mult, ALU.add)
                dve.drain()
                dve.tensor_scalar(turns, turns, 12582912.0, None, ALU.subtract)
                rest = 2 * np.pi
                for bits in (8, 11, 24):
                    exponent = np.floor(np.log2(rest))
                    part = float(np.float32(np.floor(rest / 2.0 ** (exponent - bits)) * 2.0 ** (exponent - bits)))
                    rest -= part
                    dve.drain()
                    dve.scalar_tensor_tensor(a0, turns, -part, a0, ALU.mult, ALU.add)
                dve.drain()
                dve.tensor_scalar(a0, a0, 3.1415925, -3.1415925, ALU.min, ALU.max)
                dve.drain()
                dve.tensor_scalar(a1, a0, -1.0, None, ALU.mult)
                dve.drain()
                dve.tensor_tensor(a1, a1, a0, ALU.min)
                dve.drain()
                dve.tensor_scalar(a1, a1, float(np.pi / 2), None, ALU.add).then_inc(angles, 1)
                dve.wait_ge(router_split, 1)
                dve.tensor_tensor(router_lo[:, :], router_w[:, :], router_hi[:, :].bitcast(F32), ALU.subtract
                                  ).then_inc(router_done, 1)

            dve.memset(vT[:, :, 0:2], 0.0).then_inc(slab_split, RAW)
            dve.memset(vec_rows[:, :, :], 0.0).then_inc(rows_zero, 1)
            if not stages_used[0].deferred:
                scaled(stages_used[0])
            dve.wait_ge(vecs_full, 1)
            dve.tensor_copy(vecs[:, :, :].rearrange("p a b -> p (a b)"), gu[:, 1, 0:3 * P]).then_inc(vecs_ready, 1)
            ahead(0, -2)
            norm(stages_used[0])
            ahead(0, -1)
            for f in stages_used[1:]:
                if f is tables_at:
                    tables()
                if f.kind == "norm":
                    norm(f)
                elif f.kind == "attention":
                    attention(f)
                elif f.kind == "router":
                    router(f)
                elif f.kind == "ssm_in":
                    ssm_in(f)
                elif f.kind == "ssd":
                    ssd(f)
                elif f.kind == "ssm_out":
                    ssm_out(f)
                elif f.kind == "mla_down":
                    for n in range(4):
                        ahead(f.s0, n)
                        if n == 0:
                            norm_late(f.before)
                    for b in range(3):
                        dve.wait_ge(tp_hi, f.h0 + b + 1)
                        for kt in range(2 * b, min(2 * b + 2, 5)):
                            v = col(V_QA, kt) if kt < 3 else col(V_KVA, kt - 3)
                            r = dve.scalar_tensor_tensor(actB_lo[:, kt, :], tp[:, (f.u0 + b) % 2, (kt % 2) * SEQ:(kt % 2 + 1) * SEQ],
                                                         v, actB_hi[:, kt, :].bitcast(F32), ALU.mult, ALU.subtract)
                        r.then_inc(tp_read, 1)
                elif f.kind == "mla_up":
                    q = f.attention
                    for n in range(7):
                        ahead(f.s0, n)
                        if n == 4:
                            dve.wait_ge(q.sems["qk_square"], 1)
                            dve.tensor_reduce(qk_ss[:, 0, :], q.mem["s"].rearrange("p (g n) -> p g n", n=q.Dh), AX.X,
                                              ALU.add).then_inc(q.sems["qk_sum"], 1)
                            dve.wait_ge(gains_loaded, 64)
                            dve.wait_ge(tables_ready, 1)
                        if n == 5:
                            g = head_gains(q, 1)[:, QK_NOPE:]
                            v = mla_dn[:, :, LATENT:]
                            half = QK_ROPE // 2
                            dve.wait_ge(rope_key_done, 1)
                            dve.tensor_tensor(v, v, g.unsqueeze(1).broadcast_to([P, NT, QK_ROPE]), ALU.mult)
                            temp = [q.mem["s"][:, 64 * j:64 * (j + 1)].rearrange("p (t n) -> p t n", t=NT) for j in range(4)]
                            rotate(v[:, :, 0:half], v[:, :, half:], rope_cos[:, :, 0:half], rope_sin[:, :, 0:half], temp)
                        if n == 6:
                            latent_scaled(q, 0, 0, q.Dh)
                elif f.kind == "qkv":
                    for n in range(12):
                        ahead(f.s0, n)
                        if n == 0:
                            norm_late(f.before)
                        if n == 6:
                            dve.wait_ge(gains_loaded, 64)
                            dve.wait_ge(tables_ready, 1)
                        if n in (6, 8, 10, 11):
                            block_heads(f.attention, n // 10, (6, 8, 10, 11).index(n) % 2)
                elif f.kind == "conv_in":
                    for n in range(12):
                        ahead(f.s0, n)
                        g = n // 3
                        bank = banks6[n % 3].rearrange("p (b n) -> p b n", b=2)
                        if n % 3 == 1:
                            dve.wait_ge(conv_c, g + 1)
                            used(dve, f.s0, n)
                            dve.tensor_tensor(vT[:, :, 2:], bank, cT.rearrange("p (b n) -> p b n", b=2),
                                              ALU.mult).then_inc(conv_read, 1)
                            for b in range(2):
                                kt = 2 * g + b
                                cv = convT[:, b * SEQ:(b + 1) * SEQ]
                                dve.drain()
                                dve.tensor_scalar(cv, vT[:, b, 0:SEQ], col(V_CONV, kt), None, ALU.mult)
                                for j in (1, 2):
                                    dve.drain()
                                    dve.scalar_tensor_tensor(cv, vT[:, b, j:j + SEQ], col(V_CONV, j * KT + kt), cv,
                                                             ALU.mult, ALU.add)
                        if n % 3 == 2:
                            used(dve, f.s0, n)
                            dve.drain()
                            if g:
                                dve.wait_ge(conv_hi, g)
                            dve.tensor_tensor(gT, banks6[n % 3], convT, ALU.mult).then_inc(conv_g, 1)
                            dve.wait_ge(conv_hi, g + 1)
                            dve.tensor_tensor(actB_lo[:, 2 * g:2 * g + 2, :].rearrange("p b n -> p (b n)"), gT,
                                              actB_hi[:, 2 * g:2 * g + 2, :].rearrange("p b n -> p (b n)").bitcast(F32),
                                              ALU.subtract).then_inc(conv_lo, 1)
                elif f.kind == "out":
                    for n in range(4):
                        ahead(f.s0, n)
                        if n == 3:
                            norm_early(f.after)
                        if n % 2:
                            used(dve, f.s0, n)
                            add_half(n // 2, lambda t: acc[:, 2 * (n // 2) + t])
                elif f.kind == "ffn" and f.gates is not None:
                    one_tile_or_all(dve, lambda: routed(f), lambda: ffn(f))
                elif f.kind == "ffn":
                    ffn(f)

        @block.tensor
        def _(pe):
            def wait_slab(base, k, i=0, per=0):
                pe.wait_ge(slab_split, base + k + 1 + RAW + RAW * i + RAW * per)

            def three(o, xh, xl, wh, wl, start, stop):
                pe.matmul(o, xh, wh, start=start, stop=False)
                pe.matmul(o, xh, wl, start=False, stop=False)
                return pe.matmul(o, xl, wh, start=False, stop=stop)

            def norm_T(f, bs):
                for b in bs:
                    u = f.u0 + b
                    if u >= 2:
                        pe.wait_ge(tp_read, u - 1)
                    if not f.deferred:
                        pe.wait_ge(norm_tok, 2 * (f.dm + 1))
                    elif f.x0:
                        pe.wait_ge(x_ready, f.x0 - 1 + b // 2)
                    else:
                        pe.wait_ge(x_loaded, 16 * NT)
                    src = x if f.deferred else hn
                    for j in range(2):
                        for t in range(NT):
                            r = pe.transpose(tp[:, u % 2, (2 * j + t) * P:(2 * j + t + 1) * P],
                                             src[:, t, (2 * b + j) * P:(2 * b + j + 1) * P], ident[:, :])
                    r.then_inc(tp_full, 1)

            def norm_early(f):
                if f is not None:
                    norm_T(f, (0, 1))

            def norm_late(f):
                if f is not None:
                    norm_T(f, (2, 3))

            def norm(f):
                if not f.early:
                    norm_T(f, (0, 1))
                if not f.late:
                    norm_T(f, (2, 3))

            def operand_ready(f, kt):
                pe.wait_ge(tp_read, f.u0 - 3 + kt // 2)

            def rows_slab(f, n, aT_hi, aT_lo, kts, width, banks, start, stop, first=False, between=None):
                sl = (f.s0 + n) % SPLIT
                w = [z[:, sl, 0:len(kts) * width].rearrange("p (k n) -> p k n", n=width) for z in (whi, wlo)]
                for j, kt in enumerate(kts):
                    if first:
                        operand_ready(f, kt)
                    if j == 2 and between:
                        between()
                    for t in range(NT):
                        ts = slice(t * P, (t + 1) * P)
                        r = three(banks[t][:, 0:width], aT_hi[:, kt, ts], aT_lo[:, kt, ts], w[0][:, j], w[1][:, j],
                                  start and j == 0, stop and j == len(kts) - 1)
                return r.then_inc(slab_used, 1)

            def cols_slab(f, n, bank, aT_hi, aT_lo, first=False):
                sl = (f.s0 + n) % SPLIT
                w = [z[:, sl].rearrange("p (k n) -> p k n", n=2 * P) for z in (whi, wlo)]
                for b in range(2):
                    bs = slice(b * P, (b + 1) * P)
                    for kt in range(KT):
                        if first and b == 0:
                            operand_ready(f, kt)
                        o = bank[:, b * SEQ:(b + 1) * SEQ]
                        pe.matmul(o, w[0][:, kt, bs], aT_hi[:, kt], start=kt == 0, stop=False)
                        pe.matmul(o, w[0][:, kt, bs], aT_lo[:, kt], start=False, stop=False)
                        r = pe.matmul(o, w[1][:, kt, bs], aT_hi[:, kt], start=False, stop=kt == KT - 1)
                return r.then_inc(slab_used, 1)

            def ffn(f):
                C = f.C

                def transposes(c, i, ex):
                    pe.wait_ge(gu_read, f.c0 + c + 1 + 2 * i + C * ex)
                    pe.wait_ge(tp_read, f.u0 + c - 1 + 2 * i + C * ex)
                    for j in range(2):
                        for t in range(NT):
                            r = pe.transpose(tp[:, (f.u0 + c) % 2, (2 * j + t) * P:(2 * j + t + 1) * P],
                                             h_tok[:, t, j * P:(j + 1) * P], ident[:, :])
                    r.then_inc(tp_full, 1)

                def at(k, i, ex):
                    kind, c = ffn_kind(f, k, ex)
                    per = C // 2 * ex
                    wait_slab(f.s0, k, i, per)
                    sl = (f.s0 + k) % SPLIT
                    if kind == "down":
                        pe.wait_ge(tp_read, f.u0 + c + 1 + 2 * i + C * ex)
                        w = [z[:, sl].rearrange("p (j n) -> p j n", j=2) for z in (whi, wlo)]
                        last = c == C - 1
                        if f.gates is not None and c == 0:
                            pe.wait_ge(x_ready, f.x0 + 2 * ex)
                        for n in range(2):
                            ns = slice(n * 512, (n + 1) * 512)
                            for j in range(2):
                                if k == 3 * C - 1 and n and j:
                                    norm_early(f.after)
                                for t in range(NT):
                                    cs = slice((2 * j + t) * P, (2 * j + t + 1) * P)
                                    r = three(acc[:, 2 * t + n], hT_hi[:, cs], hT_lo[:, cs],
                                              w[0][:, j, ns], w[1][:, j, ns],
                                              f.gates is not None and c == 0 and j == 0, last and j == 1)
                            if last and n == 0 and f.gates is None:
                                r.then_inc(acc_half, 1)
                        r.then_inc(slab_used, 1)
                        if k != 3 * C - 1:
                            transposes(c + 1, i, ex)
                        return
                    w = [z[:, sl].rearrange("p (k n) -> p k n", k=4) for z in (whi, wlo)]
                    k0 = 0 if kind == "up_a" else 4
                    if kind == "up_a":
                        if f.c0 + c > 0:
                            pe.wait_ge(gu_read, f.c0 + c + 2 * i + C * ex)
                    for kt in range(4):
                        if k < 2:
                            operand_ready(f, k0 + kt)
                        if k == 0 and kt == 2:
                            norm_late(f.before)
                        for t in range(NT):
                            ts = slice(t * P, (t + 1) * P)
                            r = three(gu[:, t], actA_hi[:, k0 + kt, ts], actA_lo[:, k0 + kt, ts], w[0][:, kt], w[1][:, kt],
                                      kind == "up_a" and kt == 0, kind == "up_b" and kt == 3)
                    r.then_inc(slab_used, 1)
                    if k == 1:
                        if f.gates is None:
                            pe.wait_ge(x_ready, f.x0)
                        for b in range(4 if f.gates is None else 0):
                            pe.matmul(acc[:, b].rearrange("p (a n) -> p a n", a=4), zero_r[:, :],
                                      zero_r[:, :].unsqueeze(1).broadcast_to([P, 4, P]), start=True, stop=False)
                        transposes(0, 0, ex)
                positions(pe, f, at)

            def attention(f):
                q = f.sems
                mem = f.mem
                pe.wait_ge(q["qk_done"], 4)

                def to_staging(h):
                    for w in range(2):
                        if h:
                            pe.wait_ge((q["head_q"], q["head_k"])[w], h)
                        for n, (d0, dn) in enumerate(f.parts):
                            for t in range(NT):
                                r = pe.transpose(gu[0:dn, w, n * SEQ + t * P:n * SEQ + (t + 1) * P],
                                                 mem["qk"][w][:, t, h, d0:d0 + dn], ident[:, :])
                    r.then_inc(q["head_T"], 1)

                def scores(h):
                    pe.wait_ge(q["head_q"], h + 1)
                    pe.wait_ge(q["head_k"], h + 1)
                    if h >= 4:
                        pe.wait_ge(q["head_masked"], h - 3)
                    qT, kT = mem["stage"][h % 2]
                    for t in range(NT):
                        for n, (d0, dn) in enumerate(f.parts):
                            r = pe.matmul(acc[:, h % 4, t * P:(2 * t + 1) * P],
                                          qT[0:dn, n * SEQ + t * P:n * SEQ + (t + 1) * P], kT[0:dn, n * SEQ:n * SEQ + (t + 1) * P],
                                          start=n == 0, stop=n == len(f.parts) - 1)
                    r.then_inc(q["head_scores"], 1)

                def probs(h):
                    pe.wait_ge(q["head_p"], h + 1)
                    if h >= 2:
                        pe.wait_ge(q["head_pcopy"], h - 1)
                    for b in range(3):
                        r = pe.transpose(gu[:, h % 2, b * P:(b + 1) * P],
                                         mem["s"][:, h * 384 + b * P:h * 384 + (b + 1) * P], ident[:, :])
                    r.then_inc(q["head_pT"], 1)

                def values(h):
                    pe.wait_ge(q["head_pcopy"], h + 1)
                    if h >= 4:
                        pe.wait_ge(q["head_olo"], h - 3)
                    pT = mem["pT"][:, h * 384:(h + 1) * 384]
                    hs = slice(h * HEAD, (h + 1) * HEAD)
                    pe.matmul(acc[:, h % 4, 0:SEQ], mem["v"][:, 0, hs], pT[:, 0:SEQ], start=True, stop=False)
                    pe.matmul(acc[:, h % 4, P:SEQ], mem["v"][:, 1, hs], pT[:, SEQ:], start=False,
                              stop=True).then_inc(q["head_o"], 1)

                to_staging(0)
                for h in range(HEADS):
                    if h + 1 < HEADS:
                        to_staging(h + 1)
                    scores(h)
                probs(0)
                for h in range(HEADS):
                    if h + 1 < HEADS:
                        probs(h + 1)
                    values(h)

            def router(f):
                pe.wait_ge(router_done, 1)
                pe.wait_ge(tp_read, f.u0)
                for kt in range(KT):
                    es = slice(kt * EXPERTS, (kt + 1) * EXPERTS)
                    r = three(acc[0:EXPERTS, 0, 0:SEQ], router_hi[:, es], router_lo[:, es], actA_hi[:, kt, :], actA_lo[:, kt, :],
                              kt == 0, kt == KT - 1)
                r.then_inc(router_logits, 1)
                pe.wait_ge(router_copied, 1)
                for t in range(NT):
                    r = pe.transpose(acc[:, 2, t * EXPERTS:(t + 1) * EXPERTS], logits_T[:, t * P:(t + 1) * P],
                                     ident[0:EXPERTS, 0:EXPERTS])
                r.then_inc(router_tokens, 1)
                pe.wait_ge(route_const, 1)
                pe.wait_ge(route_sel, 1)
                pe.matmul(acc[:, 1, 0:8], r_tri, sel[:, 0:8], start=True, stop=True)
                pe.matmul(acc[:, 1, 8:16], r_tri, sel[:, 8:16], start=True, stop=False)
                pe.matmul(acc[:, 1, 8:16], r_ones, sel[:, 0:8], start=False, stop=True)
                pe.matmul(acc[:, 1, 16:24], r_ones, sel[:, 0:8], start=True, stop=False)
                pe.matmul(acc[:, 1, 16:24], r_ones, sel[:, 8:16], start=False, stop=True).then_inc(route_cum, 1)

            def routed(f):
                C = f.C

                def gather(e, n):
                    pe.wait_ge(picked, n + 1)
                    for kt in range(KT):
                        o = acc[:, 2 + kt // 4, (kt % 4) * P:(kt % 4 + 1) * P]
                        for t in range(NT):
                            for part, rows in enumerate((rows_hi, rows_lo)):
                                r = pe.matmul(o, rows[:, t, kt * P:(kt + 1) * P], pick[:, t * P:(t + 1) * P],
                                              start=t == 0 and part == 0, stop=t == 1 and part == 1)
                    r.then_inc(gathered, 1)

                def scatter(n, t):
                    pe.wait_ge(yg_done, n + 1)
                    if t:
                        pe.wait_ge(x_ready, f.x0 + 2 * n + 1)
                    for b in range(2):
                        bs = slice(b * 512, (b + 1) * 512)
                        ts = slice(t * P, (t + 1) * P)
                        r = pe.matmul(acc[:, 2 + b, :], put[:, ts], yg[:, bs], start=True, stop=True)
                    r.then_inc(scattered, 1)

                def transposes(c, ex):
                    pe.wait_ge(gu_read, f.c0 + c + 1 + C * ex)
                    if f.u0 + c >= 2 or not isinstance(ex, int):
                        pe.wait_ge(tp_read, f.u0 + c - 1 + C * ex)
                    for j in range(2):
                        r = pe.transpose(tp[:, (f.u0 + c) % 2, j * P:(j + 1) * P], h_tok[:, 0, j * P:(j + 1) * P], ident[:, :])
                    if c == 3:
                        for t in range(NT):
                            r = pe.transpose(tp[:, (f.u0 + c) % 2, (2 + t) * P:(3 + t) * P],
                                             pick[:, t * P:(t + 1) * P].bitcast(F32), ident[:, :])
                    r.then_inc(tp_full, 1)

                def at(k, ex, first, last, parity):
                    kind, c = ffn_kind(f, k, ex)
                    if c == C:
                        parity = 1 - parity
                    if kind == "up_a" and c % C == 0:
                        pe.wait_ge(xg_lo_done, ex + 1 + c // C)
                    wait_slab(f.s0, k, 0, C // 2 * ex)
                    sl = (f.s0 + k) % SPLIT
                    if kind == "down":
                        pe.wait_ge(tp_read, f.u0 + c + 1 + C * ex)
                        if c == 0 and not first:
                            pe.wait_ge(yg_done, ex)
                        w = [z[:, sl].rearrange("p (j n) -> p j n", j=2) for z in (whi, wlo)]
                        for j in range(2):
                            cs = slice(j * P, (j + 1) * P)
                            for n in range(2):
                                ns = slice(n * 512, (n + 1) * 512)
                                r = three(acc[:, n], hT_hi[:, cs], hT_lo[:, cs], w[0][:, j, ns], w[1][:, j, ns],
                                          c == 0 and j == 0, c == C - 1 and j == 1)
                        r.then_inc(slab_used, 1)
                        if k != 3 * C - 1:
                            transposes(c + 1, ex)
                    else:
                        w = [z[:, sl].rearrange("p (k n) -> p k n", k=4) for z in (whi, wlo)]
                        k0 = 0 if kind == "up_a" else 4
                        if kind == "up_a" and (f.c0 + c >= 2 or not isinstance(ex, int)):
                            pe.wait_ge(gu_read, f.c0 + c - 1 + C * ex)
                        for kt in range(4):
                            ks = slice((k0 + kt) * P, (k0 + kt + 1) * P)
                            r = three(gu[:, c % 2], xg_hi[parity][:, ks], xg_lo[parity][:, ks], w[0][:, kt], w[1][:, kt],
                                      kind == "up_a" and kt == 0, kind == "up_b" and kt == 3)
                        r.then_inc(slab_used, 1)
                        if k == 1:
                            transposes(0, ex)
                    if not first and k in (3, 5):
                        scatter(ex - 1, k // 4)
                    if not last and k == OPERAND_AT - 1:
                        if not first:
                            pe.wait_ge(x_ready, f.x0 + 2 * ex)
                        gather(ex + 1, ex + 1)

                pe.wait_ge(rows_lo_done, 1)
                gather(0, 0)
                each_expert(pe, at)
                pe.wait_ge(yg_done, EXPERTS)
                for n in range(2):
                    ns = slice(n * 512, (n + 1) * 512)
                    for t in range(NT):
                        ts = slice(t * P, (t + 1) * P)
                        r = pe.matmul(acc[:, (2, 0)[n] + t, :], put[:, ts], yg[:, ns], start=True, stop=True)
                    r.then_inc(scattered, 1)

            def ssm_in(f):

                def x_tokens(p):
                    pe.wait_ge(sx_silu, p + 1)
                    pe.wait_ge(tp_read, f.u0 + p - 1)
                    for t in range(NT):
                        for b in range(2):
                            r = pe.transpose(tp[:, (f.u0 + p) % 2, (2 * t + b) * P:(2 * t + b + 1) * P],
                                             si_x[p % 2][:, b * SEQ + t * P:b * SEQ + (t + 1) * P], ident[:, :])
                    r.then_inc(tp_full, 1)

                for n in range(25):
                    wait_slab(f.s0, n)
                    if n == 0:
                        w = [z[:, f.s0 % SPLIT, 0:KT * SSM_HEADS] for z in (whi, wlo)]
                        for kt in range(KT):
                            hs = slice(kt * SSM_HEADS, (kt + 1) * SSM_HEADS)
                            operand_ready(f, kt)
                            r = three(gu[0:SSM_HEADS, 0, 0:SEQ], w[0][:, hs], w[1][:, hs], actA_hi[:, kt, :], actA_lo[:, kt, :],
                                      kt == 0, kt == KT - 1)
                        r.then_inc(slab_used, 1)
                    elif n <= 16:
                        p = n - 1
                        if p >= 3:
                            pe.wait_ge(sx_conv, p - 2)
                        cols_slab(f, n, banks6[p % 3], *A)
                        if n == 1:
                            pe.wait_ge(dt_copied, 1)
                            for t in range(NT):
                                r = pe.transpose(gu[:, t, 0:SSM_HEADS], dt_heads[:, t * P:(t + 1) * P],
                                                 ident[0:SSM_HEADS, 0:SSM_HEADS])
                            r.then_inc(dt_tokens, 1)
                        if 2 <= p < 10:
                            x_tokens(p - 2)
                        if n == 8:
                            pe.wait_ge(a_ready, 1)
                            pe.wait_ge(ssm_const, 1)
                            for t in range(NT):
                                pe.matmul(gu[:, 1, 32 * t:32 * (t + 1)], tri, a_tok[:, 32 * t:32 * (t + 1)], start=True, stop=True)
                            pe.matmul(gu[:, 1, 64:96], ones, a_tok[:, 0:32], start=True, stop=True).then_inc(cum_full, 1)
                    else:
                        c = (n - 17) // 2
                        if n == 17:
                            pe.wait_ge(cum_neg, 2)
                        if n == 19:
                            pe.wait_ge(sx_conv, 16)
                        if c == 3:
                            pe.wait_ge(sz_silu, 1)
                        k4 = 4 * ((n - 17) % 2)
                        rows_slab(f, n, *A, list(range(k4, k4 + 4)), 512, banks_pair_of((c + 2) % 3), k4 == 0, k4 == 4)

            def ssd(f):
                def first(n):
                    g, t = n // 2, n % 2
                    ts = slice(t * P, (t + 1) * P)
                    if n:
                        pe.wait_ge(sd_cbe, n)
                    r = pe.matmul(gu[:, 0, 0:P], ssm_bc[:, g, ts], ssm_bc[:, 8 + g, ts], start=True, stop=True)
                    if t == 0:
                        r = pe.transpose(gu[:, 0, P:2 * P], ssm_bc[:, g, ts], ident[:, :])
                    r.then_inc(sd_cb, 1)
                    if n >= 2:
                        pe.wait_ge(sd_exp, n - 1)
                    pe.matmul(acc[:, n % 2].rearrange("p (a n) -> p a n", a=PER_GROUP), ident_r[:, :],
                              later_r[:, :].unsqueeze(1).broadcast_to([P, PER_GROUP, P]), start=True, stop=False)
                    for r in range(PER_GROUP):
                        h = SSM_HEADS * t + PER_GROUP * g + r
                        i = pe.matmul(acc[:, n % 2, r * P:(r + 1) * P], a_tok[:, h:h + 1].broadcast_to([P, P]), tri,
                                      start=False, stop=r == PER_GROUP - 1)
                    i.then_inc(sd_seg, 1)

                def second(n):
                    g, t = n // 2, n % 2
                    pe.wait_ge(sd_x, n + 1)
                    pe.wait_ge(sd_m, n + 1)
                    if n >= 2:
                        pe.wait_ge(sd_read, n - 1)
                    for r in range(PER_GROUP):
                        hs = slice(r * SSM_HEAD, (r + 1) * SSM_HEAD)
                        i = pe.matmul(acc[:, 2 + n % 2, hs], m_buf[n % 2][:, r * P:(r + 1) * P], xdt_buf[n % 2][:, hs],
                                      start=True, stop=True)
                    if t == 0:
                        i = pe.matmul(gu[:, 1, 0:256], b_tok, xdecay, start=True, stop=True)
                    else:
                        pe.wait_ge(sd_st, g + 1)
                        i = pe.matmul(acc[:, 2 + n % 2, 256:512], ssm_bc[:, 8 + g, P:2 * P], state, start=True, stop=True)
                    i.then_inc(sd_y, 1)

                pe.wait_ge(sz_silu, 4)
                for n in range(17):
                    if n < 16:
                        first(n)
                    if n:
                        second(n - 1)

            def ssm_out(f):
                def transposes(*bs):
                    for b in bs:
                        u = f.u0 + b
                        pe.wait_ge(sd_tok, b + 1)
                        pe.wait_ge(tp_read, u - 1)
                        for j in range(2):
                            for t in range(NT):
                                r = pe.transpose(tp[:, u % 2, (2 * j + t) * P:(2 * j + t + 1) * P],
                                                 ssm_x[:, t, (2 * b + j) * P:(2 * b + j + 1) * P], ident[:, :])
                        r.then_inc(tp_full, 1)

                transposes(0, 1)
                for n in range(8):
                    wait_slab(f.s0, n)
                    c, q4 = n // 4, n % 4
                    if n < 4:
                        pe.wait_ge(tp_read, f.u0 + 2 * n + 2)
                    between = None
                    if n < 3:
                        between = lambda: transposes(2 * n + 2, 2 * n + 3)
                    elif n == 7:
                        between = lambda: norm_early(f.after)
                    rows_slab(f, n, *(A if q4 < 2 else B), list(range(4 * (q4 % 2), 4 * (q4 % 2) + 4)), 512, banks_pair_of(c),
                              q4 == 0, q4 == 3, between=between)

            pe.sem_inc(slab_used, SPLIT)
            pe.wait_ge(masks_ready, 2)
            pe.wait_ge(rows_loaded, 16 * len(row_loads))
            for t in range(3):
                r = pe.transpose(gu[:, 1, t * P:(t + 1) * P], vec_rows[:, t, :], ident[:, :])
            r.then_inc(vecs_full, 1)
            pe.wait_ge(vecs_ready, 1)
            for f in stages_used:
                if f.kind == "norm":
                    norm(f)
                elif f.kind == "conv_in":
                    for n in range(12):
                        wait_slab(f.s0, n)
                        if n >= 3:
                            g = n // 3
                            if n % 3 == 0:
                                pe.wait_ge(conv_c, g)
                            elif n % 3 == 1:
                                pe.wait_ge(conv_read, g)
                            else:
                                pe.wait_ge(conv_g, g)
                        cols_slab(f, n, banks6[n % 3], *A, first=n == 0)
                elif f.kind == "out":
                    pe.wait_ge(*f.ready)
                    for n in range(4):
                        wait_slab(f.s0, n)
                        c = n // 2
                        rows_slab(f, n, *f.act, list(range(4 * (n % 2), 4 * (n % 2) + 4)), 512,
                                  [acc[:, 2 * c], acc[:, 2 * c + 1]], n % 2 == 0, n % 2 == 1,
                                  between=(lambda: norm_early(f.after)) if n == 3 else None)
                elif f.kind == "attention":
                    attention(f)
                elif f.kind == "router":
                    router(f)
                elif f.kind == "ssm_in":
                    ssm_in(f)
                elif f.kind == "ssd":
                    ssd(f)
                elif f.kind == "ssm_out":
                    ssm_out(f)
                elif f.kind == "mla_down":
                    for n in range(4):
                        wait_slab(f.s0, n)
                        c = n // 2
                        rows_slab(f, n, *A, list(range(4 * (n % 2), 4 * (n % 2) + 4)), 352,
                                  banks_pair_of((2, 0)[c]), n % 2 == 0, n % 2 == 1, n < 2,
                                  (lambda: norm_late(f.before)) if n == 0 else None)
                    for b in range(3):
                        u = f.u0 + b
                        pe.wait_ge(lat_full, 1 if b == 0 else 2)
                        pe.wait_ge(tp_read, u - 1)
                        for kt in range(2 * b, min(2 * b + 2, 5)):
                            for t in range(NT):
                                r = pe.transpose(tp[:, u % 2, (2 * (kt % 2) + t) * P:(2 * (kt % 2) + t + 1) * P],
                                                 mla_dn[:, t, kt * P:(kt + 1) * P], ident[:, :])
                        r.then_inc(tp_full, 1)
                elif f.kind == "mla_up":
                    pe.wait_ge(tp_read, f.u0 - 1)
                    for n in range(7):
                        wait_slab(f.s0, n)
                        if n == 3:
                            pe.wait_ge(tp_read, f.u0)
                        if n >= 2:
                            pe.wait_ge(mla_evac, n - 1)
                        rows_slab(f, n, *B, [0, 1, 2] if n < 3 else [3, 4], 512, banks_pair_of(n % 2), True, True)
                elif f.kind == "qkv":
                    for n in range(12):
                        wait_slab(f.s0, n)
                        c = n // 2
                        if n >= 6:
                            pe.wait_ge(qkv_evac, c - 2)
                        rows_slab(f, n, *A, list(range(4 * (n % 2), 4 * (n % 2) + 4)), 512, banks_pair_of((c + 2) % 3),
                                  n % 2 == 0, n % 2 == 1, n < 2, (lambda: norm_late(f.before)) if n == 0 else None)
                elif f.kind == "ffn" and f.gates is not None:
                    one_tile_or_all(pe, lambda: routed(f), lambda: ffn(f))
                elif f.kind == "ffn":
                    ffn(f)


def constants():
    f = [np.float32(THETA) ** (-np.arange(0, QK_ROPE, 2, dtype=np.float32) / np.float32(QK_ROPE)),
         np.float32(THETA) ** (-np.arange(HEAD // 2, dtype=np.float32) / np.float32(HEAD // 2))]
    return {"inv_freq": np.concatenate(f).astype(np.float32)[None]}


_OUT = ((1, SEQ, D), "float32")


def kernel(**inputs):
    import concourse.bacc as bacc
    from concourse.bass_utils import run_bass_kernel_spmd

    nc = bacc.Bacc("TRN2", target_bir_lowering=False, num_devices=1)
    arrays, args = {}, {}
    for name, value in {**inputs, **constants()}.items():
        v = np.ascontiguousarray(value)
        arrays[f"in_{name}"] = v
        args[name] = nc.dram_tensor(f"in_{name}", v.shape, mybir.dt.from_np(v.dtype), kind="ExternalInput").ap()
    args["x"] = args["x"].rearrange("b s d -> (b s) d")
    out = nc.dram_tensor("out", _OUT[0], F32, kind="ExternalOutput").ap()
    program(nc, args, out.rearrange("b s d -> (b s) d"))
    r = run_bass_kernel_spmd(nc, [arrays], core_ids=[0])
    return r.results[0]["out"]
```
